# Optimizing a Trainium2 kernel written in Bass

```python
import math
import jax, jax.numpy as jnp
from jax import lax
import numpy as np

D_MODEL = 1024
BATCH = 1
SEQ = 512
DEPTH = 2

HEAD_DIM = 64
FOX_HEADS = 8
RET_HEADS = 8
FOX_WIDTH = FOX_HEADS * HEAD_DIM
RET_WIDTH = RET_HEADS * HEAD_DIM
EVEN_MIX_WIDTH = FOX_WIDTH + RET_WIDTH
FOX_Q_BLOCK = 128
RET_CHUNK = 128
EVEN_SIZES = (FOX_WIDTH, FOX_WIDTH, FOX_WIDTH, FOX_HEADS, RET_WIDTH, RET_WIDTH, RET_WIDTH, EVEN_MIX_WIDTH)
EVEN_IN = sum(EVEN_SIZES)
EVEN_SPLITS = tuple(int(v) for v in np.cumsum(EVEN_SIZES)[:-1])
NSA_HEADS = 16
NSA_KV_GROUPS = 4
NSA_HEADS_PER_GROUP = NSA_HEADS // NSA_KV_GROUPS
NSA_WIDTH = NSA_HEADS * HEAD_DIM
NSA_KV_WIDTH = NSA_KV_GROUPS * HEAD_DIM
N_BRANCH = 3
CMP_BLOCK = 32
CMP_STRIDE = 16
CMP_HIDDEN = 256
SLC_BLOCK = 64
SLC_TOPK = 16
WINDOW = 512
NSA_Q_BLOCK = 64
ODD_SIZES = (NSA_WIDTH,) + (NSA_KV_WIDTH,) * 6 + (NSA_HEADS * N_BRANCH, NSA_WIDTH)
ODD_IN = sum(ODD_SIZES)
ODD_SPLITS = tuple(int(v) for v in np.cumsum(ODD_SIZES)[:-1])

RMS_EPS = 1e-6
GN_EPS = 1e-5
NEG = -1e30
FORCE_BONUS = 1e6


def rms_norm(x, g):
    xf = x.astype(jnp.float32)
    y = xf * lax.rsqrt(jnp.mean(xf * xf, axis=-1, keepdims=True) + RMS_EPS)
    return (y * g.astype(jnp.float32)).astype(x.dtype)

def masked_softmax(s, mask):
    s = jnp.where(mask, s, NEG)
    p = jax.nn.softmax(s, axis=-1)
    return jnp.where(mask, p, 0.0)

def alibi_slopes(n):
    return jnp.asarray(2.0 ** (-8.0 * (np.arange(n) + 1) / n), jnp.float32)

def fox_attention(q, k, v, f_logit):
    B, S, H, d = q.shape
    nb = S // FOX_Q_BLOCK
    scale = d ** -0.5
    c = jnp.cumsum(jax.nn.log_sigmoid(f_logit.astype(jnp.float32)), axis=1)
    c_h = c.transpose(0, 2, 1)
    kh = k.transpose(0, 2, 1, 3)
    vh = v.transpose(0, 2, 1, 3)
    qb = q.reshape(B, nb, FOX_Q_BLOCK, H, d).transpose(1, 0, 3, 2, 4)
    cb = c.reshape(B, nb, FOX_Q_BLOCK, H).transpose(1, 0, 3, 2)
    key_pos = jnp.arange(S)

    def block(args):
        qi, ci, bi = args
        t = bi * FOX_Q_BLOCK + jnp.arange(FOX_Q_BLOCK)
        s = jnp.einsum('bhqd,bhkd->bhqk', qi, kh).astype(jnp.float32) * scale
        s = s + ci[..., None] - c_h[:, :, None, :]
        p = masked_softmax(s, key_pos[None, :] <= t[:, None])
        return jnp.einsum('bhqk,bhkd->bhqd', p.astype(vh.dtype), vh)

    o = lax.map(block, (qb, cb, jnp.arange(nb)))
    return o.transpose(1, 0, 3, 2, 4).reshape(B, S, H, d)

def retention_decays(n_heads, chunk):
    lg = np.log(1.0 - 2.0 ** (-5.0 - np.arange(n_heads)))
    i = np.arange(chunk)
    diff = i[:, None] - i[None, :]
    inner = np.where(diff[None] >= 0, np.exp(lg[:, None, None] * np.maximum(diff, 0)[None]), 0.0)
    cross = np.exp(lg[:, None] * (i[None, :] + 1))
    kdec = np.exp(lg[:, None] * (chunk - 1 - i)[None, :])
    cdec = np.exp(lg * chunk)
    return (jnp.asarray(inner, jnp.float32), jnp.asarray(cross, jnp.float32),
            jnp.asarray(kdec, jnp.float32), jnp.asarray(cdec, jnp.float32))

def retention(q, k, v):
    B, S, H, d = q.shape
    n = S // RET_CHUNK
    inner, cross, kdec, cdec = retention_decays(H, RET_CHUNK)

    def chunks(a):
        return a.astype(jnp.float32).reshape(B, n, RET_CHUNK, H, d).transpose(1, 0, 3, 2, 4)

    qc, kc, vc = chunks(q), chunks(k) * (d ** -0.5), chunks(v)

    def step(state, xs):
        qi, ki, vi = xs
        a = jnp.einsum('bhid,bhjd->bhij', qi, ki) * inner
        o = jnp.einsum('bhij,bhje->bhie', a, vi) + jnp.einsum('bhid,bhde->bhie', qi, state) * cross[None, :, :, None]
        state = state * cdec[None, :, None, None] + jnp.einsum('bhjd,bhje->bhde', ki * kdec[None, :, :, None], vi)
        return state, o

    _, o = lax.scan(step, jnp.zeros((B, H, d, d), jnp.float32), (qc, kc, vc))
    o = o.transpose(1, 0, 3, 2, 4).reshape(B, S, H, d)
    mu = jnp.mean(o, axis=-1, keepdims=True)
    var = jnp.mean(jnp.square(o - mu), axis=-1, keepdims=True)
    return ((o - mu) * lax.rsqrt(var + GN_EPS)).reshape(B, S, H * d)

def even_layer(x, norm_g, w_in, b_f, gn_g, w_out):
    B, S, _ = x.shape
    h = rms_norm(x, norm_g)
    u = h @ w_in
    q_f, k_f, v_f, f_l, q_r, k_r, v_r, z = jnp.split(u, EVEN_SPLITS, axis=-1)
    hd = lambda a, n: a.reshape(B, S, n, HEAD_DIM)
    o_f = fox_attention(hd(q_f, FOX_HEADS), hd(k_f, FOX_HEADS), hd(v_f, FOX_HEADS), f_l + b_f)
    o_f = o_f.reshape(B, S, FOX_WIDTH)
    o_r = (retention(hd(q_r, RET_HEADS), hd(k_r, RET_HEADS), hd(v_r, RET_HEADS)) * gn_g).astype(x.dtype)
    y = jnp.concatenate([o_f, o_r], axis=-1) * jax.nn.silu(z)
    return x + y @ w_out

def compress_blocks(a, idx, pe, w1, w2):
    B = a.shape[0]
    nc, l = idx.shape
    ab = a[:, idx] + pe[None, None, :, None, :]
    ab = ab.transpose(0, 1, 3, 2, 4).reshape(B, nc, NSA_KV_GROUPS, l * HEAD_DIM)
    return jax.nn.silu(ab @ w1) @ w2

def nsa_attention(q, kc, vc, ks, vs, kw, vw, gate_logit, pe_k, pe_v, wk1, wk2, wv1, wv2):
    B, S, H, d = q.shape
    G, Hg, QB = NSA_KV_GROUPS, NSA_HEADS_PER_GROUP, NSA_Q_BLOCK
    scale = d ** -0.5
    dtype = q.dtype
    nc = (S - CMP_BLOCK) // CMP_STRIDE + 1
    idx = np.arange(nc)[:, None] * CMP_STRIDE + np.arange(CMP_BLOCK)[None, :]
    cmp_end = jnp.asarray(idx[:, -1], jnp.int32)
    k_cmp = compress_blocks(kc, idx, pe_k, wk1, wk2)
    v_cmp = compress_blocks(vc, idx, pe_v, wv1, wv2)
    ns = S // SLC_BLOCK
    topk = min(SLC_TOPK, ns)
    c0 = np.arange(nc)[:, None] * CMP_STRIDE
    s0 = np.arange(ns)[None, :] * SLC_BLOCK
    overlap = np.clip(np.minimum(c0 + CMP_BLOCK, s0 + SLC_BLOCK) - np.maximum(c0, s0), 0, None)
    cmp_to_slc = jnp.asarray(overlap / CMP_STRIDE, jnp.float32)
    slopes = alibi_slopes(H).reshape(G, Hg)[None, :, :, None, None]
    ks_g = ks.transpose(0, 2, 1, 3)
    vs_g = vs.transpose(0, 2, 1, 3)
    kw_pad = jnp.pad(kw, ((0, 0), (WINDOW, 0), (0, 0), (0, 0)))
    vw_pad = jnp.pad(vw, ((0, 0), (WINDOW, 0), (0, 0), (0, 0)))
    nqb = S // QB
    qb = q.reshape(B, nqb, QB, G, Hg, d).transpose(1, 0, 2, 3, 4, 5)
    gb = gate_logit.reshape(B, nqb, QB, G, Hg, N_BRANCH).transpose(1, 0, 2, 3, 4, 5)
    b_idx = jnp.arange(B)[:, None, None, None]
    g_idx = jnp.arange(G)[None, :, None, None]
    blk = jnp.arange(ns)

    def block(args):
        qi, gi, bi = args
        t = bi * QB + jnp.arange(QB)
        s = jnp.einsum('bqghd,bcgd->bghqc', qi, k_cmp).astype(jnp.float32) * scale
        s = s - slopes * (t[:, None] - cmp_end[None, :]).astype(jnp.float32)
        p_cmp = masked_softmax(s, cmp_end[None, :] <= t[:, None])
        o_cmp = jnp.einsum('bghqc,bcgd->bqghd', p_cmp.astype(dtype), v_cmp)
        imp = p_cmp.sum(axis=2) @ cmp_to_slc
        cur = t // SLC_BLOCK
        valid = blk[None, :] * SLC_BLOCK <= t[:, None]
        forced = (blk[None, :] == 0) | (blk[None, :] == cur[:, None]) | (blk[None, :] == cur[:, None] - 1)
        score = jnp.where(valid, imp + jnp.where(forced, FORCE_BONUS, 0.0), NEG)
        _, sel = lax.top_k(score, topk)
        tok = (sel[..., None] * SLC_BLOCK + jnp.arange(SLC_BLOCK)).reshape(B, G, QB, topk * SLC_BLOCK)
        k_sel = ks_g[b_idx, g_idx, tok]
        v_sel = vs_g[b_idx, g_idx, tok]
        s = jnp.einsum('bqghd,bgqld->bghql', qi, k_sel).astype(jnp.float32) * scale
        s = s - slopes * (t[None, None, :, None] - tok).astype(jnp.float32)[:, :, None]
        p = masked_softmax(s, (tok <= t[None, None, :, None])[:, :, None])
        o_slc = jnp.einsum('bghql,bgqld->bqghd', p.astype(dtype), v_sel)
        start = bi * QB
        k_win = lax.dynamic_slice_in_dim(kw_pad, start, QB + WINDOW, axis=1)
        v_win = lax.dynamic_slice_in_dim(vw_pad, start, QB + WINDOW, axis=1)
        sp = start - WINDOW + jnp.arange(QB + WINDOW)
        wmask = (sp[None, :] <= t[:, None]) & (sp[None, :] > t[:, None] - WINDOW) & (sp[None, :] >= 0)
        s = jnp.einsum('bqghd,bkgd->bghqk', qi, k_win).astype(jnp.float32) * scale
        s = s - slopes * (t[:, None] - sp[None, :]).astype(jnp.float32)
        p = masked_softmax(s, wmask)
        o_win = jnp.einsum('bghqk,bkgd->bqghd', p.astype(dtype), v_win)
        g = jax.nn.sigmoid(gi.astype(jnp.float32)).astype(dtype)
        return g[..., 0:1] * o_cmp + g[..., 1:2] * o_slc + g[..., 2:3] * o_win

    o = lax.map(block, (qb, gb, jnp.arange(nqb)))
    return o.transpose(1, 0, 2, 3, 4, 5).reshape(B, S, H * d)

def odd_layer(x, norm_g, w_in, b_gate, pe_k, pe_v, wk1, wk2, wv1, wv2, w_out):
    B, S, _ = x.shape
    h = rms_norm(x, norm_g)
    u = h @ w_in
    q, kc, vc, ks, vs, kw, vw, gl, z = jnp.split(u, ODD_SPLITS, axis=-1)
    kv = lambda a: a.reshape(B, S, NSA_KV_GROUPS, HEAD_DIM)
    gl = (gl + b_gate).reshape(B, S, NSA_HEADS, N_BRANCH)
    o = nsa_attention(q.reshape(B, S, NSA_HEADS, HEAD_DIM), kv(kc), kv(vc), kv(ks), kv(vs), kv(kw), kv(vw),
                      gl, pe_k, pe_v, wk1, wk2, wv1, wv2)
    return x + (o * jax.nn.silu(z)) @ w_out

def first_inputs(seed: int = 0) -> dict:
    key = jax.random.key(seed)
    ks = jax.random.split(key, 24)
    ne = (DEPTH + 1) // 2
    no = DEPTH // 2
    nrm = lambda k, shape, sc: jax.random.normal(k, shape, jnp.float32) * sc
    fan_cmp = CMP_BLOCK * HEAD_DIM
    return {
        "x": nrm(ks[0], (BATCH, SEQ, D_MODEL), 1.0),
        "even_norm_g": 1.0 + nrm(ks[1], (ne, D_MODEL), 0.05),
        "even_w_in": nrm(ks[2], (ne, D_MODEL, EVEN_IN), D_MODEL ** -0.5),
        "even_b_f": 1.0 + nrm(ks[3], (ne, FOX_HEADS), 0.1),
        "even_gn_g": 1.0 + nrm(ks[4], (ne, RET_WIDTH), 0.05),
        "even_w_out": nrm(ks[5], (ne, EVEN_MIX_WIDTH, D_MODEL), EVEN_MIX_WIDTH ** -0.5),
        "odd_norm_g": 1.0 + nrm(ks[6], (no, D_MODEL), 0.05),
        "odd_w_in": nrm(ks[7], (no, D_MODEL, ODD_IN), D_MODEL ** -0.5),
        "odd_b_gate": nrm(ks[8], (no, NSA_HEADS * N_BRANCH), 0.1),
        "odd_pe_k": nrm(ks[9], (no, CMP_BLOCK, HEAD_DIM), 0.1),
        "odd_pe_v": nrm(ks[10], (no, CMP_BLOCK, HEAD_DIM), 0.1),
        "odd_wk1": nrm(ks[11], (no, fan_cmp, CMP_HIDDEN), fan_cmp ** -0.5),
        "odd_wk2": nrm(ks[12], (no, CMP_HIDDEN, HEAD_DIM), CMP_HIDDEN ** -0.5),
        "odd_wv1": nrm(ks[13], (no, fan_cmp, CMP_HIDDEN), fan_cmp ** -0.5),
        "odd_wv2": nrm(ks[14], (no, CMP_HIDDEN, HEAD_DIM), CMP_HIDDEN ** -0.5),
        "odd_w_out": nrm(ks[15], (no, NSA_WIDTH, D_MODEL), NSA_WIDTH ** -0.5),
        "final_g": 1.0 + nrm(ks[16], (D_MODEL,), 0.05),
    }

def first_block(x, even_norm_g, even_w_in, even_b_f, even_gn_g, even_w_out,
              odd_norm_g, odd_w_in, odd_b_gate, odd_pe_k, odd_pe_v, odd_wk1, odd_wk2, odd_wv1, odd_wv2, odd_w_out,
              final_g):
    for layer in range(DEPTH):
        i = layer // 2
        if layer % 2 == 0:
            x = even_layer(x, even_norm_g[i], even_w_in[i], even_b_f[i], even_gn_g[i], even_w_out[i])
        else:
            x = odd_layer(x, odd_norm_g[i], odd_w_in[i], odd_b_gate[i], odd_pe_k[i], odd_pe_v[i],
                          odd_wk1[i], odd_wk2[i], odd_wv1[i], odd_wv2[i], odd_w_out[i])
    return rms_norm(x, final_g)


DEPTH_2 = 1

HG_HEADS = 4
HG_DK = 128
HG_DV = 128
HG_WIDTH = HG_HEADS * HG_DV
SA_HEADS = 4
SA_DH = 64
SA_WIDTH = SA_HEADS * SA_DH
MEM_HEADS = 4
MEM_DH = 64
MEM_WIDTH = MEM_HEADS * MEM_DH
MIX_WIDTH = HG_WIDTH + SA_WIDTH + MEM_WIDTH
IDX_HEADS = 8
IDX_DH = 64
TOPK_MAX = 256
N_MEM = 256
D_FF = -(-8 * D_MODEL // (3 * 256)) * 256
CHUNK = 64
Q_BLOCK = 128
EPS = 1e-6
IN_SIZES = (HG_HEADS * HG_DK, HG_HEADS * HG_DK, HG_WIDTH, HG_WIDTH,
            SA_WIDTH, SA_WIDTH, SA_WIDTH,
            IDX_HEADS * IDX_DH, IDX_DH, IDX_HEADS,
            MEM_WIDTH)
IN_WIDTH = sum(IN_SIZES)


f32 = jnp.float32

def rmsnorm(x, gain):
    x32 = x.astype(f32)
    y = x32 * lax.rsqrt(jnp.mean(x32 * x32, axis=-1, keepdims=True) + EPS)
    return (y * gain.astype(f32)).astype(x.dtype)

def split_in(p):
    offs, acc = [], 0
    for s in IN_SIZES[:-1]:
        acc += s
        offs.append(acc)
    return jnp.split(p, offs, axis=-1)

def to_chunks(a, B, N):
    return a.reshape(B, N, CHUNK, a.shape[2], a.shape[3]).transpose(1, 0, 3, 2, 4)

def hgrn2_mix(q, f_logit, i, g, lb, out_gain):
    B, L = q.shape[:2]
    N = L // CHUNK
    lb = lb.reshape(HG_HEADS, HG_DK)
    z = f_logit.astype(f32)
    log_f = jnp.logaddexp(jnp.log(lb), jnp.log1p(-lb) + jax.nn.log_sigmoid(z))
    k = (1.0 - lb) * jax.nn.sigmoid(-z)
    qf = jax.nn.silu(q.astype(f32))
    xs = (to_chunks(qf, B, N), to_chunks(k, B, N),
          to_chunks(i.astype(f32), B, N), to_chunks(log_f, B, N))
    causal = jnp.tril(jnp.ones((CHUNK, CHUNK), dtype=bool))

    def step(S, inp):
        qc, kc, vc, gc = inp
        b = jnp.cumsum(gc, axis=2)
        o_inter = jnp.einsum('bhck,bhkv->bhcv', qc * jnp.exp(b), S)
        diff = b[:, :, :, None, :] - b[:, :, None, :, :]
        decay = jnp.exp(jnp.where(causal[:, :, None], diff, -jnp.inf))
        A = jnp.einsum('bhtk,bhtsk,bhsk->bhts', qc, decay, kc)
        o = o_inter + jnp.einsum('bhts,bhsv->bhtv', A, vc)
        b_last = b[:, :, -1:, :]
        S = jnp.exp(b_last[:, :, 0, :])[..., None] * S + \
            jnp.einsum('bhck,bhcv->bhkv', kc * jnp.exp(b_last - b), vc)
        return S, o

    S0 = jnp.zeros((B, HG_HEADS, HG_DK, HG_DV), f32)
    _, o = lax.scan(step, S0, xs)
    o = o.transpose(1, 0, 3, 2, 4).reshape(B, L, HG_HEADS, HG_DV)
    o = rmsnorm(o, out_gain) * jax.nn.silu(g.astype(f32))
    return o.reshape(B, L, HG_WIDTH).astype(q.dtype)

def dsa_mix(q, k, v, iq, ik, iw, q_gain, k_gain):
    B, L = q.shape[:2]
    topk = min(TOPK_MAX, L // 4)
    nb = L // Q_BLOCK
    q = rmsnorm(q, q_gain).astype(f32)
    k = rmsnorm(k, k_gain).astype(f32)
    v32 = v.astype(f32)
    ik32 = ik.astype(f32)
    iw32 = iw.astype(f32) * (IDX_HEADS ** -0.5 * IDX_DH ** -0.5)
    key_pos = jnp.arange(L)
    bidx = jnp.arange(B)[:, None, None]

    def blockify(a):
        return a.reshape(B, nb, Q_BLOCK, *a.shape[2:]).swapaxes(0, 1)

    def one_block(args):
        blk, qb, iqb, iwb = args
        qpos = blk * Q_BLOCK + jnp.arange(Q_BLOCK)
        s = jnp.einsum('bqhd,bsd->bqhs', iqb.astype(f32), ik32)
        score = jnp.einsum('bqh,bqhs->bqs', iwb, jax.nn.relu(s))
        visible = key_pos[None, :] <= qpos[:, None]
        score = jnp.where(visible[None], score, -jnp.inf)
        _, idx = lax.top_k(score, topk)
        valid = idx <= qpos[None, :, None]
        kg = k[bidx, idx]
        vg = v32[bidx, idx]
        logits = jnp.einsum('bqhd,bqkhd->bhqk', qb, kg) * (SA_DH ** -0.5)
        logits = jnp.where(valid[:, None], logits, -jnp.inf)
        p = jax.nn.softmax(logits, axis=-1)
        return jnp.einsum('bhqk,bqkhd->bqhd', p, vg)

    out = lax.map(one_block, (jnp.arange(nb), blockify(q), blockify(iq), blockify(iw32)))
    return out.swapaxes(0, 1).reshape(B, L, SA_WIDTH).astype(v.dtype)

def mem_mix(qm, mem_n, w_kv, q_gain, k_gain):
    B, L = qm.shape[:2]
    km, vm = jnp.split(mem_n @ w_kv, 2, axis=-1)
    M = mem_n.shape[1]
    km = km.reshape(B, M, MEM_HEADS, MEM_DH)
    vm = vm.reshape(B, M, MEM_HEADS, MEM_DH)
    qm = rmsnorm(qm, q_gain).astype(f32)
    km = rmsnorm(km, k_gain).astype(f32)
    logits = jnp.einsum('bqhd,bmhd->bhqm', qm, km) * (MEM_DH ** -0.5)
    p = jax.nn.softmax(logits, axis=-1)
    out = jnp.einsum('bhqm,bmhd->bqhd', p, vm.astype(f32))
    return out.reshape(B, L, MEM_WIDTH).astype(mem_n.dtype)

def second_inputs(seed: int = 0) -> dict:
    key = jax.random.key(seed)
    ks = jax.random.split(key, 16)
    nrm = jax.random.normal

    def gain(k, n):
        return 1.0 + 0.02 * nrm(k, (DEPTH_2, n), f32)

    return {
        "x": nrm(ks[0], (BATCH, SEQ, D_MODEL), f32),
        "mem": nrm(ks[1], (BATCH, N_MEM, D_MODEL), f32),
        "w_in": nrm(ks[2], (DEPTH_2, D_MODEL, IN_WIDTH), f32) * D_MODEL ** -0.5,
        "w_out": nrm(ks[3], (DEPTH_2, MIX_WIDTH, D_MODEL), f32) * MIX_WIDTH ** -0.5,
        "w_mem_kv": nrm(ks[4], (DEPTH_2, D_MODEL, 2 * MEM_WIDTH), f32) * D_MODEL ** -0.5,
        "lb_logits": nrm(ks[5], (DEPTH_2, HG_HEADS * HG_DK), f32),
        "norm_mix": gain(ks[6], D_MODEL),
        "norm_mem": gain(ks[7], D_MODEL),
        "norm_ffn": gain(ks[8], D_MODEL),
        "hg_out_gain": gain(ks[9], HG_DV),
        "sa_q_gain": gain(ks[10], SA_DH),
        "sa_k_gain": gain(ks[11], SA_DH),
        "mem_q_gain": gain(ks[12], MEM_DH),
        "mem_k_gain": gain(ks[13], MEM_DH),
        "w_ffn_in": nrm(ks[14], (DEPTH_2, D_MODEL, 2 * D_FF), f32) * D_MODEL ** -0.5,
        "w_ffn_out": nrm(ks[15], (DEPTH_2, D_FF, D_MODEL), f32) * D_FF ** -0.5,
    }

def second_block(x, mem, w_in, w_out, w_mem_kv, lb_logits, norm_mix, norm_mem, norm_ffn,
              hg_out_gain, sa_q_gain, sa_k_gain, mem_q_gain, mem_k_gain,
              w_ffn_in, w_ffn_out):
    B, L, _ = x.shape
    lb = jnp.cumsum(jax.nn.softmax(lb_logits.astype(f32), axis=0), axis=0)
    lb = lb - lb[0:1]
    for layer in range(DEPTH_2):
        h = rmsnorm(x, norm_mix[layer])
        hq, hf, hi, hg, sq, sk, sv, iq, ik, iw, mq = split_in(h @ w_in[layer])
        o_hg = hgrn2_mix(hq.reshape(B, L, HG_HEADS, HG_DK), hf.reshape(B, L, HG_HEADS, HG_DK),
                         hi.reshape(B, L, HG_HEADS, HG_DV), hg.reshape(B, L, HG_HEADS, HG_DV),
                         lb[layer], hg_out_gain[layer])
        o_sa = dsa_mix(sq.reshape(B, L, SA_HEADS, SA_DH), sk.reshape(B, L, SA_HEADS, SA_DH),
                       sv.reshape(B, L, SA_HEADS, SA_DH), iq.reshape(B, L, IDX_HEADS, IDX_DH),
                       ik, iw, sa_q_gain[layer], sa_k_gain[layer])
        mem_n = rmsnorm(mem, norm_mem[layer])
        o_mem = mem_mix(mq.reshape(B, L, MEM_HEADS, MEM_DH), mem_n, w_mem_kv[layer],
                        mem_q_gain[layer], mem_k_gain[layer])
        mixed = jnp.concatenate([o_hg, o_sa, o_mem], axis=-1)
        x = x + (mixed @ w_out[layer]).astype(x.dtype)
        h = rmsnorm(x, norm_ffn[layer])
        a, b = jnp.split(h @ w_ffn_in[layer], 2, axis=-1)
        x = x + ((jax.nn.silu(a) * b) @ w_ffn_out[layer]).astype(x.dtype)
    return x


def setup_inputs(seed=0):
    out = dict(first_inputs(seed))
    for name, value in second_inputs(seed + 1).items():
        if name != "x":
            out[name + "_2"] = value
    return out


def reference(
    x, even_norm_g, even_w_in, even_b_f, even_gn_g, even_w_out, odd_norm_g, odd_w_in,
    odd_b_gate, odd_pe_k, odd_pe_v, odd_wk1, odd_wk2, odd_wv1, odd_wv2, odd_w_out, final_g,
    mem_2, w_in_2, w_out_2, w_mem_kv_2, lb_logits_2, norm_mix_2, norm_mem_2, norm_ffn_2,
    hg_out_gain_2, sa_q_gain_2, sa_k_gain_2, mem_q_gain_2, mem_k_gain_2, w_ffn_in_2,
    w_ffn_out_2,
):
    x = first_block(
        x, even_norm_g, even_w_in, even_b_f, even_gn_g, even_w_out, odd_norm_g, odd_w_in,
        odd_b_gate, odd_pe_k, odd_pe_v, odd_wk1, odd_wk2, odd_wv1, odd_wv2, odd_w_out, final_g,
    )
    return second_block(
        x, mem_2, w_in_2, w_out_2, w_mem_kv_2, lb_logits_2, norm_mix_2, norm_mem_2, norm_ffn_2,
        hg_out_gain_2, sa_q_gain_2, sa_k_gain_2, mem_q_gain_2, mem_k_gain_2, w_ffn_in_2,
        w_ffn_out_2,
    )


_drawn_inputs = setup_inputs


def setup_inputs(seed=0):
    import zlib

    import numpy as np

    out = dict(_drawn_inputs(seed))
    spreads = {}
    factors = {'even_b_f': 3.383,
     'odd_b_gate': 4.829,
     'odd_pe_k': 8.0,
     'odd_pe_v': 2.674,
     'norm_mix_2': 3.634,
     'norm_mem_2': 23.878,
     'norm_ffn_2': 12.174,
     'hg_out_gain_2': 21.301,
     'sa_q_gain_2': 134.562,
     'sa_k_gain_2': 113.313,
     'mem_q_gain_2': 8.0,
     'mem_k_gain_2': 25.074}
    for name, (base, spread) in spreads.items():
        noise = np.random.default_rng([zlib.crc32(name.encode()), seed]).standard_normal(out[name].shape)
        drawn = base * np.exp(spread * noise) if base else spread * noise
        out[name] = __import__('jax').numpy.asarray(drawn.astype(out[name].dtype))
    for name, factor in factors.items():
        out[name] = (out[name] * factor).astype(out[name].dtype)
    return out
```

```python
from contextlib import ExitStack

import numpy as np
import concourse.bass as bass
from concourse import mybir

f32 = mybir.dt.float32
f32r = mybir.dt.float32r
bf16 = mybir.dt.bfloat16
u32 = mybir.dt.uint32
ALU = mybir.AluOpType
ACT = mybir.ActivationFunctionType
AX = mybir.AxisListType

P = 128
T = 512
NT = T // P
D = 1024
NK = D // P
HD = 64
R = 4
FF = 2816
NF = FF // P
NEG = -1e30
TAKEN = -3e38
RMS_EPS = 1e-6
GN_EPS = 1e-5
CMP = 31
CREDIT = 16
HALVES = [64, 32, 16, 8, 4, 2, 1]
S_BANK, T_BANK, O_BANK = (0, 1, 4, 5), (6, 7), (2, 3)
FFN_ORDER = (0, 2, 1, 3)

STREAM = [("mem", 1, 4), ("even_qk", 4, 4), ("even_v", 2, 4), ("even_z", 2, 4), ("even_out", 2, 4),
          ("odd_q", 2, 4), ("odd_kv", 2, 4), ("odd_v", 1, 4), ("odd_z", 2, 4), ("cmp", 2, 0), ("odd_out", 2, 4),
          ("hg_f", 2, 4), ("hg_n", 2, 4), ("sa_i", 1, 4), ("sa_n", 2, 4), ("sec_out", 2, 4), ("ffn_in", 11, 4)]
BLOCKS = {name: n for name, n, _ in STREAM}
CH, OUT, ODONE = {}, {}, {}
_c = _o = _d = 0
for _name, _blocks, _outs in STREAM:
    CH[_name], OUT[_name], ODONE[_name] = _c, _o, _d
    _c, _o, _d = _c + R * _blocks, _o + _outs * _blocks, _d + (1 if _name == "mem" else max(_outs - 1, 0)) * _blocks
CH["ffn_out"], OUT["ffn_out"], ODONE["ffn_out"] = _c, _o, _d
OUT_CHUNKS = NF // 2
UNITS = {"fox": 0, "odd": 32, "sa": 160, "mem": 176, "end": 192}

FEATURES = ("mem", "even", "even_y", "odd", "odd_y", "sec", "sec_y", "ffn")
SQUARES = {"mem": 0, "even": 2, "odd": 6, "fin": 10, "sec": 14, "ffn": 18}
NORMED = {"mem": 0, "even": 2, "even_y": 6, "odd": 10, "odd_y": 14, "sec": 18, "ffn": 22}
RSTDS = ("mem", "even", "gn", "odd", "fin", "sec", "hgo", "sa", "ffn")
AT = {name: NK * i for i, name in enumerate(FEATURES)}

GAINS = [("norm_mem_2", 0), ("even_norm_g", 0), ("even_gn_g", 4), ("odd_norm_g", 0), ("norm_mix_2", 0),
         ("norm_ffn_2", 0)]
G_MEM, G_EVEN, G_GN, G_ODD, G_SEC, G_FFN, G_HG = range(7)
HEAD_GAINS = ["sa_q_gain_2", "sa_k_gain_2", "mem_q_gain_2", "mem_k_gain_2"]
N_CONST = 4 + len(GAINS) + 1 + 2 * len(HEAD_GAINS)


def program(nc, w, c, out):
    ctx = ExitStack()
    with ctx:
        def sb(on, name, shape, dt=f32):
            return on.enter_context(nc.sbuf_tensor(name, shape, dt))

        made = {}

        def sem(name):
            if name not in made:
                made[name] = ctx.enter_context(nc.semaphore(name))
            return made[name]

        X = sb(ctx, "x_tokens", [P, NT, D])
        RAW = sb(ctx, "weight_raw", [P, R, 2, 512])
        WH = sb(ctx, "weight_high", [P, R, 2, 512], f32r)
        WL = sb(ctx, "weight_low", [P, R, 2, 512], f32r)
        SMR = sb(ctx, "small_raw", [P, NK, 72])
        SMH = sb(ctx, "small_high", [P, NK, 72], f32r)
        SML = sb(ctx, "small_low", [P, NK, 72], f32r)
        ID = sb(ctx, "identity", [P, P])
        IDB = sb(ctx, "identity_bf16", [P, P], bf16)
        CAUSAL = sb(ctx, "causal_bf16", [P, P], bf16)
        MINUS3 = sb(ctx, "minus_ones_bf16", [3, P], bf16)
        HALF = sb(ctx, "minus_half", [P, 64])
        SS = sb(ctx, "mean_squares", [P, 64])
        RS = sb(ctx, "rstd", [P, 64])
        NMAX = sb(ctx, "minus_max", [P, 4])
        SUM = sb(ctx, "sums", [P, 4])
        RSUM = sb(ctx, "one_over_sum", [P, 4])
        SCL = sb(ctx, "gate_over_sum", [P, 4])
        GAIN = sb(ctx, "gains", [P, 12, NK])
        MEMKV = sb(ctx, "mem_k_v", [P, 2, 512])

        lay = ExitStack()
        AH = sb(lay, "act_high", [P, NK, T], f32r)
        AL = sb(lay, "act_low", [P, NK, T], f32r)
        H = sb(lay, "h_tokens", [P, NT, D])
        lay_e = ExitStack()
        E_UT = sb(lay_e, "even_qk", [P, 16, T])
        E_V = sb(lay_e, "even_v", [P, NT, D])
        E_Z = sb(lay_e, "even_silu_z", [P, NT, D])
        FL = sb(lay_e, "forget_tokens", [P, NT, 8])
        FL2 = sb(lay_e, "forget_abs", [P, NT, 8])
        BF = sb(lay_e, "forget_bias", [P, 8])
        lay_e.close()
        lay_o = ExitStack()
        O_Q = sb(lay_o, "odd_q", [P, 8, T])
        O_K = sb(lay_o, "odd_k", [P, 2, 4, T])
        O_V = sb(lay_o, "odd_v", [P, NT, 512])
        O_Z = sb(lay_o, "odd_silu_z", [P, NT, D])
        KCVC = sb(lay_o, "kc_vc", [P, 4, T])
        ALS = sb(lay_o, "alibi_slopes", [P, 16, P], bf16)
        ALJ = sb(lay_o, "alibi_positions", [P, T], bf16)
        GATE = sb(lay_o, "gates", [P, NT, 48])
        BG = sb(lay_o, "gate_bias", [P, 48])
        PE2 = sb(lay_o, "cmp_pe", [P, 2, 16])
        W2 = sb(lay_o, "cmp_w2", [P, 2, 2, HD])
        W2D = sb(lay_o, "cmp_w2_twice", [P, 2, 2, HD])
        CHID = sb(lay_o, "cmp_hidden", [P, 2, 2, 4, 32])
        lay_o.close()
        lay_s = ExitStack()
        S_N = sb(lay_s, "sa_q_k_v_mq", [P, NT, D])
        I_Q = sb(lay_s, "index_q", [P, 4, T])
        I_K = sb(lay_s, "index_k", [P, T])
        I_KN = sb(lay_s, "index_k_tokens", [P, NT, P])
        I_W = sb(lay_s, "index_w", [P, NT, 8])
        lay_g = ExitStack()
        G_F = sb(lay_g, "hg_q_f", [P, 8, T])
        G_N = sb(lay_g, "hg_i_g", [P, NT, D])
        G_B = sb(lay_g, "hg_cumsum", [P, 4, T])
        G_M = sb(lay_g, "hg_masks", [P, 8, P], u32)
        G_S = sb(lay_g, "hg_state", [P, 4, 3, P])
        G_X = sb(lay_g, "hg_last", [P, 4, NT])
        lay_g.close()
        lay_a = ExitStack()
        S_2 = sb(lay_a, "sa_squares", [P, NT, D])
        S_QK = sb(lay_a, "sa_q_k", [P, 4, T])
        M_Q = sb(lay_a, "mem_q", [P, 2, T])
        M_K = sb(lay_a, "mem_k", [P, 2, 2 * P])
        RL = sb(lay_a, "index_relu", [P, 2, T])
        SCO = sb(lay_a, "index_scores", [P, T])
        SCP = sb(lay_a, "index_left", [P, T])
        MX8 = sb(lay_a, "max8", [P, 8])
        SEL = sb(lay_a, "sel_mask", [P, NT, T], bf16)
        MASKF = sb(lay_a, "causal_f32", [P, P])
        lay_a.close()
        lay_s.close()
        lay.close()
        ov = ExitStack()
        E_Q = sb(ov, "even_q_stage", [P, 2, T])
        E_K = sb(ov, "even_k_stage", [P, 2, T])
        E_P = sb(ov, "even_probs", [P, 2, T])
        E_PT = sb(ov, "even_probs_t", [P, 2, T])
        ov1 = ExitStack()
        FB = sb(ov1, "forget_parts", [8, 3, T], bf16)
        FC = sb(ov1, "forget_cumsum", [8, T])
        FO = sb(ov1, "forget_ones", [8, T])
        ov1.close()
        RD = sb(ov, "retention_decay", [P, 2, 2, T])
        C3 = sb(ov, "decay_rows", [3, 8, T], bf16)
        ov.close()
        ovc = ExitStack()
        CI = sb(ovc, "cmp_in", [P, 16, 4, CMP])
        CIH = sb(ovc, "cmp_in_high", [P, 16, 4 * CMP], f32r)
        CIL = sb(ovc, "cmp_in_low", [P, 16, 4 * CMP], f32r)
        CB = sb(ovc, "cmp_bias", [P, 16, 32])
        KCMP = sb(ovc, "k_cmp", [P, 4, 32])
        BDV = sb(ovc, "v_cmp_blocks", [P, 4, 4, HD])
        ovc.close()
        ovd = ExitStack()
        SC = sb(ovd, "cmp_scores", [P, 16, 32])
        CPT = sb(ovd, "cmp_probs_t", [P, 4, P])
        CMX = sb(ovd, "cmp_max", [P, 4, 16])
        ovd.close()
        ovo = ExitStack()
        O_QS = sb(ovo, "odd_q_stage", [P, 2, 2, T])
        O_KS = sb(ovo, "odd_k_stage", [P, 2, T])
        O_P = sb(ovo, "odd_probs", [P, 2, T])
        O_PT = sb(ovo, "odd_probs_t", [P, 2, T])
        ovo.close()
        ovg = ExitStack()
        G_E = sb(ovg, "hg_decay", [P, 2, 4, T])
        G_A = sb(ovg, "hg_weights", [P, 4, 4, P])
        G_KT = sb(ovg, "hg_key_tokens", [P, 4, 3, P])
        G_R = sb(ovg, "scan_reset", [P, T])
        ovg.close()
        ovf = ExitStack()
        FING = sb(ovf, "final_gain", [P, D])
        ovf.close()
        ova = ExitStack()
        S_P = sb(ova, "sa_probs", [P, 2, T])
        S_PT = sb(ova, "sa_probs_t", [P, 2, T])
        ova.close()
        ffn = ExitStack()
        sb(ffn, "act_still_there", [P, 2 * NK * T])
        FH = sb(ffn, "ffn_high", [P, NF, T], f32r)
        FLO = sb(ffn, "ffn_low", [P, NF, T], f32r)
        FT = sb(ffn, "ffn_silu", [P, 2, T])
        ffn.close()

        PS = ctx.enter_context(nc.psum_tensor("psum", [P, 8, 512], f32))

        raw_ready = [sem(f"raw_ready{i}") for i in range(R)]
        high_ready = sem("high_ready")
        split_ready = sem("split_ready")
        chunk_done = sem("chunk_done")
        out_done = sem("out_done")
        bank_free = sem("bank_free")
        squares_ready = sem("squares_ready")
        mean_ready = sem("mean_ready")
        rstd_ready = sem("rstd_ready")
        normed_ready = sem("normed_ready")
        turned = sem("turned")
        act_high = sem("act_high")
        act_low = sem("act_low")
        sc_ready = sem("scores_ready")
        mx_ready = sem("max_ready")
        p_ready = sem("probs_ready")
        t_ready = sem("transposed_ready")
        pt_ready = sem("probs_t_ready")
        o_ready = sem("values_ready")
        o_done = sem("output_taken")

        def wait_out(eng, name, i, k, last):
            outs = 2 if name == "mem" else 4
            if last:
                eng.wait_ge(chunk_done, R + CH[name] + R * i + R)
            else:
                eng.wait_ge(out_done, ODONE[name] + (outs - 1) * i + k + 1)

        def wait_group(eng, name):
            eng.wait_ge(bank_free, 4 + OUT[name] + BLOCKS[name] * 4)

        block = ctx.enter_context(nc.Block())

        @block.sync
        def _(sp):
            sp.dma_start(H[:, 0:2, :], w["mem_2"][0].rearrange("(t p) d -> p t d", p=P)).then_inc(sem("mem_loaded"), 16)

            def chunk(n, parts):
                if n >= R:
                    sp.wait_ge(split_ready, n - R + 1)
                for at, src in parts:
                    sp.dma_start(RAW[:, n % R, :, at:at + src.shape[1]],
                                 src.rearrange("(k p) n -> p k n", p=P)).then_inc(
                                     raw_ready[n % R], 32 // len(parts))

            def load_block(n, mat, parts):
                for r in range(R):
                    chunk(n + r, [(at, mat[256 * r:256 * r + 256, a:a + m]) for at, a, m in parts])

            def small(k, mat, a, m):
                if k:
                    sp.wait_ge(sem("small_done"), k)
                sp.dma_start(SMR[:, :, 0:m], mat[:, a:a + m].rearrange("(k p) n -> p k n", p=P)).then_inc(
                    sem("small_loaded"), 16)

            load_block(CH["mem"], w["w_mem_kv_2"][0], [(0, 0, 512)])
            sp.dma_start(X[:, :, :], w["x"][0].rearrange("(t p) d -> p t d", p=P)).then_inc(sem("x_loaded"), 16)
            we = w["even_w_in"][0]
            small(0, we, 1536, 8)
            for i, a in enumerate((0, 512, 1544, 2056)):
                load_block(CH["even_qk"] + R * i, we, [(0, a, 512)])
            for i, a in enumerate((1024, 2568)):
                load_block(CH["even_v"] + R * i, we, [(0, a, 512)])
            for i in range(2):
                load_block(CH["even_z"] + R * i, we, [(0, 3080 + 512 * i, 512)])
            for i in range(2):
                load_block(CH["even_out"] + R * i, w["even_w_out"][0], [(0, 512 * i, 512)])
            wo = w["odd_w_in"][0]
            small(1, wo, 2560, 48)
            for i in range(2):
                load_block(CH["odd_q"] + R * i, wo, [(0, 512 * i, 512)])
            load_block(CH["odd_kv"], wo, [(0, 1024, 512)])
            load_block(CH["odd_kv"] + R, wo, [(0, 1536, 256), (256, 2048, 256)])
            load_block(CH["odd_v"], wo, [(0, 1792, 256), (256, 2304, 256)])
            for i in range(2):
                load_block(CH["odd_z"] + R * i, wo, [(0, 2608 + 512 * i, 512)])
            for i, name in enumerate(("odd_wk1", "odd_wv1")):
                for r in range(R):
                    n = CH["cmp"] + R * i + r
                    sp.wait_ge(split_ready, n - R + 1)
                    sp.dma_start(RAW[:, n % R, :, :].rearrange("p a (b n) -> p (a b) n", b=2),
                                 w[name][0][512 * r:512 * r + 512, :].rearrange("(k p) n -> p k n", p=P)).then_inc(
                                     raw_ready[n % R], 32)
            for i in range(2):
                load_block(CH["odd_out"] + R * i, w["odd_w_out"][0], [(0, 512 * i, 512)])
            w2 = w["w_in_2"][0]
            small(2, w2, 3328, 72)
            for i in range(2):
                load_block(CH["hg_f"] + R * i, w2, [(0, 512 * i, 512)])
            for i in range(2):
                load_block(CH["hg_n"] + R * i, w2, [(0, 1024 + 512 * i, 512)])
            load_block(CH["sa_i"], w2, [(0, 2816, 512)])
            load_block(CH["sa_n"], w2, [(0, 2048, 512)])
            load_block(CH["sa_n"] + R, w2, [(0, 2560, 256), (256, 3400, 256)])
            for i in range(2):
                load_block(CH["sec_out"] + R * i, w["w_out_2"][0], [(0, 512 * i, 512)])
            for i in range(BLOCKS["ffn_in"]):
                load_block(CH["ffn_in"] + R * i, w["w_ffn_in_2"][0], [(0, 256 * i, 256), (256, FF + 256 * i, 256)])
            for i in range(2):
                for r in range(OUT_CHUNKS):
                    chunk(CH["ffn_out"] + OUT_CHUNKS * i + r,
                          [(0, w["w_ffn_out_2"][0][256 * r:256 * r + 256, 512 * i:512 * i + 512])])
            for i in range(2):
                sp.wait_ge(bank_free, 4 + OUT["ffn_out"] + 4 * (i + 1))
                sp.dma_start(out[0].rearrange("(t p) d -> p t d", p=P)[:, :, 512 * i:512 * i + 512],
                             X[:, :, 512 * i:512 * i + 512]).then_inc(sem("stored"), 16)
            sp.wait_ge(sem("stored"), 32)

        @block.gpsimd
        def _(pool):
            def load(dst, src, name):
                pool.dma_start(dst, src).then_inc(sem(name), 16)

            def split(n0, blocks):
                with pool.Fori(0, blocks) as i:
                    for r in range(R):
                        pool.wait_ge(high_ready, n0 + R * i + r + 1)
                        nc.gpsimd.tensor_tensor(WL[:, r], RAW[:, r], WH[:, r].bitcast(f32),
                                                ALU.subtract).then_inc(split_ready, 1)

            def split_ahead(name):
                split(CH[name] + R, BLOCKS[name])

            def small_split(k, m):
                pool.wait_ge(sem("small_high"), k + 1)
                nc.gpsimd.tensor_tensor(SML[:, :, 0:m], SMR[:, :, 0:m], SMH[:, :, 0:m].bitcast(f32),
                                        ALU.subtract).then_inc(sem("small_low"), 1)

            def rstd(use, n):
                pool.wait_ge(mean_ready, RSTDS.index(use) + 1)
                nc.gpsimd.tensor_tensor(RS[:, 0:n], SS[:, 0:n], HALF[:, 0:n], ALU.pow).then_inc(rstd_ready, 1)

            nc.gpsimd.memset(HALF[:, :], -0.5)
            nc.gpsimd.memset(GAIN[:, G_GN, 0:4], 1.0)
            nc.gpsimd.memset(GAIN[:, G_HG, 4:8], 1.0).then_inc(sem("half_ready"), 1)
            pool.wait_ge(sem("half_ready"), 1)
            load(ID[:, :], c["identity"], "const")
            load(IDB[:, :], c["identity_bf16"], "const")
            load(CAUSAL[:, :], c["causal_bf16"], "const")
            load(MINUS3[:, :], c["minus_one3"], "const")
            with nc.allow_non_contiguous_dma(reason="gain vectors, once"):
                for i, (name, first) in enumerate(GAINS):
                    load(GAIN[:, i, first:NK], w[name][0].rearrange("(k p) -> p k", p=P), "const")
                load(GAIN[:, G_HG, 0:1], w["hg_out_gain_2"][0].rearrange("(d o) -> d o", o=1), "const")
                for i, name in enumerate(HEAD_GAINS):
                    for half in range(2):
                        load(GAIN[HD * half:HD * half + HD, 8 + i, 0:1],
                             w[name][0].rearrange("(d o) -> d o", o=1), "const")
            load(BF[:, :], w["even_b_f"][0:1, :].to_broadcast((P, 8)), "forget_bias")
            split(0, 1)
            rstd("mem", 2)
            rstd("even", NT)
            split_ahead("mem")
            small_split(0, 8)
            split_ahead("even_qk")
            split_ahead("even_v")
            split_ahead("even_z")
            pool.wait_ge(sem("forget_parts"), 1)
            for i in range(3):
                load(C3[i:i + 1, :, :], FB[:, i, :], "decay_rows")
            with pool.Fori(0, 2) as i:
                for b in range(2):
                    pool.wait_ge(sc_ready, CREDIT + UNITS["fox"] + 8 * (2 * i + b) - 8)
                    nc.gpsimd.tensor_copy(E_K[:, b, :], E_UT[:, bass.ds(4 + 2 * i + b, 1), :].rearrange(
                        "p a t -> p (a t)")).then_inc(sem("k_staged"), 1)
            pool.wait_ge(sc_ready, CREDIT + UNITS["odd"])
            with pool.Fori(0, 2) as i:
                for b in range(2):
                    pool.wait_ge(sem("ret_used"), CREDIT + 8 * (2 * i + b) - 8)
                    load(RD[:, b], c["retention"][:, bass.ds(4 * i + 2 * b, 2), :], f"ret_decay{b}")
                    nc.gpsimd.tensor_copy(E_K[:, b, :], E_UT[:, bass.ds(12 + 2 * i + b, 1), :].rearrange(
                        "p a t -> p (a t)")).then_inc(sem("ret_k_staged"), 1)
            rstd("gn", 32)
            split_ahead("even_out")
            rstd("odd", NT)
            wait_group(pool, "even_out")
            load(ALS[:, :, :], c["alibi_slopes"], "odd_tables")
            load(ALJ[:, :], c["alibi_positions"], "odd_tables")
            load(BG[:, :], w["odd_b_gate"][0:1, :].to_broadcast((P, 48)), "odd_tables")
            with nc.allow_non_contiguous_dma(reason="position vectors, once"):
                for i, name in enumerate(("odd_pe_k", "odd_pe_v")):
                    for l in range(2):
                        load(PE2[HD * l:HD * l + HD, i, :],
                             w[name][0].rearrange("(a l) d -> d l a", l=2)[:, l, :], "odd_tables")
            for i, name in enumerate(("odd_wk2", "odd_wv2")):
                load(W2[:, i, :, :], w[name][0].rearrange("(k p) d -> p k d", p=P), "odd_tables")
            for k in range(2):
                load(W2D[:, :, k, :], w["odd_wk2"][0].rearrange("(k p) d -> p k d", p=P), "odd_tables")
            nc.gpsimd.memset(CHID[:, :, :, :, :], 0.0).then_inc(sem("cmp_hidden_zero"), 1)
            small_split(1, 48)
            split_ahead("odd_q")
            split_ahead("odd_kv")
            split_ahead("odd_v")
            split_ahead("odd_z")
            split_ahead("cmp")
            for t in range(NT):
                if t:
                    pool.wait_ge(sem("cmp_biased"), t)
                else:
                    pool.wait_ge(chunk_done, R + CH["cmp"])
                load(CB[:, :, :], c["cmp_bias"][:, t], "cmp_bias")
            pool.wait_ge(sem("cmp_taken"), 2 * NT)
            with pool.Fori(0, 4) as i:
                for b in range(2):
                    pool.wait_ge(sc_ready, CREDIT + UNITS["odd"] + 16 * (2 * i + b) - 16)
                    nc.gpsimd.tensor_copy(O_KS[:, b, :], O_K[:, b, bass.ds(i, 1), :].rearrange(
                        "p a t -> p (a t)")).then_inc(sem("k_staged"), 1)
            split_ahead("odd_out")
            rstd("fin", NT)
            wait_group(pool, "odd_out")
            load(FING[:, :], w["final_g"].rearrange("(o d) -> o d", o=1).to_broadcast((P, D)), "final_gain")
            load(G_M[:, :, :], c["tree_masks"], "sec_tables")
            rstd("sec", NT)
            for name in ("hg_f", "hg_n", "sa_i", "sa_n"):
                if name == "sa_i":
                    small_split(2, 72)
                split_ahead(name)
            pool.wait_ge(sem("small_done"), 3)
            load(G_R[:, :], c["scan_reset"], "scan_reset")
            rstd("hgo", 16)
            pool.wait_ge(sem("hg_gated"), 1)
            load(MASKF[:, :], c["causal_f32"], "sa_tables")
            rstd("sa", 56)
            split_ahead("sec_out")
            rstd("ffn", NT)
            split_ahead("ffn_in")
            split(CH["ffn_out"] + R, 4)
            for r in range(2):
                pool.wait_ge(high_ready, CH["ffn_out"] + 5 * R + r + 1)
                nc.gpsimd.tensor_tensor(WL[:, r], RAW[:, r], WH[:, r].bitcast(f32),
                                        ALU.subtract).then_inc(split_ready, 1)

        @block.scalar
        def _(act):
            act.sem_inc(p_ready, CREDIT)
            act.sem_inc(sem("ret_taken"), CREDIT)

            def split(n0, blocks):
                def body(i):
                    for r in range(R):
                        act.wait_ge(raw_ready[r], 32 * (n0 // R + i + 1))
                        act.wait_ge(chunk_done, n0 + R * i + r + 1)
                        nc.scalar.activation(WH[:, r], RAW[:, r], ACT.Copy).then_inc(high_ready, 1)
                if blocks == 1:
                    body(0)
                else:
                    with act.Fori(0, blocks) as i:
                        body(i)

            def split_ahead(name):
                split(CH[name] + R, BLOCKS[name])

            def small_split(k, m):
                act.wait_ge(sem("small_loaded"), 16 * (k + 1))
                nc.scalar.activation(SMH[:, :, 0:m], SMR[:, :, 0:m], ACT.Copy).then_inc(sem("small_high"), 1)

            def squares(use, src, dst, nt=NT):
                for t in range(nt):
                    nc.scalar.activation(dst[:, t, :], src[:, t, :], ACT.Square,
                                         accum_out=SS[:, t:t + 1]).then_inc(squares_ready, 1)

            def features(use, gain, nt=NT):
                for k in range(NK):
                    act.wait_ge(turned, AT[use] + k + 1)
                    g = 0 if gain == G_HG and k < 4 else k
                    scale = 1.0 if gain is None else GAIN[:, gain, g:g + 1]
                    nc.scalar.activation(AH[:, k, 0:P * nt], PS[:, 4 + k % 4, 0:P * nt],
                                         ACT.Identity, scale=scale).then_inc(act_high, 1)

            def exps(at0, nu, ext, probs):
                for u in range(nu):
                    act.wait_ge(mx_ready, CREDIT + at0 + u + 1)
                    act.wait_ge(t_ready, CREDIT + at0 + u - 1)
                    n = ext(u)
                    nc.scalar.activation(probs[:, u % 2, 0:n], PS[:, S_BANK[u % 4], 0:n], ACT.Exp,
                                         bias=NMAX[:, u % 4:u % 4 + 1],
                                         accum_out=SUM[:, u % 4:u % 4 + 1]).then_inc(p_ready, 1)

            def causal_ext(u):
                return P * (u % 4 + 1)

            def silu_z(name, dst):
                for i in range(2):
                    split(CH[name] + R + R * i, 1)
                    for j in range(4):
                        wait_out(act, name, i, j, j == 3)
                        nc.scalar.activation(dst[:, j, 512 * i:512 * i + 512], PS[:, j, :],
                                             ACT.Silu).then_inc(bank_free, 1)

            split(0, 1)
            act.wait_ge(sem("mem_loaded"), 16)
            act.wait_ge(sem("const"), 16 * N_CONST)
            act.wait_ge(sem("half_ready"), 1)
            squares("mem", H, H[:, 2:4, :], 2)
            features("mem", G_MEM, 2)
            act.wait_ge(sem("x_loaded"), 16)
            squares("even", X, H)
            split_ahead("mem")
            small_split(0, 8)
            features("even", G_EVEN)
            split_ahead("even_qk")
            split_ahead("even_v")
            act.wait_ge(sem("forget_abs"), 1)
            nc.scalar.activation(FL2[:, :, :], FL2[:, :, :], ACT.Exp, scale=-1.0)
            nc.scalar.drain()
            nc.scalar.activation(FL2[:, :, :], FL2[:, :, :], ACT.Ln, bias=1.0).then_inc(sem("forget_ln"), 1)
            silu_z("even_z", E_Z)
            with act.Fori(0, 2) as i:
                for b in range(2):
                    at0 = UNITS["fox"] + 8 * (2 * i + b)
                    act.wait_ge(sc_ready, CREDIT + at0 - 8)
                    nc.scalar.activation(E_Q[:, b, :], E_UT[:, bass.ds(2 * i + b, 1), :].rearrange(
                        "p a t -> p (a t)"), ACT.Copy, scale=0.125).then_inc(sem("q_staged"), 1)
                    exps(at0, 8, causal_ext, E_P)
            with act.Fori(0, 2) as i:
                for b in range(2):
                    at0 = 8 * (2 * i + b)
                    act.wait_ge(sem("ret_used"), CREDIT + at0 - 8)
                    nc.scalar.activation(E_Q[:, b, :], E_UT[:, bass.ds(8 + 2 * i + b, 1), :].rearrange(
                        "p a t -> p (a t)"), ACT.Copy, scale=0.125).then_inc(sem("ret_q_staged"), 1)
                    for a in range(2):
                        act.wait_ge(sem("ret_used"), CREDIT + at0 + 4 * a + 4)
                        nc.scalar.activation(H[:, :, bass.ds(512 + 256 * i + HD * (2 * b + a), HD)],
                                             PS[:, O_BANK[a], 0:4 * HD].rearrange("p (t d) -> p t d", t=4),
                                             ACT.Copy).then_inc(sem("ret_taken"), 1)
            act.wait_ge(sem("gn_centered"), 1)
            nc.scalar.activation(E_UT[:, 8:12, :], H[:, :, 512:1024], ACT.Square).then_inc(sem("gn_squared"), 1)
            features("even_y", G_GN)
            split_ahead("even_out")
            wait_group(act, "even_out")
            squares("odd", X, H)
            features("odd", G_ODD)
            small_split(1, 48)
            split_ahead("odd_q")
            split_ahead("odd_kv")
            split_ahead("odd_v")
            act.wait_ge(sem("gate_sum"), 1)
            nc.scalar.activation(GATE[:, :, :], GATE[:, :, :], ACT.Sigmoid).then_inc(sem("gates"), 1)
            silu_z("odd_z", O_Z)
            for i in range(2):
                act.wait_ge(sem("cmp_in"), i + 1)
                nc.scalar.activation(CIH[:, :, :], CI[:, :, :, :].rearrange("p l g c -> p l (g c)"),
                                     ACT.Copy).then_inc(sem("cmp_high"), 1)
                split(CH["cmp"] + R + R * i, 1)
                act.wait_ge(chunk_done, R + CH["cmp"] + R * i + R)
                if i == 0:
                    act.wait_ge(sem("cmp_hidden_zero"), 1)
                for h in range(2):
                    nc.scalar.activation(CHID[:, i, h, :, 0:CMP],
                                         PS[:, 4 + 2 * i + h, 0:4 * CMP].rearrange("p (g c) -> p g c", g=4),
                                         ACT.Silu).then_inc(sem("cmp_hidden"), 1)
            for t in range(NT):
                act.wait_ge(sem("cmp_shifted"), t + 1)
                nc.scalar.activation(SC[:, :, :], SC[:, :, :], ACT.Exp, scale=0.125).then_inc(sem("cmp_exp"), 1)
            act.wait_ge(sem("cmp_taken"), 2 * NT)
            with act.Fori(0, 4) as i:
                for b in range(2):
                    at0 = UNITS["odd"] + 16 * (2 * i + b)
                    act.wait_ge(sc_ready, CREDIT + at0 - 16)
                    act.sem_inc(sem("q_stage_free"), 1)
                    nc.scalar.activation(O_QS[:, b], O_Q[:, bass.ds(2 * i, 2), :], ACT.Copy,
                                         scale=0.125).then_inc(sem("q_staged"), 1)
                    exps(at0, 16, causal_ext, O_P)
            features("odd_y", None)
            split_ahead("odd_out")
            wait_group(act, "odd_out")
            squares("fin", X, H)
            act.wait_ge(sem("fin_x"), NT)
            squares("sec", X, H)
            features("sec", G_SEC)
            split_ahead("hg_f")
            split_ahead("hg_n")
            small_split(2, 72)
            split_ahead("sa_i")
            split_ahead("sa_n")
            act.wait_ge(sem("hg_abs"), 1)
            nc.scalar.activation(G_E[:, 0], G_E[:, 0], ACT.Exp, scale=-1.0)
            nc.scalar.drain()
            nc.scalar.activation(G_E[:, 0], G_E[:, 0], ACT.Ln, bias=1.0).then_inc(sem("hg_ln"), 1)
            act.wait_ge(sem("hg_logf"), 1)
            nc.scalar.activation(G_F[:, 4:8, :], G_F[:, 4:8, :], ACT.Sigmoid, scale=-1.0)
            nc.scalar.activation(G_F[:, 0:4, :], G_F[:, 0:4, :], ACT.Silu)
            nc.scalar.activation(G_N[:, :, 512:D], G_N[:, :, 512:D], ACT.Silu).then_inc(sem("hg_qk"), 1)
            act.wait_ge(sem("hg_cumsum"), 1)
            nc.scalar.activation(G_X[:, :, :], G_B[:, :, P - 1::P], ACT.Exp).then_inc(sem("hg_lasts"), 1)
            for l in range(len(HALVES) + 2):
                if l < len(HALVES) + 1:
                    act.wait_ge(sem("hg_diff"), l + 1)
                else:
                    act.wait_ge(sem("hg_buffer_free"), 1)
                src = G_E[:, l % 2] if l < len(HALVES) + 1 else G_B[:, :, :]
                nc.scalar.activation(G_E[:, l % 2], src, ACT.Exp).then_inc(sem("hg_exp"), 1)
            for h in range(4):
                act.wait_ge(sem("hg_out"), h + 1)
                nc.scalar.activation(H[:, :, P * h:P * h + P], PS[:, 4 + h, :].rearrange("p (t d) -> p t d", t=4),
                                     ACT.Copy)
            nc.scalar.drain()
            nc.scalar.activation(G_E[:, 0], H[:, :, 0:512], ACT.Square).then_inc(sem("hg_squared"), 1)
            act.wait_ge(sem("hg_gated"), 1)
            nc.scalar.activation(S_2[:, :, 0:512], S_N[:, :, 0:512], ACT.Square)
            nc.scalar.activation(S_2[:, :, 512:768], S_N[:, :, 768:D], ACT.Square)
            nc.scalar.activation(S_2[:, 0:2, 768:D], MEMKV[:, :, 0:256], ACT.Square).then_inc(sem("sa_squared"), 1)
            for k in range(8):
                act.wait_ge(sem("sa_turned"), k + 1)
                which, pair = divmod(k, 2)
                dst = (S_QK[:, pair, :], S_QK[:, 2 + pair, :], M_Q[:, pair, :], M_K[:, pair, :])[which]
                nc.scalar.activation(dst, PS[:, 4 + k % 4, 0:2 * P if which == 3 else T], ACT.Identity,
                                     scale=GAIN[:, 8 + which, 0:1]).then_inc(sem("sa_features"), 1)
            for n in range(24):
                t, h = n // 8 + 1, n % 8
                act.wait_ge(sem("index_ready"), n + 1)
                if n >= 2:
                    act.wait_ge(sem("index_added"), n - 1)
                nc.scalar.activation(RL[:, n % 2, 0:P * t + P], PS[:, 4 + n % 2, 0:P * t + P],
                                     ACT.Relu).then_inc(sem("index_relu"), 1)
            for b in range(2):
                exps(UNITS["sa"] + 8 * b, 8, causal_ext, S_P)
            for b in range(2):
                exps(UNITS["mem"] + 8 * b, 8, lambda u: 2 * P, S_P)
            features("sec_y", G_HG)
            split_ahead("sec_out")
            wait_group(act, "sec_out")
            squares("ffn", X, H)
            features("ffn", G_FFN)
            with act.Fori(0, BLOCKS["ffn_in"]) as i:
                for r in range(R):
                    n = CH["ffn_in"] + R + R * i + r
                    act.wait_ge(raw_ready[r], 32 * ((CH["ffn_in"] + R) // R + i + 1))
                    act.wait_ge(chunk_done, n + 1)
                    nc.scalar.activation(WH[:, r], RAW[:, r], ACT.Copy).then_inc(high_ready, 1)
                for j in range(2):
                    act.wait_ge(out_done, ODONE["ffn_in"] + 3 * i + 2 * j + 1)
                    act.wait_ge(sem("hidden_low"), 2 * i)
                    nc.scalar.activation(FT[:, j, :], PS[:, j, :], ACT.Silu).then_inc(sem("ffn_silu"), 1)
                for j in range(2):
                    act.wait_ge(sem("ffn_mul"), 2 + 2 * i + j + 1)
                    nc.scalar.activation(FH[:, bass.ds(2 * i + j, 1), :].rearrange("p a t -> p (a t)"),
                                         FT[:, j, :], ACT.Copy).then_inc(sem("hidden_high"), 1)
            split(CH["ffn_out"] + R, 4)
            for r in range(2):
                n = CH["ffn_out"] + 5 * R + r
                act.wait_ge(raw_ready[r], 32 * (n // R + 1))
                act.wait_ge(chunk_done, n + 1)
                nc.scalar.activation(WH[:, r], RAW[:, r], ACT.Copy).then_inc(high_ready, 1)

        @block.vector
        def _(dve):
            v = nc.vector
            dve.sem_inc(bank_free, 4)
            dve.sem_inc(sem("ffn_mul"), 2)
            for one in (mx_ready, pt_ready, o_done, sem("ret_weighted")):
                dve.sem_inc(one, CREDIT)

            def norm(use, src, nt=NT):
                dve.wait_ge(squares_ready, SQUARES[use] + nt)
                v.tensor_scalar(SS[:, 0:nt], SS[:, 0:nt], 1.0 / D, RMS_EPS, ALU.mult, ALU.add).then_inc(mean_ready, 1)
                dve.wait_ge(rstd_ready, RSTDS.index(use) + 1)
                for t in range(nt):
                    v.tensor_scalar(H[:, t, :], src[:, t, :], RS[:, t:t + 1], None, ALU.mult).then_inc(normed_ready, 1)

            def features(use, gain, nt=NT):
                for k in range(NK):
                    dve.wait_ge(act_high, AT[use] + k + 1)
                    g = 0 if gain == G_HG and k < 4 else k
                    scale = 1.0 if gain is None else GAIN[:, gain, g:g + 1]
                    v.scalar_tensor_tensor(AL[:, k, 0:P * nt], PS[:, 4 + k % 4, 0:P * nt], scale,
                                           AH[:, k, 0:P * nt].bitcast(f32), ALU.mult, ALU.subtract).then_inc(act_low, 1)

            def take(name, dst, loop=True):
                def body(i):
                    for j in range(4):
                        wait_out(dve, name, i, j, j == 3)
                        v.tensor_copy(dst(i, j), PS[:, j, :]).then_inc(bank_free, 1)
                if BLOCKS[name] == 1 or not loop:
                    for i in range(BLOCKS[name]):
                        body(i)
                else:
                    with dve.Fori(0, BLOCKS[name]) as i:
                        body(i)

            def residual(name):
                for i in range(2):
                    for j in range(4):
                        wait_out(dve, name, i, j, j == 3)
                        v.tensor_tensor(X[:, j, 512 * i:512 * i + 512], PS[:, j, :],
                                        X[:, j, 512 * i:512 * i + 512], ALU.add).then_inc(bank_free, 1)

            def units(at0, nu, ext, pt, take_output):
                for u in range(nu + 2):
                    if u < nu:
                        dve.wait_ge(sc_ready, CREDIT + at0 + u + 1)
                        v.tensor_reduce(NMAX[:, u % 4:u % 4 + 1], PS[:, S_BANK[u % 4], 0:ext(u)], AX.X, ALU.max,
                                        negate=True).then_inc(mx_ready, 1)
                    if 1 <= u <= nu:
                        k = u - 1
                        dve.wait_ge(t_ready, CREDIT + at0 + k + 1)
                        dve.wait_ge(o_ready, CREDIT + at0 + k - 1)
                        v.tensor_copy(pt[:, k % 2, 0:ext(k)], PS[:, T_BANK[k % 2], 0:ext(k)]).then_inc(pt_ready, 1)
                    if u >= 2:
                        k = u - 2
                        v.reciprocal(RSUM[:, k % 4:k % 4 + 1], SUM[:, k % 4:k % 4 + 1])
                        v.drain()
                        take_output(k, at0 + k)

            def causal_ext(u):
                return P * (u % 4 + 1)

            dve.wait_ge(sem("const"), 16 * N_CONST)
            for k in (8, 10):
                v.tensor_scalar(GAIN[:, k, 0:1], GAIN[:, k, 0:1], 0.125, None, ALU.mult)
            norm("mem", H, 2)
            features("mem", G_MEM, 2)
            norm("even", X)
            for j in range(2):
                wait_out(dve, "mem", 0, j, j == 1)
                v.tensor_copy(MEMKV[:, j, :], PS[:, j, :]).then_inc(bank_free, (1, 3)[j])
            features("even", G_EVEN)
            take("even_qk", lambda i, j: E_UT[:, bass.ds(4 * i + j, 1), :].rearrange("p a t -> p (a t)"))
            take("even_v", lambda i, j: E_V[:, j, bass.ds(512 * i, 512)])
            dve.wait_ge(sem("small_done"), 1)
            dve.wait_ge(sem("forget_bias"), 16)
            v.tensor_tensor(FL[:, :, :], PS[:, 4, 0:4 * 8].rearrange("p (t h) -> p t h", t=4),
                            BF[:, :].unsqueeze(1).to_broadcast((P, NT, 8)), ALU.add)
            v.drain()
            v.scalar_tensor_tensor(FL2[:, :, :], FL[:, :, :], -1.0, FL[:, :, :], ALU.mult, ALU.max).then_inc(sem("forget_abs"), 1)
            dve.wait_ge(sem("forget_ln"), 1)
            v.scalar_tensor_tensor(FL[:, :, :], FL[:, :, :], 0.0, FL2[:, :, :], ALU.min, ALU.subtract).then_inc(
                sem("forget_log"), 1)
            dve.wait_ge(sem("forget_turned"), 1)
            dve.wait_ge(chunk_done, R + CH["even_out"])
            v.memset(FO[:, :], 1.0)
            v.drain()
            v.tensor_tensor_scan(FC[:, :], FO[:, :], PS[0:8, 4, :], 0.0, ALU.mult, ALU.add)
            v.drain()
            v.tensor_copy(FB[:, 0, :], FC[:, :])
            v.drain()
            v.tensor_tensor(FO[:, :], FC[:, :], FB[:, 0, :], ALU.subtract)
            v.drain()
            v.tensor_copy(FB[:, 1, :], FO[:, :])
            v.drain()
            v.tensor_tensor(FC[:, :], FO[:, :], FB[:, 1, :], ALU.subtract)
            v.drain()
            v.tensor_copy(FB[:, 2, :], FC[:, :]).then_inc(sem("forget_parts"), 1)

            with dve.Fori(0, 2) as i:
                for b in range(2):
                    def fox_out(k, at, i=i, b=b):
                        dve.wait_ge(o_ready, CREDIT + at + 1)
                        v.tensor_scalar(H[:, k % 4, bass.ds(256 * i + HD * (2 * b + k // 4), HD)],
                                        PS[:, O_BANK[k % 2], 0:HD], RSUM[:, k % 4:k % 4 + 1], None,
                                        ALU.mult).then_inc(o_done, 1)
                    units(UNITS["fox"] + 8 * (2 * i + b), 8, causal_ext, E_PT, fox_out)
            with dve.Fori(0, 2) as i:
                for b in range(2):
                    dve.wait_ge(sem(f"ret_decay{b}"), 16 * (i + 1))
                    for u in range(8):
                        at = 8 * (2 * i + b) + u
                        n = T - P * (u % 4)
                        dve.wait_ge(sem("ret_scores"), at + 1)
                        dve.wait_ge(sem("ret_used"), CREDIT + at - 1)
                        v.tensor_tensor(E_P[:, u % 2, 0:n], PS[:, S_BANK[u % 4], 0:n], RD[:, b, u // 4, 0:n],
                                        ALU.mult).then_inc(sem("ret_weighted"), 1)
            HR = H[:, :, 512:D].rearrange("p t (h d) -> p t h d", h=8)
            MEAN = SS[:, 0:32].rearrange("p (t h) -> p t h", t=4)
            dve.wait_ge(sem("ret_taken"), CREDIT + 8)
            v.tensor_reduce(MEAN, HR, AX.X, ALU.add)
            v.drain()
            v.tensor_scalar(SS[:, 0:32], SS[:, 0:32], 1.0 / HD, None, ALU.mult)
            v.drain()
            v.tensor_tensor(HR, HR, MEAN.unsqueeze(3).to_broadcast((P, NT, 8, HD)), ALU.subtract).then_inc(
                sem("gn_centered"), 1)
            dve.wait_ge(sem("gn_squared"), 1)
            v.tensor_reduce(MEAN, E_UT[:, 8:12, :].rearrange("p t (h d) -> p t h d", h=8), AX.X, ALU.add)
            v.drain()
            v.tensor_scalar(SS[:, 0:32], SS[:, 0:32], 1.0 / HD, GN_EPS, ALU.mult, ALU.add).then_inc(mean_ready, 1)
            dve.wait_ge(rstd_ready, RSTDS.index("gn") + 1)
            v.tensor_tensor(HR, HR, RS[:, 0:32].rearrange("p (t h) -> p t h", t=4).unsqueeze(3).to_broadcast(
                (P, NT, 8, HD)), ALU.mult)
            v.drain()
            for t in range(NT):
                v.tensor_tensor(H[:, t, :], H[:, t, :], E_Z[:, t, :], ALU.mult).then_inc(normed_ready, 1)
            features("even_y", G_GN)
            residual("even_out")
            norm("odd", X)
            features("odd", G_ODD)

            take("odd_q", lambda i, j: O_Q[:, bass.ds(4 * i + j, 1), :].rearrange("p a t -> p (a t)"))
            for j in range(4):
                wait_out(dve, "odd_kv", 0, j, j == 3)
                v.tensor_copy(KCVC[:, j, :], PS[:, j, :]).then_inc(bank_free, 1)
            for j in range(4):
                wait_out(dve, "odd_kv", 1, j, j == 3)
                for gg in range(2):
                    for half in range(2):
                        last = v.tensor_copy(O_K[HD * half:HD * half + HD, j // 2, 2 * (j % 2) + gg, :],
                                             PS[HD * gg:HD * gg + HD, j, :])
                last.then_inc(bank_free, 1)
            take("odd_v", lambda i, j: O_V[:, j, :])
            dve.wait_ge(sem("odd_tables"), 16 * 11)
            dve.wait_ge(sem("small_done"), 2)
            v.tensor_tensor(GATE[:, :, :], PS[:, 4, 0:4 * 48].rearrange("p (t h) -> p t h", t=4),
                            BG[:, :].unsqueeze(1).to_broadcast((P, NT, 48)), ALU.add).then_inc(sem("gate_sum"), 1)
            dve.wait_ge(chunk_done, R + CH["cmp"])
            for i in range(2):
                if i:
                    dve.wait_ge(chunk_done, R + CH["cmp"] + R)
                for l in range(2):
                    for g in range(4):
                        src = KCVC[HD * (g % 2):HD * (g % 2) + HD, 2 * i + g // 2, :]
                        lo = src[:, l:l + 480].rearrange("p (c a r) -> p a c r", c=30, r=2)[:, :, :, 0]
                        v.tensor_copy(CI[HD * l:HD * l + HD, 0:8, g, 0:30], lo)
                        hi = src[:, 16 + l:16 + l + 480].rearrange("p (c a r) -> p a c r", c=30, r=2)[:, :, :, 0] \
                            if l == 0 else src[:, 17:497].rearrange("p (c a r) -> p a c r", c=30, r=2)[:, :, :, 0]
                        v.tensor_copy(CI[HD * l:HD * l + HD, 8:16, g, 0:30], hi)
                        v.tensor_copy(CI[HD * l:HD * l + HD, :, g, 30], src[:, 480 + l:512:2])
                v.drain()
                v.tensor_tensor(CI[:, :, :, :], CI[:, :, :, :],
                                PE2[:, i, :].unsqueeze(2).unsqueeze(3).to_broadcast((P, 16, 4, CMP)),
                                ALU.add).then_inc(sem("cmp_in"), 1)
                dve.wait_ge(sem("cmp_high"), i + 1)
                v.tensor_tensor(CIL[:, :, :], CI[:, :, :, :].rearrange("p l g c -> p l (g c)"),
                                CIH[:, :, :].bitcast(f32), ALU.subtract).then_inc(sem("cmp_low"), 1)
            v.memset(BDV[:, :, :, :], 0.0)
            dve.wait_ge(sem("cmp_kv"), 1)
            v.tensor_copy(KCMP[:, :, :], PS[:, 0, 0:P].rearrange("p (g c) -> p g c", g=4))
            v.drain()
            for j in range(4):
                last = v.tensor_copy(BDV[32 * j:32 * j + 32, :, j, :],
                                     PS[0:32, 1, 0:256].rearrange("p (g d) -> p g d", g=4))
            last.then_inc(sem("cmp_kv_taken"), 1)
            dve.wait_ge(sem("gates"), 1)
            for t in range(NT):
                dve.wait_ge(sem("cmp_scores"), t + 1)
                dve.wait_ge(sem("cmp_bias"), 16 * (t + 1))
                for odd in range(2):
                    last = v.tensor_tensor(SC[:, odd:16:2, :],
                                           PS[:, t % 2 + 4 * odd, 0:256].rearrange("p (h c) -> p h c", h=8),
                                           CB[:, odd:16:2, :], ALU.add)
                last.then_inc(sem("cmp_biased"), 1)
                v.drain()
                v.tensor_reduce(CMX[:, 0, :], SC[:, :, :], AX.X, ALU.max)
                v.drain()
                v.tensor_scalar(CMX[:, 0, :], CMX[:, 0, :], NEG / 10, None, ALU.max)
                v.drain()
                v.tensor_tensor(SC[:, :, :], SC[:, :, :], CMX[:, 0, :].unsqueeze(2).to_broadcast((P, 16, 32)),
                                ALU.subtract).then_inc(sem("cmp_shifted"), 1)
                dve.wait_ge(sem("cmp_exp"), t + 1)
                v.tensor_reduce(CMX[:, 1, :], SC[:, :, :], AX.X, ALU.add)
                v.drain()
                v.tensor_scalar(CMX[:, 1, :], CMX[:, 1, :], 1e-30, None, ALU.max)
                v.drain()
                v.reciprocal(CMX[:, 2, :], CMX[:, 1, :])
                v.drain()
                v.tensor_tensor(CMX[:, 3, :], CMX[:, 2, :], GATE[:, t, 0:48:3], ALU.mult)
                dve.wait_ge(sem("cmp_turned"), t + 1)
                v.tensor_copy(CPT[:, :, :], PS[:, 6, :].rearrange("p (g q) -> p g q", g=4)).then_inc(
                    sem("cmp_pt"), 1)
                dve.wait_ge(sem("cmp_values"), t + 1)
                for k in range(2):
                    v.tensor_tensor(H[:, t, 512 * k:512 * k + 512].rearrange("p (h d) -> p h d", h=8),
                                    PS[:, 2 + k, :].rearrange("p (h d) -> p h d", h=8),
                                    CMX[:, 3, 8 * k:8 * k + 8].unsqueeze(2).to_broadcast((P, 8, HD)),
                                    ALU.mult).then_inc(sem("cmp_taken"), 1)
            with dve.Fori(0, 4) as i:
                for b in range(2):
                    def odd_out(k, at, i=i, b=b):
                        a, q = k // 4, k % 4
                        v.tensor_tensor(SCL[:, q:q + 1], RSUM[:, q:q + 1],
                                        GATE[:, q, bass.ds(12 * i + 3 * a + 1 + b, 1)], ALU.mult)
                        v.drain()
                        dve.wait_ge(o_ready, CREDIT + at + 1)
                        cols = bass.ds(256 * i + HD * a, HD)
                        v.scalar_tensor_tensor(H[:, q, cols], PS[:, O_BANK[k % 2], 0:HD], SCL[:, q:q + 1],
                                               H[:, q, cols], ALU.mult, ALU.add).then_inc(o_done, 1)
                    units(UNITS["odd"] + 16 * (2 * i + b), 16, causal_ext, O_PT, odd_out)
            v.drain()
            for t in range(NT):
                v.tensor_tensor(H[:, t, :], H[:, t, :], O_Z[:, t, :], ALU.mult).then_inc(normed_ready, 1)
            features("odd_y", None)
            residual("odd_out")
            dve.wait_ge(squares_ready, SQUARES["fin"] + NT)
            v.tensor_scalar(SS[:, 0:NT], SS[:, 0:NT], 1.0 / D, RMS_EPS, ALU.mult, ALU.add).then_inc(mean_ready, 1)
            dve.wait_ge(rstd_ready, RSTDS.index("fin") + 1)
            dve.wait_ge(sem("final_gain"), 16)
            for t in range(NT):
                v.scalar_tensor_tensor(X[:, t, :], X[:, t, :], RS[:, t:t + 1], FING[:, :], ALU.mult,
                                       ALU.mult).then_inc(sem("fin_x"), 1)

            norm("sec", X)
            features("sec", G_SEC)
            take("hg_f", lambda i, j: G_F[:, bass.ds(4 * i + j, 1), :].rearrange("p a t -> p (a t)"))
            take("hg_n", lambda i, j: G_N[:, j, bass.ds(512 * i, 512)])
            take("sa_i", lambda i, j: I_Q[:, j, :])
            take("sa_n", lambda i, j: S_N[:, j, bass.ds(512 * i, 512)])
            dve.wait_ge(sem("small_done"), 3)
            small = PS[:, 4, 0:4 * 72].rearrange("p (t n) -> p t n", t=4)
            v.tensor_copy(I_KN[:, :, 0:HD], small[:, :, 0:HD])
            v.tensor_copy(I_KN[:, :, HD:P], small[:, :, 0:HD])
            v.tensor_scalar(I_W[:, :, :], small[:, :, HD:72], 8 ** -0.5 * 64 ** -0.5, None, ALU.mult).then_inc(
                sem("index_kw"), 1)
            dve.wait_ge(sem("index_k_turned"), 1)
            v.tensor_copy(I_K[:, :], PS[:, 5, :]).then_inc(sem("index_k"), 1)
            v.scalar_tensor_tensor(G_E[:, 0], G_F[:, 4:8, :], -1.0, G_F[:, 4:8, :], ALU.mult, ALU.max).then_inc(sem("hg_abs"), 1)
            v.memset(G_A[:, :, :, :], 0.0)
            dve.wait_ge(sem("hg_ln"), 1)
            v.scalar_tensor_tensor(G_E[:, 1], G_F[:, 4:8, :], 0.0, G_E[:, 0], ALU.min, ALU.subtract).then_inc(
                sem("hg_logf"), 1)
            v.drain()
            dve.wait_ge(sem("scan_reset"), 16)
            for h in range(4):
                last = v.tensor_tensor_scan(G_B[:, h, :], G_R[:, :], G_E[:, 1, h, :], 0.0, ALU.mult, ALU.add)
            last.then_inc(sem("hg_cumsum"), 1)
            dve.wait_ge(sem("hg_qk"), 1)
            dve.wait_ge(sem("sec_tables"), 16)
            v.drain()

            def halves(ap, s):
                a = ap.rearrange("p h (n s) -> p (h n) s", s=2 * s)
                return a[:, :, 0:s], a[:, :, s:2 * s]

            def differences(l):
                s = HALVES[l]
                n = 4 * T // (2 * s)
                if l >= 2:
                    dve.wait_ge(sem("hg_products"), 4 * (l - 2) + 4)
                lo, up = halves(G_E[:, l % 2], s)
                blo, bup = halves(G_B[:, :, :], s)
                mid = blo[:, :, s - 1:s].to_broadcast((P, n, s))
                v.tensor_tensor(up, bup, mid, ALU.subtract)
                v.tensor_tensor(lo, mid, blo, ALU.subtract).then_inc(sem("hg_diff"), 1)

            def mixed(l):
                s = HALVES[l]
                dve.wait_ge(sem("hg_exp"), l + 1)
                lo, up = halves(G_E[:, l % 2], s)
                v.tensor_tensor(up, up, halves(G_F[:, 0:4, :], s)[1], ALU.mult)
                v.tensor_tensor(lo, lo, halves(G_F[:, 4:8, :], s)[0], ALU.mult).then_inc(sem("hg_mixed"), 1)

            def products(l):
                for h in range(4):
                    dve.wait_ge(sem("hg_products"), 4 * l + h + 1)
                    v.copy_predicated(G_A[:, h], G_M[:, l, :].unsqueeze(1).to_broadcast((P, 4, P)),
                                      PS[:, 4 + h, :].rearrange("p (t q) -> p t q", t=4)).then_inc(
                                          sem("hg_weighted"), 1)

            NL = len(HALVES)
            differences(0)
            for l in range(NL):
                if l + 1 < NL:
                    differences(l + 1)
                mixed(l)
                if l >= 1:
                    products(l - 1)
            dve.wait_ge(sem("hg_products"), 4 * (NL - 2) + 4)
            last_b = G_B[:, :, :].rearrange("p h (t s) -> p (h t) s", s=P)
            v.tensor_tensor(G_E[:, NL % 2].rearrange("p h (t s) -> p (h t) s", s=P),
                            last_b[:, :, P - 1:P].to_broadcast((P, 16, P)), last_b, ALU.subtract).then_inc(
                                sem("hg_diff"), 1)
            products(NL - 1)
            dve.sem_inc(sem("hg_buffer_free"), 1)
            dve.wait_ge(sem("hg_exp"), NL + 1)
            v.tensor_tensor(G_E[:, NL % 2], G_E[:, NL % 2], G_F[:, 4:8, :], ALU.mult).then_inc(sem("hg_mixed"), 1)
            dve.wait_ge(sem("hg_exp"), NL + 2)
            v.tensor_tensor(G_E[:, (NL + 1) % 2], G_E[:, (NL + 1) % 2], G_F[:, 0:4, :], ALU.mult).then_inc(
                sem("hg_mixed"), 1)
            products(NL)
            for h in range(4):
                dve.wait_ge(sem("hg_k_turned"), h + 1)
                v.tensor_copy(G_KT[:, h], PS[:, h, 0:3 * P].rearrange("p (t d) -> p t d", t=3)).then_inc(
                    sem("hg_kt"), 1)
            dve.wait_ge(sem("hg_lasts"), 1)
            for h in range(4):
                dve.wait_ge(sem("hg_kv"), h + 1)
                v.tensor_copy(G_S[:, h, 0, :], PS[:, h, 0:P])
                for t in range(1, 3):
                    v.drain()
                    last = v.scalar_tensor_tensor(G_S[:, h, t, :], G_S[:, h, t - 1, :], G_X[:, h, t:t + 1],
                                                  PS[:, h, P * t:P * t + P], ALU.mult, ALU.add)
                last.then_inc(sem("hg_state"), 1)
            dve.wait_ge(sem("hg_squared"), 1)
            HG = H[:, :, 0:512].rearrange("p t (h d) -> p t h d", h=4)
            v.tensor_reduce(SS[:, 0:16].rearrange("p (t h) -> p t h", t=4),
                            G_E[:, 0].rearrange("p t (h d) -> p t h d", h=4), AX.X, ALU.add)
            v.drain()
            v.tensor_scalar(SS[:, 0:16], SS[:, 0:16], 1.0 / P, RMS_EPS, ALU.mult, ALU.add).then_inc(mean_ready, 1)
            dve.wait_ge(rstd_ready, RSTDS.index("hgo") + 1)
            v.tensor_tensor(HG, HG, RS[:, 0:16].rearrange("p (t h) -> p t h", t=4).unsqueeze(3).to_broadcast(
                (P, NT, 4, P)), ALU.mult)
            v.drain()
            v.tensor_tensor(H[:, :, 0:512], H[:, :, 0:512], G_N[:, :, 512:D], ALU.mult).then_inc(sem("hg_gated"), 1)
            dve.wait_ge(sem("sa_squared"), 1)
            v.tensor_reduce(SS[:, 0:32].rearrange("p (t h) -> p t h", t=4),
                            S_2[:, :, 0:512].rearrange("p t (h d) -> p t h d", d=HD), AX.X, ALU.add)
            v.tensor_reduce(SS[:, 32:48].rearrange("p (t h) -> p t h", t=4),
                            S_2[:, :, 512:768].rearrange("p t (h d) -> p t h d", d=HD), AX.X, ALU.add)
            v.tensor_reduce(SS[:, 48:56].rearrange("p (t h) -> p t h", t=2),
                            S_2[:, 0:2, 768:D].rearrange("p t (h d) -> p t h d", d=HD), AX.X, ALU.add)
            v.drain()
            v.tensor_scalar(SS[:, 0:56], SS[:, 0:56], 1.0 / HD, RMS_EPS, ALU.mult, ALU.add).then_inc(mean_ready, 1)
            dve.wait_ge(rstd_ready, RSTDS.index("sa") + 1)
            for ap, a, t, h in ((S_N[:, :, 0:512], 0, 4, 8), (S_N[:, :, 768:D], 32, 4, 4), (MEMKV[:, :, 0:256], 48, 2, 4)):
                four = ap.rearrange("p t (h d) -> p t h d", d=HD)
                v.tensor_tensor(four, four, RS[:, a:a + t * h].rearrange("p (t h) -> p t h", t=t).unsqueeze(
                    3).to_broadcast((P, t, h, HD)), ALU.mult).then_inc(sem("sa_normed"), 1)
            v.tensor_copy(SEL[:, 0, 0:P], CAUSAL[:, :])
            dve.wait_ge(sem("sa_tables"), 16)
            for t in range(1, NT):
                n = P * (t + 1)
                for h in range(8):
                    dve.wait_ge(sem("index_relu"), 8 * (t - 1) + h + 1)
                    one, rl = I_W[:, t, h:h + 1], RL[:, h % 2, 0:n]
                    if h == 0:
                        v.tensor_scalar(SCO[:, 0:n], rl, one, None, ALU.mult).then_inc(sem("index_added"), 1)
                    else:
                        v.scalar_tensor_tensor(SCO[:, 0:n], rl, one, SCO[:, 0:n], ALU.mult, ALU.add).then_inc(
                            sem("index_added"), 1)
                    v.drain()
                v.tensor_tensor(SCO[:, n - P:n], SCO[:, n - P:n], MASKF[:, :], ALU.add)
                v.drain()
                for k in range(16):
                    v.max(MX8[:, :], SCO[:, 0:n])
                    v.drain()
                    v.match_replace(SCO[:, 0:n], MX8[:, :], SCO[:, 0:n], TAKEN)
                    v.drain()
                v.tensor_scalar(SEL[:, t, 0:n], SCO[:, 0:n], TAKEN / 2, NEG, ALU.is_gt, ALU.mult).then_inc(
                    sem("selected"), 1)
                v.drain()
            for name, col in (("sa", 512), ("mem", 768)):
                for b in range(2):
                    def out_take(k, at, b=b, col=col):
                        dve.wait_ge(o_ready, CREDIT + at + 1)
                        a = col + HD * (2 * b + k // 4)
                        v.tensor_scalar(H[:, k % 4, a:a + HD], PS[:, O_BANK[k % 2], 0:HD], RSUM[:, k % 4:k % 4 + 1],
                                        None, ALU.mult).then_inc(o_done, 1)
                    units(UNITS[name] + 8 * b, 8, causal_ext if name == "sa" else (lambda u: 2 * P), S_PT, out_take)
            features("sec_y", G_HG)
            residual("sec_out")
            norm("ffn", X)
            features("ffn", G_FFN)
            with dve.Fori(0, BLOCKS["ffn_in"]) as i:
                for j in range(2):
                    dve.wait_ge(sem("ffn_silu"), 2 * i + j + 1)
                    if j:
                        dve.wait_ge(chunk_done, R + CH["ffn_in"] + R * i + R)
                    else:
                        dve.wait_ge(out_done, ODONE["ffn_in"] + 3 * i + 2)
                    v.tensor_tensor(FT[:, j, :], PS[:, 2 + j, :], FT[:, j, :], ALU.mult).then_inc(sem("ffn_mul"), 1)
                for j in range(2):
                    dve.wait_ge(sem("hidden_high"), 2 * i + j + 1)
                    v.tensor_tensor(FLO[:, bass.ds(2 * i + j, 1), :].rearrange("p a t -> p (a t)"), FT[:, j, :],
                                    FH[:, bass.ds(2 * i + j, 1), :].rearrange("p a t -> p (a t)").bitcast(f32),
                                    ALU.subtract).then_inc(sem("hidden_low"), 1)
            dve.sem_inc(bank_free, 4 * BLOCKS["ffn_in"])
            for i in range(2):
                for j in range(4):
                    if j == NT - 1:
                        dve.wait_ge(chunk_done, R + CH["ffn_out"] + OUT_CHUNKS * (i + 1))
                    else:
                        dve.wait_ge(sem("ffn_out_done"), 3 * i + j + 1)
                    v.tensor_tensor(X[:, j, 512 * i:512 * i + 512], PS[:, 4 * i + j, :],
                                    X[:, j, 512 * i:512 * i + 512], ALU.add).then_inc(bank_free, 1)

        @block.tensor
        def _(pe):
            mm = nc.tensor.matmul
            pe.sem_inc(chunk_done, R)
            for one in (sc_ready, t_ready, o_ready, sem("ret_used")):
                pe.sem_inc(one, CREDIT)

            def features(use, nt=NT, normed=True):
                if normed:
                    pe.wait_ge(normed_ready, NORMED[use] + nt)
                for k in range(NK):
                    if k >= 4:
                        pe.wait_ge(act_low, AT[use] + k - 3)
                    for t in range(nt):
                        last = nc.tensor.transpose(PS[:, 4 + k % 4, P * t:P * t + P], H[:, t, P * k:P * k + P],
                                                   ID[:, :])
                    last.then_inc(turned, 1)
                pe.wait_ge(act_low, AT[use] + NK)

            def three(bank, hi_l, lo_l, hi_r, lo_r, start, stop):
                mm(bank, hi_l, hi_r, start=start, stop=False, skip_group_check=True)
                mm(bank, hi_l, lo_r, start=False, stop=False, skip_group_check=True)
                return mm(bank, lo_l, hi_r, start=False, stop=stop, skip_group_check=True)

            def block_products(n0, o0, tokens, outs=4, order=(0, 1, 2, 3), free=None):
                for r in range(R):
                    pe.wait_ge(split_ready, n0 + r + 1)
                    for at, j in enumerate(order[:outs]):
                        if r == 0:
                            if free:
                                free(at)
                            else:
                                pe.wait_ge(bank_free, o0 + at + 1)
                        for k in range(2):
                            kt = 2 * r + k
                            s = slice(P * j, P * j + P)
                            if tokens:
                                args = (AH[:, kt, s], AL[:, kt, s], WH[:, r, k, :], WL[:, r, k, :])
                            else:
                                args = (WH[:, r, k, s], WL[:, r, k, s], AH[:, kt, :], AL[:, kt, :])
                            last = three(PS[:, j, :], *args, start=kt == 0, stop=kt == NK - 1)
                        if r == R - 1 and at < outs - 1:
                            last.then_inc(out_done, 1)
                    last.then_inc(chunk_done, 1)

            def project(name, tokens):
                if BLOCKS[name] == 1:
                    block_products(CH[name], OUT[name], tokens)
                else:
                    with pe.Fori(0, BLOCKS[name]) as i:
                        block_products(CH[name] + R * i, OUT[name] + 4 * i, tokens)

            def small(k, m):
                pe.wait_ge(sem("small_low"), k + 1)
                for t in range(NT):
                    for kt in range(NK):
                        s = slice(P * t, P * t + P)
                        last = three(PS[:, 4, m * t:m * t + m], AH[:, kt, s], AL[:, kt, s], SMH[:, kt, 0:m],
                                     SML[:, kt, 0:m], start=kt == 0, stop=kt == NK - 1)
                last.then_inc(sem("small_done"), 1)

            def units(at0, nu, ext, probs, pt, scores, values):
                for u in range(nu + 2):
                    if u < nu:
                        pe.wait_ge(p_ready, CREDIT + at0 + u - 3)
                        scores(u, PS[:, S_BANK[u % 4], 0:ext(u)]).then_inc(sc_ready, 1)
                    if 1 <= u <= nu:
                        k = u - 1
                        pe.wait_ge(p_ready, CREDIT + at0 + k + 1)
                        pe.wait_ge(pt_ready, CREDIT + at0 + k - 1)
                        for t in range(ext(k) // P):
                            last = nc.tensor.transpose(PS[:, T_BANK[k % 2], P * t:P * t + P],
                                                       probs[:, k % 2, P * t:P * t + P], ID[:, :])
                        last.then_inc(t_ready, 1)
                    if u >= 2:
                        k = u - 2
                        pe.wait_ge(pt_ready, CREDIT + at0 + k + 1)
                        pe.wait_ge(o_done, CREDIT + at0 + k - 1)
                        nt = ext(k) // P
                        for t in range(nt):
                            last = mm(PS[:, O_BANK[k % 2], 0:HD], pt[:, k % 2, P * t:P * t + P], values(k, t),
                                      start=t == 0, stop=t == nt - 1)
                        last.then_inc(o_ready, 1)

            def causal_ext(u):
                return P * (u % 4 + 1)

            def attention_done(name):
                pe.wait_ge(p_ready, CREDIT + UNITS[name])
                pe.wait_ge(o_done, CREDIT + UNITS[name])

            pe.wait_ge(sem("const"), 16 * N_CONST)
            features("mem", 2)
            block_products(CH["mem"], OUT["mem"], True, 2)
            features("even")
            project("even_qk", False)
            project("even_v", True)
            small(0, 8)
            project("even_z", True)
            pe.wait_ge(sem("forget_log"), 1)
            for t in range(NT):
                last = nc.tensor.transpose(PS[0:8, 4, P * t:P * t + P], FL[:, t, :], ID[:, :])
            last.then_inc(sem("forget_turned"), 1)
            wait_group(pe, "even_z")
            pe.wait_ge(sem("decay_rows"), 48)
            with pe.Fori(0, 2) as i:
                for b in range(2):
                    pe.wait_ge(sem("q_staged"), 2 * i + b + 1)
                    pe.wait_ge(sem("k_staged"), 2 * i + b + 1)

                    def fox_scores(u, bank, i=i, b=b):
                        half, q, n = HD * (u // 4), u % 4, P * (u % 4 + 1)
                        mm(bank, E_Q[half:half + HD, b, P * q:P * q + P], E_K[half:half + HD, b, 0:n],
                           start=True, stop=False, skip_group_check=True)
                        mm(bank, MINUS3[:, :], C3[:, bass.ds(4 * i + 2 * b + u // 4, 1), 0:n].rearrange(
                            "p a t -> p (a t)"), start=False, stop=False, skip_group_check=True)
                        return mm(bank[:, n - P:n], IDB[:, :], CAUSAL[:, :], start=False, stop=True,
                                  skip_group_check=True)

                    units(UNITS["fox"] + 8 * (2 * i + b), 8, causal_ext, E_P, E_PT, fox_scores,
                          lambda k, t, i=i, b=b: E_V[:, t, bass.ds(256 * i + HD * (2 * b + k // 4), HD)])
            attention_done("odd")
            with pe.Fori(0, 2) as i:
                for b in range(2):
                    pe.wait_ge(sem("ret_q_staged"), 2 * i + b + 1)
                    pe.wait_ge(sem("ret_k_staged"), 2 * i + b + 1)
                    for u in range(9):
                        at = 8 * (2 * i + b) + u
                        if u < 8:
                            half, k = HD * (u // 4), u % 4
                            pe.wait_ge(sem("ret_weighted"), CREDIT + at - 3)
                            mm(PS[:, S_BANK[u % 4], 0:T - P * k], E_K[half:half + HD, b, P * k:P * k + P],
                               E_Q[half:half + HD, b, P * k:T], start=True, stop=True).then_inc(sem("ret_scores"), 1)
                        if u >= 1:
                            a, k = divmod(u - 1, 4)
                            pe.wait_ge(sem("ret_weighted"), CREDIT + at)
                            if k == 0:
                                pe.wait_ge(sem("ret_taken"), CREDIT + 4 * i + 2 * b + a - 1)
                            for q in range(k, NT):
                                last = mm(PS[:, O_BANK[a], HD * q:HD * q + HD],
                                          E_P[:, (u - 1) % 2, P * (q - k):P * (q - k) + P],
                                          E_V[:, k, bass.ds(512 + 256 * i + HD * (2 * b + a), HD)],
                                          start=k == 0 and q == 0, stop=k == q, skip_group_check=True)
                            last.then_inc(sem("ret_used"), 1)
            pe.wait_ge(sem("ret_taken"), CREDIT + 8)
            features("even_y")
            project("even_out", True)
            features("odd")

            small(1, 48)
            project("odd_q", False)
            project("odd_kv", False)
            project("odd_v", True)
            project("odd_z", True)
            pe.wait_ge(sem("gate_sum"), 1)
            for i in range(2):
                pe.wait_ge(sem("cmp_low"), i + 1)
                for r in range(R):
                    n = CH["cmp"] + R * i + r
                    pe.wait_ge(split_ready, n + 1)
                    for q in range(4):
                        l = 4 * r + q
                        for h in range(2):
                            s = slice(256 * (q % 2) + P * h, 256 * (q % 2) + P * h + P)
                            last = three(PS[:, 4 + 2 * i + h, 0:4 * CMP], WH[:, r, q // 2, s], WL[:, r, q // 2, s],
                                         CIH[:, l, :], CIL[:, l, :], start=l == 0, stop=l == 15)
                    last.then_inc(chunk_done, 1)
            pe.wait_ge(sem("odd_tables"), 16 * 11)
            pe.wait_ge(sem("cmp_hidden"), 4)
            wait_group(pe, "odd_z")
            for h in range(2):
                mm(PS[:, 0, 0:P], W2D[:, h, :, :].rearrange("p a d -> p (a d)"),
                   CHID[:, 0, h, :, :].rearrange("p g c -> p (g c)"), start=h == 0, stop=h == 1)
            for g in range(4):
                for h in range(2):
                    last = mm(PS[0:32, 1, HD * g:HD * g + HD], CHID[:, 1, h, g, :], W2[:, 1, h, :],
                              start=h == 0, stop=h == 1)
            last.then_inc(sem("cmp_kv"), 1)
            pe.wait_ge(sem("cmp_kv_taken"), 1)

            def cmp_scores(t):
                if t >= 2:
                    pe.wait_ge(sem("cmp_biased"), t - 1)
                for h in range(16):
                    half = HD * (h % 2)
                    last = mm(PS[:, t % 2 + 4 * (h % 2), 16 * h - 16 * (h % 2):16 * h - 16 * (h % 2) + 32], O_Q[half:half + HD, h // 2, P * t:P * t + P],
                              KCMP[half:half + HD, h // 4, :], start=True, stop=True, skip_group_check=True)
                last.then_inc(sem("cmp_scores"), 1)

            cmp_scores(0)
            for t in range(NT):
                if t + 1 < NT:
                    cmp_scores(t + 1)
                pe.wait_ge(sem("cmp_exp"), t + 1)
                for g in range(4):
                    last = nc.tensor.transpose(PS[:, 6, P * g:P * g + P],
                                               SC[:, 4 * g:4 * g + 4, :].rearrange("p h c -> p (h c)"), ID[:, :])
                last.then_inc(sem("cmp_turned"), 1)
                pe.wait_ge(sem("cmp_pt"), t + 1)
                if t:
                    pe.wait_ge(sem("cmp_taken"), 2 * t)
                for g in range(4):
                    last = mm(PS[:, 2 + g // 2, 256 * (g % 2):256 * (g % 2) + 256], CPT[:, g, :],
                              BDV[:, g, :, :].rearrange("p j d -> p (j d)"), start=True, stop=True,
                              skip_group_check=True)
                last.then_inc(sem("cmp_values"), 1)
            pe.wait_ge(sem("cmp_taken"), 2 * NT)
            with pe.Fori(0, 4) as i:
                for b in range(2):
                    pe.wait_ge(sem("q_staged"), 4 + 2 * i + b + 1)
                    pe.wait_ge(sem("k_staged"), 4 + 2 * i + b + 1)

                    def odd_scores(u, bank, i=i, b=b):
                        a, q = divmod(u, 4)
                        half, n = HD * (a % 2), P * (q + 1)
                        mm(bank, O_QS[half:half + HD, b, a // 2, P * q:P * q + P], O_KS[half:half + HD, b, 0:n],
                           start=True, stop=False, skip_group_check=True)
                        mm(bank, ALS[:, bass.ds(4 * i + a, 1), :].rearrange("p a q -> p (a q)"),
                           ALJ[:, T - P - P * q:T - P - P * q + n], start=False, stop=False, skip_group_check=True)
                        return mm(bank[:, n - P:n], IDB[:, :], CAUSAL[:, :], start=False, stop=True,
                                  skip_group_check=True)

                    units(UNITS["odd"] + 16 * (2 * i + b), 16, causal_ext, O_P, O_PT, odd_scores,
                          lambda k, t, i=i, b=b: O_V[:, t, bass.ds(256 * b + HD * i, HD)])
            attention_done("sa")
            features("odd_y")
            project("odd_out", True)

            features("sec")
            project("hg_f", False)
            project("hg_n", True)
            project("sa_i", False)
            project("sa_n", True)
            small(2, 72)
            pe.wait_ge(sem("index_kw"), 1)
            for t in range(NT):
                last = nc.tensor.transpose(PS[:, 5, P * t:P * t + P], I_KN[:, t, :], ID[:, :])
            last.then_inc(sem("index_k_turned"), 1)
            pe.wait_ge(sem("index_k"), 1)
            wait_group(pe, "sa_n")
            NL = len(HALVES)
            for l in range(NL + 1):
                if l < NL:
                    pe.wait_ge(sem("hg_mixed"), l + 1)
                for h in range(4):
                    if l:
                        pe.wait_ge(sem("hg_weighted"), 4 * (l - 1) + h + 1)
                    for t in range(NT):
                        s = slice(P * t, P * t + P)
                        lhs, rhs = (G_E[:, l % 2, h, s],) * 2 if l < NL else (G_F[:, 4 + h, s], G_F[:, h, s])
                        last = mm(PS[:, 4 + h, s], lhs, rhs, start=True, stop=True, skip_group_check=True)
                    last.then_inc(sem("hg_products"), 1)
            pe.wait_ge(sem("hg_mixed"), NL + 1)
            for h in range(4):
                for t in range(3):
                    last = nc.tensor.transpose(PS[:, h, P * t:P * t + P], G_E[:, NL % 2, h, P * t:P * t + P],
                                               ID[:, :])
                last.then_inc(sem("hg_k_turned"), 1)
            for h in range(4):
                pe.wait_ge(sem("hg_kt"), h + 1)
                for t in range(3):
                    last = mm(PS[:, h, P * t:P * t + P], G_KT[:, h, t, :], G_N[:, t, P * h:P * h + P],
                              start=True, stop=True, skip_group_check=True)
                last.then_inc(sem("hg_kv"), 1)
            pe.wait_ge(sem("hg_weighted"), 4 * (NL + 1))
            pe.wait_ge(sem("hg_mixed"), NL + 2)
            for h in range(4):
                pe.wait_ge(sem("hg_state"), h + 1)
                for t in range(NT):
                    s = slice(P * t, P * t + P)
                    last = mm(PS[:, 4 + h, s], G_A[:, h, t, :], G_N[:, t, P * h:P * h + P],
                              start=True, stop=t == 0, skip_group_check=True)
                    if t:
                        last = mm(PS[:, 4 + h, s], G_E[:, (NL + 1) % 2, h, s], G_S[:, h, t - 1, :],
                                  start=False, stop=True, skip_group_check=True)
                last.then_inc(sem("hg_out"), 1)
            pe.wait_ge(sem("sa_normed"), 3)
            for k in range(8):
                which, pair = divmod(k, 2)
                if k >= 4:
                    pe.wait_ge(sem("sa_features"), k - 3)
                for t in range(2 if which == 3 else NT):
                    src = MEMKV[:, t, P * pair:P * pair + P] if which == 3 else \
                        S_N[:, t, (0, 256, 768)[which] + P * pair:(0, 256, 768)[which] + P * pair + P]
                    last = nc.tensor.transpose(PS[:, 4 + k % 4, P * t:P * t + P], src, ID[:, :])
                last.then_inc(sem("sa_turned"), 1)
            pe.wait_ge(sem("sa_features"), 8)
            for n in range(24):
                t, h = n // 8 + 1, n % 8
                half = HD * (h % 2)
                if n >= 2:
                    pe.wait_ge(sem("index_relu"), n - 1)
                mm(PS[:, 4 + n % 2, 0:P * t + P], I_Q[half:half + HD, h // 2, P * t:P * t + P],
                   I_K[half:half + HD, 0:P * t + P], start=True, stop=True).then_inc(sem("index_ready"), 1)
            pe.wait_ge(sem("index_relu"), 24)
            pe.wait_ge(sem("selected"), 3)
            for b in range(2):
                def sa_scores(u, bank, b=b):
                    half, q, n = HD * (u // 4), u % 4, P * (u % 4 + 1)
                    mm(bank, S_QK[half:half + HD, b, P * q:P * q + P], S_QK[half:half + HD, 2 + b, 0:n],
                       start=True, stop=False, skip_group_check=True)
                    return mm(bank, IDB[:, :], SEL[:, q, 0:n], start=False, stop=True, skip_group_check=True)

                units(UNITS["sa"] + 8 * b, 8, causal_ext, S_P, S_PT, sa_scores,
                      lambda k, t, b=b: S_N[:, t, 512 + HD * (2 * b + k // 4):512 + HD * (2 * b + k // 4) + HD])
            for b in range(2):
                def mem_scores(u, bank, b=b):
                    half, q = HD * (u // 4), u % 4
                    return mm(bank, M_Q[half:half + HD, b, P * q:P * q + P], M_K[half:half + HD, b, :],
                              start=True, stop=True)

                units(UNITS["mem"] + 8 * b, 8, lambda u: 2 * P, S_P, S_PT, mem_scores,
                      lambda k, t, b=b: MEMKV[:, t, 256 + HD * (2 * b + k // 4):256 + HD * (2 * b + k // 4) + HD])
            attention_done("end")
            pe.wait_ge(sem("hg_gated"), 1)
            features("sec_y", normed=False)
            project("sec_out", True)
            features("ffn")
            with pe.Fori(0, BLOCKS["ffn_in"]) as i:
                def free(at, i=i):
                    if at % 2 == 0:
                        pe.wait_ge(sem("ffn_mul"), 2 * i + at // 2 + 1)
                block_products(CH["ffn_in"] + R * i, 0, False, 4, FFN_ORDER, free)
            for i in range(2):
                if i == 0:
                    pe.wait_ge(sem("hidden_low"), NF)
                    wait_group(pe, "ffn_in")
                for r in range(OUT_CHUNKS):
                    n = CH["ffn_out"] + OUT_CHUNKS * i + r
                    pe.wait_ge(split_ready, n + 1)
                    for t in range(NT):
                        s = slice(P * t, P * t + P)
                        for k in range(2):
                            kt = 2 * r + k
                            last = three(PS[:, 4 * i + t, :], FH[:, kt, s], FLO[:, kt, s], WH[:, n % R, k, :],
                                         WL[:, n % R, k, :], start=kt == 0, stop=kt == NF - 1)
                        if t == NT - 1:
                            last.then_inc(chunk_done, 1)
                        elif r == OUT_CHUNKS - 1:
                            last.then_inc(sem("ffn_out_done"), 1)


def tables():
    bf = np.dtype("bfloat16")
    i = np.arange(P)
    c = {"identity": np.eye(P, dtype=np.float32)}
    c["identity_bf16"] = c["identity"].astype(bf)
    c["causal_f32"] = np.where(i[None, :] <= i[:, None], 0.0, NEG).astype(np.float32)
    c["causal_bf16"] = c["causal_f32"].astype(bf)
    c["minus_one3"] = np.full((3, P), -1.0, np.float32).astype(bf)
    lg = np.log(1.0 - 2.0 ** (-5.0 - np.arange(8)))
    diff = np.arange(T)[None, :] - i[:, None]
    dec = np.where(diff[None] >= 0, np.exp(lg[:, None, None] * np.maximum(diff, 0)[None]), 0.0)
    c["retention"] = np.ascontiguousarray(dec.transpose(1, 0, 2)).astype(np.float32)
    slopes = (2.0 ** (-8.0 * (np.arange(16) + 1) / 16)).astype(np.float32)
    parts, rest = [], slopes.copy()
    for _ in range(3):
        parts.append(rest.astype(bf))
        rest = rest - parts[-1].astype(np.float32)
    j = np.arange(T) - (T - P)
    places = [j // 16 * 16, j % 16]
    c["alibi_slopes"] = np.zeros((P, 16, P), bf)
    c["alibi_positions"] = np.zeros((P, T), bf)
    for a in range(3):
        for b in range(2):
            c["alibi_slopes"][2 * a + b] = np.broadcast_to(parts[a][:, None], (16, P))
            c["alibi_positions"][2 * a + b] = places[b].astype(np.float32).astype(bf)
    t = np.arange(T).reshape(NT, P).T
    end = np.arange(32) * 16 + 31
    gap = t[:, :, None] - end[None, None, :]
    bias = -8.0 * slopes[None, None, :, None] * gap[:, :, None, :].astype(np.float32)
    ok = (gap >= 0) & (np.arange(32) < CMP)
    c["cmp_bias"] = np.where(ok[:, :, None, :], bias, NEG).astype(np.float32)
    masks = []
    for s in HALVES:
        k, q = i[:, None], i[None, :]
        masks.append((k // (2 * s) == q // (2 * s)) & (k % (2 * s) < s) & (q % (2 * s) >= s))
    masks.append(np.eye(P, dtype=bool))
    c["tree_masks"] = np.ascontiguousarray(np.stack(masks, 1)).astype(np.uint32)
    c["scan_reset"] = np.broadcast_to((np.arange(T) % P != 0).astype(np.float32), (P, T)).copy()
    return c


INPUTS = ["x", "even_norm_g", "even_w_in", "even_b_f", "even_gn_g", "even_w_out", "odd_norm_g", "odd_w_in",
          "odd_b_gate", "odd_pe_k", "odd_pe_v", "odd_wk1", "odd_wk2", "odd_wv1", "odd_wv2", "odd_w_out", "final_g",
          "mem_2", "w_in_2", "w_out_2", "w_mem_kv_2", "lb_logits_2", "norm_mix_2", "norm_mem_2", "norm_ffn_2",
          "hg_out_gain_2", "sa_q_gain_2", "sa_k_gain_2", "mem_q_gain_2", "mem_k_gain_2", "w_ffn_in_2",
          "w_ffn_out_2"]


def kernel(**inputs):
    import concourse.bacc as bacc
    from concourse.bass_utils import run_bass_kernel_spmd

    nc = bacc.Bacc("TRN2", target_bir_lowering=False, num_devices=1)
    arrays, w, c = {}, {}, {}
    for name in INPUTS:
        a = np.ascontiguousarray(inputs[name])
        arrays[f"in_{name}"] = a
        w[name] = nc.dram_tensor(f"in_{name}", a.shape, mybir.dt.from_np(a.dtype), kind="ExternalInput").ap()
    for name, a in tables().items():
        arrays[f"table_{name}"] = a
        c[name] = nc.dram_tensor(f"table_{name}", a.shape, mybir.dt.from_np(a.dtype), kind="ExternalInput").ap()
    out = nc.dram_tensor("out", (1, T, D), f32, kind="ExternalOutput").ap()
    program(nc, w, c, out)
    r = run_bass_kernel_spmd(nc, [arrays], core_ids=[0])
    return r.results[0]["out"]
```

```python
from contextlib import ExitStack

import numpy as np
import concourse.bass as bass
from concourse import mybir

f32 = mybir.dt.float32
f32r = mybir.dt.float32r
bf16 = mybir.dt.bfloat16
u32 = mybir.dt.uint32
ALU = mybir.AluOpType
ACT = mybir.ActivationFunctionType
AX = mybir.AxisListType

P = 128
T = 512
NT = T // P
D = 1024
NK = D // P
HD = 64
R = 4
FF = 2816
NF = FF // P
NEG = -1e30
TAKEN = -3e38
RMS_EPS = 1e-6
GN_EPS = 1e-5
CMP = 31
CREDIT = 16
HALVES = [64, 32, 16, 8, 4, 2, 1]
S_BANK, T_BANK, O_BANK = (0, 1, 4, 5), (6, 7), (2, 3)
FFN_ORDER = (0, 2, 1, 3)

STREAM = [("mem", 1, 4), ("even_qk", 4, 4), ("even_v", 2, 4), ("even_z", 2, 4), ("even_out", 2, 4),
          ("odd_q", 2, 4), ("odd_kv", 2, 4), ("odd_v", 1, 4), ("odd_z", 2, 4), ("cmp", 2, 0), ("odd_out", 2, 4),
          ("sa_i", 1, 4), ("sa_n", 2, 4), ("hg_f", 2, 4), ("hg_n", 2, 4), ("sec_out", 2, 4), ("ffn_in", 11, 4)]
BLOCKS = {name: n for name, n, _ in STREAM}
CH, OUT, ODONE = {}, {}, {}
_c = _o = _d = 0
for _name, _blocks, _outs in STREAM:
    CH[_name], OUT[_name], ODONE[_name] = _c, _o, _d
    _c, _o, _d = _c + R * _blocks, _o + _outs * _blocks, _d + (1 if _name == "mem" else max(_outs - 1, 0)) * _blocks
CH["ffn_out"], OUT["ffn_out"], ODONE["ffn_out"] = _c, _o, _d
OUT_CHUNKS = NF // 2
UNITS = {"fox": 0, "odd": 32, "sa": 160, "mem": 176, "end": 192}

FEATURES = ("mem", "even", "even_y", "odd", "odd_y", "sec", "sec_y", "ffn")
SQUARES = {"mem": 0, "even": 2, "odd": 6, "fin": 10, "sec": 14, "ffn": 18}
NORMED = {"mem": 0, "even": 2, "even_y": 6, "odd": 10, "odd_y": 14, "sec": 18, "ffn": 22}
RSTDS = {"mem": 0, "even": 2, "gn": 6, "odd": 7, "fin": 11, "sec": 15, "hgo": 19, "sa": 20, "ffn": 21}
AT = {name: NK * i for i, name in enumerate(FEATURES)}

GAINS = [("norm_mem_2", 0), ("even_norm_g", 0), ("even_gn_g", 4), ("odd_norm_g", 0), ("norm_mix_2", 0),
         ("norm_ffn_2", 0)]
G_MEM, G_EVEN, G_GN, G_ODD, G_SEC, G_FFN, G_HG = range(7)
HEAD_GAINS = ["sa_q_gain_2", "sa_k_gain_2", "mem_q_gain_2", "mem_k_gain_2"]
N_CONST = 4 + len(GAINS) + 1 + 2 * len(HEAD_GAINS)


def causal_ext(u):
    return P * (u % 4 + 1)


def last_ext(u):
    return causal_ext(u) if u < 16 else 2 * P


def program(nc, w, c, out):
    ctx = ExitStack()
    with ctx:
        def sb(on, name, shape, dt=f32):
            return on.enter_context(nc.sbuf_tensor(name, shape, dt))

        made = {}

        def sem(name):
            if name not in made:
                made[name] = ctx.enter_context(nc.semaphore(name))
            return made[name]

        X = sb(ctx, "x_tokens", [P, NT, D])
        RAW = sb(ctx, "weight_raw", [P, R, 2, 512])
        WH = sb(ctx, "weight_high", [P, R, 2, 512], f32r)
        WL = sb(ctx, "weight_low", [P, R, 2, 512], f32r)
        SMR = sb(ctx, "small_raw", [P, NK, 72])
        SMH = sb(ctx, "small_high", [P, NK, 72], f32r)
        SML = sb(ctx, "small_low", [P, NK, 72], f32r)
        ID = sb(ctx, "identity", [P, P])
        IDB = sb(ctx, "identity_bf16", [P, P], bf16)
        CAUSAL = sb(ctx, "causal_bf16", [P, P], bf16)
        MINUS3 = sb(ctx, "minus_ones_bf16", [3, P], bf16)
        HALF = sb(ctx, "minus_half", [P, 64])
        SS = sb(ctx, "mean_squares", [P, 64])
        RS = sb(ctx, "rstd", [P, 64])
        NMAX = sb(ctx, "minus_max", [P, 4])
        SUM = sb(ctx, "sums", [P, 8])
        RSUM = sb(ctx, "one_over_sum", [P, 8])
        SCL = sb(ctx, "gate_over_sum", [P, 8])
        GAIN = sb(ctx, "gains", [P, 12, NK])
        MEMKV = sb(ctx, "mem_k_v", [P, 2, 512])

        lay = ExitStack()
        AH = sb(lay, "act_high", [P, NK, T], f32r)
        AL = sb(lay, "act_low", [P, NK, T], f32r)
        H = sb(lay, "h_tokens", [P, NT, D])
        lay_e = ExitStack()
        E_UT = sb(lay_e, "even_qk", [P, 16, T])
        E_V = sb(lay_e, "even_v", [P, NT, D])
        E_Z = sb(lay_e, "even_silu_z", [P, NT, D])
        FL = sb(lay_e, "forget_tokens", [P, NT, 8])
        FL2 = sb(lay_e, "forget_abs", [P, NT, 8])
        BF = sb(lay_e, "forget_bias", [P, 8])
        FB = sb(lay_e, "forget_parts", [8, 3, T], bf16)
        FC = sb(lay_e, "forget_cumsum", [8, T])
        FO = sb(lay_e, "forget_ones", [8, T])
        C3 = sb(lay_e, "decay_rows", [3, 8, T], bf16)
        lay_e.close()
        lay_f = ExitStack()
        FING = sb(lay_f, "final_gain", [P, D])
        lay_f.close()
        lay_o = ExitStack()
        O_Q = sb(lay_o, "odd_q", [P, 8, T])
        O_K = sb(lay_o, "odd_k", [P, 2, 4, T])
        O_V = sb(lay_o, "odd_v", [P, NT, 512])
        O_Z = sb(lay_o, "odd_silu_z", [P, NT, D])
        KCVC = sb(lay_o, "kc_vc", [P, 4, T])
        ALS = sb(lay_o, "alibi_slopes", [P, 16, P], bf16)
        ALJ = sb(lay_o, "alibi_positions", [P, T], bf16)
        GATE = sb(lay_o, "gates", [P, NT, 48])
        BG = sb(lay_o, "gate_bias", [P, 48])
        PE2 = sb(lay_o, "cmp_pe", [P, 2, 16])
        W2 = sb(lay_o, "cmp_w2", [P, 2, 2, HD])
        W2D = sb(lay_o, "cmp_w2_twice", [P, 2, 2, HD])
        CHID = sb(lay_o, "cmp_hidden", [P, 2, 2, 4, 32])
        lay_o.close()
        lay_s = ExitStack()
        S_N = sb(lay_s, "sa_q_k_v_mq", [P, NT, D])
        I_Q = sb(lay_s, "index_q", [P, 4, T])
        I_K = sb(lay_s, "index_k", [P, T])
        I_W = sb(lay_s, "index_w", [P, NT, 8])
        SEL = sb(lay_s, "sel_mask", [P, NT, T], bf16)
        lay_g = ExitStack()
        G_F = sb(lay_g, "hg_q_f", [P, 8, T])
        G_N = sb(lay_g, "hg_i_g", [P, NT, D])
        G_B = sb(lay_g, "hg_cumsum", [P, 4, T])
        G_M = sb(lay_g, "hg_masks", [P, 8, P], u32)
        G_S = sb(lay_g, "hg_state", [P, 4, 3, P])
        G_X = sb(lay_g, "hg_last", [P, 4, NT])
        lay_g.close()
        lay_a = ExitStack()
        S_2 = sb(lay_a, "sa_squares", [P, NT, D])
        S_QK = sb(lay_a, "sa_q_k", [P, 4, T])
        M_Q = sb(lay_a, "mem_q", [P, 2, T])
        M_K = sb(lay_a, "mem_k", [P, 2, 2 * P])
        lay_a.close()
        lay_s.close()
        lay.close()
        ov = ExitStack()
        E_Q = sb(ov, "even_q_stage", [P, 2, T])
        E_K = sb(ov, "even_k_stage", [P, 2, T])
        E_P = sb(ov, "even_probs", [P, 2, T])
        E_PT = sb(ov, "even_probs_t", [P, 2, T])
        RD = sb(ov, "retention_decay", [P, 2, 2, T])
        ov.close()
        ovc = ExitStack()
        CI = sb(ovc, "cmp_in", [P, 16, 4, CMP])
        CIH = sb(ovc, "cmp_in_high", [P, 16, 4 * CMP], f32r)
        CIL = sb(ovc, "cmp_in_low", [P, 16, 4 * CMP], f32r)
        CB = sb(ovc, "cmp_bias", [P, 16, 32])
        KCMP = sb(ovc, "k_cmp", [P, 4, 32])
        BDV = sb(ovc, "v_cmp_blocks", [P, 4, 4, HD])
        ovc.close()
        ovd = ExitStack()
        SC = sb(ovd, "cmp_scores", [P, 16, 32])
        CPT = sb(ovd, "cmp_probs_t", [P, 4, P])
        CMX = sb(ovd, "cmp_max", [P, 4, 16])
        ovd.close()
        ovo = ExitStack()
        O_QS = sb(ovo, "odd_q_stage", [P, 2, T])
        O_KS = sb(ovo, "odd_k_stage", [P, 2, T])
        O_P = sb(ovo, "odd_probs", [P, 2, T])
        O_PT = sb(ovo, "odd_probs_t", [P, 2, T])
        O_T = sb(ovo, "odd_head_out", [P, 2, 4, HD])
        ovo.close()
        ovg = ExitStack()
        G_E = sb(ovg, "hg_decay", [P, 2, 4, T])
        G_A = sb(ovg, "hg_weights", [P, 4, 4, P])
        G_KT = sb(ovg, "hg_key_tokens", [P, 4, 3, P])
        G_R = sb(ovg, "scan_reset", [P, T])
        ovg.close()
        ova = ExitStack()
        S_P = sb(ova, "sa_probs", [P, 2, T])
        S_PT = sb(ova, "sa_probs_t", [P, 2, T])
        ova.close()
        ovh = ExitStack()
        sb(ovh, "act_stays", [P, 2 * NK * T])
        I_KN = sb(ovh, "index_k_tokens", [P, NT, P])
        RL = sb(ovh, "index_relu", [P, 2, T])
        SCO = sb(ovh, "index_scores", [P, 3, T])
        MX8 = sb(ovh, "max8", [P, 8])
        MASKF = sb(ovh, "causal_f32", [P, P])
        ovh.close()
        ffn = ExitStack()
        sb(ffn, "act_still_there", [P, 2 * NK * T])
        FH = sb(ffn, "ffn_high", [P, NF, T], f32r)
        FLO = sb(ffn, "ffn_low", [P, NF, T], f32r)
        FT = sb(ffn, "ffn_silu", [P, 2, T])
        ffn.close()

        PS = ctx.enter_context(nc.psum_tensor("psum", [P, 8, 512], f32))

        raw_ready = [sem(f"raw_ready{i}") for i in range(R)]
        high_ready = sem("high_ready")
        split_ready = sem("split_ready")
        chunk_done = sem("chunk_done")
        out_done = sem("out_done")
        bank_free = sem("bank_free")
        squares_ready = sem("squares_ready")
        mean_ready = sem("mean_ready")
        rstd_ready = sem("rstd_ready")
        normed_ready = sem("normed_ready")
        turned = sem("turned")
        act_high = sem("act_high")
        act_low = sem("act_low")
        sc_ready = sem("scores_ready")
        mx_ready = sem("max_ready")
        p_ready = sem("probs_ready")
        t_ready = sem("transposed_ready")
        pt_ready = sem("probs_t_ready")
        o_ready = sem("values_ready")
        o_done = sem("output_taken")

        def wait_out(eng, name, i, k, last):
            outs = 2 if name == "mem" else 4
            if last:
                eng.wait_ge(chunk_done, R + CH[name] + R * i + R)
            else:
                eng.wait_ge(out_done, ODONE[name] + (outs - 1) * i + k + 1)

        def wait_group(eng, name):
            eng.wait_ge(bank_free, 4 + OUT[name] + BLOCKS[name] * 4)

        block = ctx.enter_context(nc.Block())

        @block.sync
        def _(sp):
            sp.dma_start(H[:, 0:2, :], w["mem_2"][0].rearrange("(t p) d -> p t d", p=P)).then_inc(sem("mem_loaded"), 16)

            def chunk(n, parts):
                if n >= R:
                    sp.wait_ge(split_ready, n - R + 1)
                for at, src in parts:
                    sp.dma_start(RAW[:, n % R, :, at:at + src.shape[1]],
                                 src.rearrange("(k p) n -> p k n", p=P)).then_inc(
                                     raw_ready[n % R], 32 // len(parts))

            def load_block(n, mat, parts):
                for r in range(R):
                    chunk(n + r, [(at, mat[256 * r:256 * r + 256, a:a + m]) for at, a, m in parts])

            def small(k, mat, a, m):
                if k:
                    sp.wait_ge(sem("small_done"), k)
                sp.dma_start(SMR[:, :, 0:m], mat[:, a:a + m].rearrange("(k p) n -> p k n", p=P)).then_inc(
                    sem("small_loaded"), 16)

            load_block(CH["mem"], w["w_mem_kv_2"][0], [(0, 0, 512)])
            sp.dma_start(X[:, :, :], w["x"][0].rearrange("(t p) d -> p t d", p=P)).then_inc(sem("x_loaded"), 16)
            we = w["even_w_in"][0]
            small(0, we, 1536, 8)
            for i, a in enumerate((0, 512, 1544, 2056)):
                load_block(CH["even_qk"] + R * i, we, [(0, a, 512)])
            for i, a in enumerate((1024, 2568)):
                load_block(CH["even_v"] + R * i, we, [(0, a, 512)])
            for i in range(2):
                load_block(CH["even_z"] + R * i, we, [(0, 3080 + 512 * i, 512)])
            for i in range(2):
                load_block(CH["even_out"] + R * i, w["even_w_out"][0], [(0, 512 * i, 512)])
            wo = w["odd_w_in"][0]
            small(1, wo, 2560, 48)
            for i in range(2):
                load_block(CH["odd_q"] + R * i, wo, [(0, 512 * i, 512)])
            load_block(CH["odd_kv"], wo, [(0, 1024, 512)])
            load_block(CH["odd_kv"] + R, wo, [(0, 1536, 256), (256, 2048, 256)])
            load_block(CH["odd_v"], wo, [(0, 1792, 256), (256, 2304, 256)])
            for i in range(2):
                load_block(CH["odd_z"] + R * i, wo, [(0, 2608 + 512 * i, 512)])
            for i, name in enumerate(("odd_wk1", "odd_wv1")):
                for r in range(R):
                    n = CH["cmp"] + R * i + r
                    sp.wait_ge(split_ready, n - R + 1)
                    sp.dma_start(RAW[:, n % R, :, :].rearrange("p a (b n) -> p (a b) n", b=2),
                                 w[name][0][512 * r:512 * r + 512, :].rearrange("(k p) n -> p k n", p=P)).then_inc(
                                     raw_ready[n % R], 32)
            for i in range(2):
                load_block(CH["odd_out"] + R * i, w["odd_w_out"][0], [(0, 512 * i, 512)])
            w2 = w["w_in_2"][0]
            small(2, w2, 3328, 72)
            load_block(CH["sa_i"], w2, [(0, 2816, 512)])
            load_block(CH["sa_n"], w2, [(0, 2048, 512)])
            load_block(CH["sa_n"] + R, w2, [(0, 2560, 256), (256, 3400, 256)])
            for i in range(2):
                load_block(CH["hg_f"] + R * i, w2, [(0, 512 * i, 512)])
            for i in range(2):
                load_block(CH["hg_n"] + R * i, w2, [(0, 1024 + 512 * i, 512)])
            for i in range(2):
                load_block(CH["sec_out"] + R * i, w["w_out_2"][0], [(0, 512 * i, 512)])
            for i in range(BLOCKS["ffn_in"]):
                load_block(CH["ffn_in"] + R * i, w["w_ffn_in_2"][0], [(0, 256 * i, 256), (256, FF + 256 * i, 256)])
            for i in range(2):
                for r in range(OUT_CHUNKS):
                    chunk(CH["ffn_out"] + OUT_CHUNKS * i + r,
                          [(0, w["w_ffn_out_2"][0][256 * r:256 * r + 256, 512 * i:512 * i + 512])])
            for i in range(2):
                sp.wait_ge(bank_free, 4 + OUT["ffn_out"] + 4 * (i + 1))
                sp.dma_start(out[0].rearrange("(t p) d -> p t d", p=P)[:, :, 512 * i:512 * i + 512],
                             X[:, :, 512 * i:512 * i + 512]).then_inc(sem("stored"), 16)
            sp.wait_ge(sem("stored"), 32)

        @block.gpsimd
        def _(pool):
            def load(dst, src, name):
                pool.dma_start(dst, src).then_inc(sem(name), 16)

            def split(n0, blocks, slots=range(R)):
                def body(i):
                    for r in slots:
                        pool.wait_ge(high_ready, n0 + R * i + r + 1)
                        nc.gpsimd.tensor_tensor(WL[:, r], RAW[:, r], WH[:, r].bitcast(f32),
                                                ALU.subtract).then_inc(split_ready, 1)
                if blocks == 1:
                    body(0)
                else:
                    with pool.Fori(0, blocks) as i:
                        body(i)

            def split_ahead(name):
                split(CH[name] + R, BLOCKS[name])

            def split_around_norm(name, use):
                split(CH[name] + R, 1)
                split(CH[name] + 2 * R, 1, range(R - 1))
                rstd(use, 1, NT)
                if use == "fin":
                    rstd("sec", 1, NT)
                split(CH[name] + 2 * R, 1, range(R - 1, R))

            def small_split(k, m):
                pool.wait_ge(sem("small_high"), k + 1)
                nc.gpsimd.tensor_tensor(SML[:, :, 0:m], SMR[:, :, 0:m], SMH[:, :, 0:m].bitcast(f32),
                                        ALU.subtract).then_inc(sem("small_low"), 1)

            def rstd(use, n, tiles=1):
                for t in range(tiles):
                    pool.wait_ge(mean_ready, RSTDS[use] + t + 1)
                    nc.gpsimd.tensor_tensor(RS[:, n * t:n * t + n], SS[:, n * t:n * t + n], HALF[:, 0:n],
                                            ALU.pow).then_inc(rstd_ready, 1)

            pool.sem_inc(sem("head_added"), 2)
            nc.gpsimd.memset(HALF[:, :], -0.5)
            nc.gpsimd.memset(GAIN[:, G_GN, 0:4], 1.0)
            nc.gpsimd.memset(GAIN[:, G_HG, 4:8], 1.0).then_inc(sem("half_ready"), 1)
            pool.wait_ge(sem("half_ready"), 1)
            load(ID[:, :], c["identity"], "const")
            load(IDB[:, :], c["identity_bf16"], "const")
            load(CAUSAL[:, :], c["causal_bf16"], "const")
            load(MINUS3[:, :], c["minus_one3"], "const")
            with nc.allow_non_contiguous_dma(reason="gain vectors, once"):
                for i, (name, first) in enumerate(GAINS):
                    load(GAIN[:, i, first:NK], w[name][0].rearrange("(k p) -> p k", p=P), "const")
                load(GAIN[:, G_HG, 0:1], w["hg_out_gain_2"][0].rearrange("(d o) -> d o", o=1), "const")
                for i, name in enumerate(HEAD_GAINS):
                    for half in range(2):
                        load(GAIN[HD * half:HD * half + HD, 8 + i, 0:1],
                             w[name][0].rearrange("(d o) -> d o", o=1), "const")
            load(BF[:, :], w["even_b_f"][0:1, :].to_broadcast((P, 8)), "forget_bias")
            split(0, 1)
            rstd("mem", 1, 2)
            rstd("even", 1, NT)
            split_ahead("mem")
            small_split(0, 8)
            split_ahead("even_qk")
            split_ahead("even_v")
            split_ahead("even_z")
            pool.wait_ge(sem("forget_parts"), 1)
            for i in range(3):
                load(C3[i:i + 1, :, :], FB[:, i, :], "decay_rows")
            pool.wait_ge(chunk_done, R + CH["even_out"])
            with pool.Fori(0, 2) as i:
                for b in range(2):
                    pool.wait_ge(sem("ret_used"), CREDIT + 8 * (2 * i + b) - 8)
                    load(RD[:, b], c["retention"][:, bass.ds(4 * i + 2 * b, 2), :], f"ret_decay{b}")
            rstd("gn", 32)
            split_around_norm("even_out", "odd")
            wait_group(pool, "even_out")
            load(ALS[:, :, :], c["alibi_slopes"], "odd_tables")
            load(ALJ[:, :], c["alibi_positions"], "odd_tables")
            load(BG[:, :], w["odd_b_gate"][0:1, :].to_broadcast((P, 48)), "odd_tables")
            with nc.allow_non_contiguous_dma(reason="position vectors, once"):
                for i, name in enumerate(("odd_pe_k", "odd_pe_v")):
                    for l in range(2):
                        load(PE2[HD * l:HD * l + HD, i, :],
                             w[name][0].rearrange("(a l) d -> d l a", l=2)[:, l, :], "odd_tables")
            for i, name in enumerate(("odd_wk2", "odd_wv2")):
                load(W2[:, i, :, :], w[name][0].rearrange("(k p) d -> p k d", p=P), "odd_tables")
            for k in range(2):
                load(W2D[:, :, k, :], w["odd_wk2"][0].rearrange("(k p) d -> p k d", p=P), "odd_tables")
            nc.gpsimd.memset(CHID[:, :, :, :, :], 0.0).then_inc(sem("cmp_hidden_zero"), 1)
            split_ahead("odd_q")
            small_split(1, 48)
            split_ahead("odd_kv")
            split_ahead("odd_v")
            split_ahead("odd_z")
            split_ahead("cmp")
            for t in range(NT):
                if t:
                    pool.wait_ge(sem("cmp_biased"), t)
                else:
                    pool.wait_ge(chunk_done, R + CH["cmp"])
                load(CB[:, :, :], c["cmp_bias"][:, t], "cmp_bias")
            with pool.Fori(0, 4) as i:
                for j in range(8):
                    pool.wait_ge(o_done, CREDIT + (UNITS["odd"] // 4) + 8 * i + j + 1)
                    pool.sem_inc(sem("head_seen"), 1)
                    cols = bass.ds(256 * i + HD * (j % 4), HD)
                    nc.gpsimd.tensor_tensor(H[:, :, cols], H[:, :, cols], O_T[:, j % 2], ALU.add).then_inc(
                        sem("head_added"), 1)
            pool.wait_ge(o_ready, CREDIT + UNITS["sa"])
            load(FING[:, :], w["final_g"].rearrange("(o d) -> o d", o=1).to_broadcast((P, D)), "final_gain")
            split_around_norm("odd_out", "fin")
            load(G_M[:, :, :], c["tree_masks"], "sec_tables")
            small_split(2, 72)
            pool.wait_ge(turned, AT["sec"] + NK)
            load(MASKF[:, :], c["causal_f32"], "sa_tables")
            for name in ("sa_i", "sa_n", "hg_f", "hg_n"):
                split_ahead(name)
            pool.wait_ge(chunk_done, R + CH["sec_out"])
            load(G_R[:, :], c["scan_reset"], "scan_reset")
            rstd("hgo", 16)
            rstd("sa", 56)
            split_around_norm("sec_out", "ffn")
            split_ahead("ffn_in")
            split(CH["ffn_out"] + R, 4)
            for r in range(2):
                pool.wait_ge(high_ready, CH["ffn_out"] + 5 * R + r + 1)
                nc.gpsimd.tensor_tensor(WL[:, r], RAW[:, r], WH[:, r].bitcast(f32),
                                        ALU.subtract).then_inc(split_ready, 1)

        @block.scalar
        def _(act):
            act.sem_inc(p_ready, CREDIT)
            act.sem_inc(sem("ret_taken"), CREDIT)

            def split(n0, blocks, slots=range(R)):
                def body(i):
                    for r in slots:
                        act.wait_ge(raw_ready[r], 32 * (n0 // R + i + 1))
                        act.wait_ge(chunk_done, n0 + R * i + r + 1)
                        nc.scalar.activation(WH[:, r], RAW[:, r], ACT.Copy).then_inc(high_ready, 1)
                if blocks == 1:
                    body(0)
                else:
                    with act.Fori(0, blocks) as i:
                        body(i)

            def split_ahead(name):
                split(CH[name] + R, BLOCKS[name])

            def small_split(k, m):
                act.wait_ge(sem("small_loaded"), 16 * (k + 1))
                nc.scalar.activation(SMH[:, :, 0:m], SMR[:, :, 0:m], ACT.Copy).then_inc(sem("small_high"), 1)

            def split_around_norm(name, use):
                split(CH[name] + R, 1)
                split(CH[name] + 2 * R, 1, range(R - 1))
                squares(use, X, H, after=(bank_free, 4 + OUT[name] + 4))
                if use == "fin":
                    squares("sec", X, H, after=(sem("fin_x"), 0))
                split(CH[name] + 2 * R, 1, range(R - 1, R))

            def squares(use, src, dst, nt=NT, after=None):
                for t in range(nt):
                    if after:
                        act.wait_ge(after[0], after[1] + t + 1)
                    nc.scalar.activation(dst[:, t, :], src[:, t, :], ACT.Square,
                                         accum_out=SS[:, t:t + 1]).then_inc(squares_ready, 1)

            def features(use, gain, nt=NT):
                for k in range(NK):
                    act.wait_ge(turned, AT[use] + k + 1)
                    g = 0 if gain == G_HG and k < 4 else k
                    scale = 1.0 if gain is None else GAIN[:, gain, g:g + 1]
                    nc.scalar.activation(AH[:, k, 0:P * nt], PS[:, 4 + k % 4, 0:P * nt],
                                         ACT.Identity, scale=scale).then_inc(act_high, 1)

            def exps(at0, nu, ext, probs):
                for u in range(nu):
                    act.wait_ge(mx_ready, CREDIT + at0 + u + 1)
                    act.wait_ge(t_ready, CREDIT + at0 + u - 1)
                    n = ext(u)
                    nc.scalar.activation(probs[:, u % 2, 0:n], PS[:, S_BANK[u % 4], 0:n], ACT.Exp,
                                         bias=NMAX[:, u % 4:u % 4 + 1],
                                         accum_out=SUM[:, u % 8:u % 8 + 1]).then_inc(p_ready, 1)


            def high(block, i, r):
                act.wait_ge(raw_ready[r], 32 * (block + i + 1))
                act.wait_ge(chunk_done, R * block + R * i + r + 1)
                nc.scalar.activation(WH[:, r], RAW[:, r], ACT.Copy).then_inc(high_ready, 1)

            def split_and_take(name, i, dst, between=None, func=ACT.Copy):
                for r in range(R):
                    if between:
                        between(R * i + r)
                    if r == R - 1:
                        for j in range(3):
                            wait_out(act, name, i, j, False)
                            nc.scalar.activation(dst[:, j, :], PS[:, j, :], func).then_inc(bank_free, 1)
                    high(CH[name] // R + 1, i, r)
                wait_out(act, name, i, 3, True)
                nc.scalar.activation(dst[:, 3, :], PS[:, 3, :], func).then_inc(bank_free, 1)

            def relus(c):
                for n in range(3 * c, 3 * c + 3):
                    act.wait_ge(sem("index_ready"), n + 1)
                    if n >= 2:
                        act.wait_ge(sem("index_added"), n - 1)
                    k = P * (n // 8 + 2)
                    nc.scalar.activation(RL[:, n % 2, 0:k], PS[:, 4 + n % 4, 0:k], ACT.Relu).then_inc(
                        sem("index_relu"), 1)

            split(0, 1)
            act.wait_ge(sem("mem_loaded"), 16)
            act.wait_ge(sem("const"), 16 * N_CONST)
            act.wait_ge(sem("half_ready"), 1)
            squares("mem", H, H[:, 2:4, :], 2)
            features("mem", G_MEM, 2)
            act.wait_ge(sem("x_loaded"), 16)
            squares("even", X, H)
            split_ahead("mem")
            small_split(0, 8)
            features("even", G_EVEN)
            split_ahead("even_qk")
            split_ahead("even_v")
            act.wait_ge(sem("forget_abs"), 1)
            nc.scalar.activation(FL2[:, :, :], FL2[:, :, :], ACT.Exp, scale=-1.0)
            nc.scalar.drain()
            nc.scalar.activation(FL2[:, :, :], FL2[:, :, :], ACT.Ln, bias=1.0).then_inc(sem("forget_ln"), 1)
            for i in range(2):
                split_and_take("even_z", i, E_Z[:, :, 512 * i:512 * i + 512], func=ACT.Silu)
            with act.Fori(0, 2) as i:
                at0 = UNITS["fox"] + 16 * i
                act.wait_ge(sc_ready, CREDIT + at0)
                nc.scalar.activation(E_K[:, :, :], E_UT[:, bass.ds(4 + 2 * i, 2), :], ACT.Copy)
                nc.scalar.activation(E_Q[:, :, :], E_UT[:, bass.ds(2 * i, 2), :], ACT.Copy,
                                     scale=0.125).then_inc(sem("q_staged"), 1)
                exps(at0, 16, causal_ext, E_P)
            with act.Fori(0, 2) as i:
                for b in range(2):
                    at0 = 8 * (2 * i + b)
                    act.wait_ge(sem("ret_used"), CREDIT + at0 - 8)
                    nc.scalar.activation(E_Q[:, b, :], E_UT[:, bass.ds(8 + 2 * i + b, 1), :].rearrange(
                        "p a t -> p (a t)"), ACT.Copy)
                    nc.scalar.activation(E_K[:, b, :], E_UT[:, bass.ds(12 + 2 * i + b, 1), :].rearrange(
                        "p a t -> p (a t)"), ACT.Copy, scale=0.125).then_inc(sem("ret_k_staged"), 1)
                    for a in range(2):
                        act.wait_ge(sem("ret_used"), CREDIT + at0 + 4 * a + 4)
                        nc.scalar.activation(H[:, :, bass.ds(512 + 256 * i + HD * (2 * b + a), HD)],
                                             PS[:, O_BANK[a], 0:4 * HD].rearrange("p (t d) -> p t d", t=4),
                                             ACT.Copy).then_inc(sem("ret_taken"), 1)
            act.wait_ge(sem("gn_centered"), 1)
            nc.scalar.activation(E_UT[:, 8:12, :], H[:, :, 512:1024], ACT.Square).then_inc(sem("gn_squared"), 1)
            features("even_y", G_GN)
            split_around_norm("even_out", "odd")
            features("odd", G_ODD)
            split_ahead("odd_q")
            small_split(1, 48)
            split_ahead("odd_kv")
            split_ahead("odd_v")
            act.wait_ge(sem("gate_sum"), 1)
            nc.scalar.activation(GATE[:, :, :], GATE[:, :, :], ACT.Sigmoid).then_inc(sem("gates"), 1)
            for i in range(2):
                split_and_take("odd_z", i, O_Z[:, :, 512 * i:512 * i + 512], func=ACT.Silu)
            for i in range(2):
                act.wait_ge(sem("cmp_in"), i + 1)
                nc.scalar.activation(CIH[:, :, :], CI[:, :, :, :].rearrange("p l g c -> p l (g c)"),
                                     ACT.Copy).then_inc(sem("cmp_high"), 1)
                split(CH["cmp"] + R + R * i, 1)
                act.wait_ge(chunk_done, R + CH["cmp"] + R * i + R)
                if i == 0:
                    act.wait_ge(sem("cmp_hidden_zero"), 1)
                for h in range(2):
                    nc.scalar.activation(CHID[:, i, h, :, 0:CMP],
                                         PS[:, 4 + 2 * i + h, 0:4 * CMP].rearrange("p (g c) -> p g c", g=4),
                                         ACT.Silu).then_inc(sem("cmp_hidden"), 1)
            for t in range(NT):
                act.wait_ge(sem("cmp_shifted"), t + 1)
                nc.scalar.activation(SC[:, :, :], SC[:, :, :], ACT.Exp, scale=0.125).then_inc(sem("cmp_exp"), 1)
            act.wait_ge(sem("cmp_taken"), 2 * NT)
            with act.Fori(0, 4) as i:
                at0 = UNITS["odd"] + 32 * i
                act.wait_ge(sc_ready, CREDIT + at0)
                act.sem_inc(sem("q_stage_free"), 1)
                nc.scalar.activation(O_KS[:, :, :].unsqueeze(2), O_K[:, :, bass.ds(i, 1), :], ACT.Copy)
                nc.scalar.activation(O_QS[:, :, :], O_Q[:, bass.ds(2 * i, 2), :], ACT.Copy,
                                     scale=0.125).then_inc(sem("q_staged"), 1)
                exps(at0, 32, causal_ext, O_P)
            features("odd_y", None)
            split_around_norm("odd_out", "fin")
            features("sec", G_SEC)
            small_split(2, 72)
            split_ahead("sa_i")
            for i in range(2):
                split_and_take("sa_n", i, S_N[:, :, 512 * i:512 * i + 512], relus)
            with act.Fori(0, 2) as i:
                split_and_take("hg_f", i, G_F[:, bass.ds(4 * i, 4), :])
            with act.Fori(0, 2) as i:
                split_and_take("hg_n", i, G_N[:, :, bass.ds(512 * i, 512)])
            act.wait_ge(sem("hg_abs"), 1)
            nc.scalar.activation(G_E[:, 0], G_E[:, 0], ACT.Exp, scale=-1.0)
            nc.scalar.drain()
            nc.scalar.activation(G_E[:, 0], G_E[:, 0], ACT.Ln, bias=1.0).then_inc(sem("hg_ln"), 1)
            act.wait_ge(sem("hg_logf"), 1)
            nc.scalar.activation(G_F[:, 4:8, :], G_F[:, 4:8, :], ACT.Sigmoid, scale=-1.0)
            nc.scalar.activation(G_F[:, 0:4, :], G_F[:, 0:4, :], ACT.Silu)
            nc.scalar.activation(G_N[:, :, 512:D], G_N[:, :, 512:D], ACT.Silu).then_inc(sem("hg_qk"), 1)
            act.wait_ge(sem("hg_cumsum"), 1)
            nc.scalar.activation(G_X[:, :, :], G_B[:, :, P - 1::P], ACT.Exp).then_inc(sem("hg_lasts"), 1)
            for l in range(len(HALVES) + 2):
                if l < len(HALVES) + 1:
                    act.wait_ge(sem("hg_diff"), l + 1)
                else:
                    act.wait_ge(sem("hg_buffer_free"), 1)
                src = G_E[:, l % 2] if l < len(HALVES) + 1 else G_B[:, :, :]
                nc.scalar.activation(G_E[:, l % 2], src, ACT.Exp).then_inc(sem("hg_exp"), 1)
            for h in range(4):
                act.wait_ge(sem("hg_out"), h + 1)
                nc.scalar.activation(H[:, :, P * h:P * h + P], PS[:, 4 + h, :].rearrange("p (t d) -> p t d", t=4),
                                     ACT.Copy)
            nc.scalar.drain()
            nc.scalar.activation(G_E[:, 0], H[:, :, 0:512], ACT.Square).then_inc(sem("hg_squared"), 1)
            act.wait_ge(sem("hg_gated"), 1)
            nc.scalar.activation(S_2[:, :, 0:512], S_N[:, :, 0:512], ACT.Square)
            nc.scalar.activation(S_2[:, :, 512:768], S_N[:, :, 768:D], ACT.Square)
            nc.scalar.activation(S_2[:, 0:2, 768:D], MEMKV[:, :, 0:256], ACT.Square).then_inc(sem("sa_squared"), 1)
            for k in range(8):
                act.wait_ge(sem("sa_turned"), k + 1)
                which, pair = divmod(k, 2)
                dst = (S_QK[:, pair, :], S_QK[:, 2 + pair, :], M_Q[:, pair, :], M_K[:, pair, :])[which]
                nc.scalar.activation(dst, PS[:, 4 + k % 4, 0:2 * P if which == 3 else T], ACT.Identity,
                                     scale=GAIN[:, 8 + which, 0:1]).then_inc(sem("sa_features"), 1)
            exps(UNITS["sa"], 32, last_ext, S_P)
            features("sec_y", G_HG)
            split_around_norm("sec_out", "ffn")
            features("ffn", G_FFN)
            with act.Fori(0, BLOCKS["ffn_in"]) as i:
                def high(r, i=i):
                    act.wait_ge(raw_ready[r], 32 * ((CH["ffn_in"] + R) // R + i + 1))
                    act.wait_ge(chunk_done, CH["ffn_in"] + R + R * i + r + 1)
                    nc.scalar.activation(WH[:, r], RAW[:, r], ACT.Copy).then_inc(high_ready, 1)
                for r in range(R - 1):
                    high(r)
                for j in range(2):
                    act.wait_ge(out_done, ODONE["ffn_in"] + 3 * i + 2 * j + 1)
                    act.wait_ge(sem("hidden_low"), 2 * i)
                    nc.scalar.activation(FT[:, j, :], PS[:, j, :], ACT.Silu).then_inc(sem("ffn_silu"), 1)
                for j in range(2):
                    if j:
                        high(R - 1)
                    act.wait_ge(sem("ffn_mul"), 2 + 2 * i + j + 1)
                    nc.scalar.activation(FH[:, bass.ds(2 * i + j, 1), :].rearrange("p a t -> p (a t)"),
                                         FT[:, j, :], ACT.Copy).then_inc(sem("hidden_high"), 1)
            split(CH["ffn_out"] + R, 4)
            for r in range(2):
                n = CH["ffn_out"] + 5 * R + r
                act.wait_ge(raw_ready[r], 32 * (n // R + 1))
                act.wait_ge(chunk_done, n + 1)
                nc.scalar.activation(WH[:, r], RAW[:, r], ACT.Copy).then_inc(high_ready, 1)

        @block.vector
        def _(dve):
            v = nc.vector
            dve.sem_inc(bank_free, 4)
            dve.sem_inc(sem("ffn_mul"), 2)
            for one in (mx_ready, pt_ready, o_done, sem("ret_weighted")):
                dve.sem_inc(one, CREDIT)

            def norm(use, src, nt=NT):
                for t in range(nt + 1):
                    if t < nt:
                        mean(use, t)
                    if t:
                        scale(use, t - 1, src)

            def mean(use, t):
                dve.wait_ge(squares_ready, SQUARES[use] + t + 1)
                v.tensor_scalar(SS[:, t:t + 1], SS[:, t:t + 1], 1.0 / D, RMS_EPS, ALU.mult, ALU.add).then_inc(
                    mean_ready, 1)

            def scale(use, t, src=X):
                dve.wait_ge(rstd_ready, RSTDS[use] + t + 1)
                if use == "fin":
                    v.scalar_tensor_tensor(X[:, t, :], X[:, t, :], RS[:, t:t + 1], FING[:, :], ALU.mult,
                                           ALU.mult).then_inc(sem("fin_x"), 1)
                else:
                    v.tensor_scalar(H[:, t, :], src[:, t, :], RS[:, t:t + 1], None, ALU.mult).then_inc(
                        normed_ready, 1)

            def features(use, gain, nt=NT):
                for k in range(NK):
                    dve.wait_ge(act_high, AT[use] + k + 1)
                    g = 0 if gain == G_HG and k < 4 else k
                    scale = 1.0 if gain is None else GAIN[:, gain, g:g + 1]
                    v.scalar_tensor_tensor(AL[:, k, 0:P * nt], PS[:, 4 + k % 4, 0:P * nt], scale,
                                           AH[:, k, 0:P * nt].bitcast(f32), ALU.mult, ALU.subtract).then_inc(act_low, 1)

            def take(name, dst, loop=True):
                def body(i):
                    for j in range(4):
                        wait_out(dve, name, i, j, j == 3)
                        v.tensor_copy(dst(i, j), PS[:, j, :]).then_inc(bank_free, 1)
                if BLOCKS[name] == 1 or not loop:
                    for i in range(BLOCKS[name]):
                        body(i)
                else:
                    with dve.Fori(0, BLOCKS[name]) as i:
                        body(i)

            def residual(name, use):
                for i in range(2):
                    for j in range(4):
                        wait_out(dve, name, i, j, j == 3)
                        v.tensor_tensor(X[:, j, 512 * i:512 * i + 512], PS[:, j, :],
                                        X[:, j, 512 * i:512 * i + 512], ALU.add).then_inc(bank_free, 1)
                        if i and j >= 1:
                            mean(use, j - 1)
                        if i and j >= 2:
                            scale(use, j - 2)
                mean(use, 3)
                scale(use, 2)
                scale(use, 3)

            def units(at0, nu, ext, pt, take_head):
                for u in range(nu + 4):
                    if u < nu:
                        dve.wait_ge(sc_ready, CREDIT + at0 + u + 1)
                        v.tensor_reduce(NMAX[:, u % 4:u % 4 + 1], PS[:, S_BANK[u % 4], 0:ext(u)], AX.X, ALU.max,
                                        negate=True).then_inc(mx_ready, 1)
                    if 2 <= u < nu + 2:
                        k = u - 2
                        dve.wait_ge(t_ready, CREDIT + at0 + k + 1)
                        dve.wait_ge(o_ready, CREDIT + at0 + k - 1)
                        v.tensor_copy(pt[:, k % 2, 0:ext(k)], PS[:, T_BANK[k % 2], 0:ext(k)]).then_inc(pt_ready, 1)
                    if u >= 7 and u % 4 == 3:
                        j = (u - 7) // 4
                        dve.wait_ge(o_ready, CREDIT + at0 + 4 * j + 4)
                        four = slice(4 * (j % 2), 4 * (j % 2) + 4)
                        v.reciprocal(RSUM[:, four], SUM[:, four])
                        v.drain()
                        take_head(j, four, PS[:, O_BANK[j % 2], 0:4 * HD].rearrange("p (q d) -> p q d", q=4))

            def each(cols):
                return cols.unsqueeze(2).to_broadcast((P, 4, HD))

            dve.wait_ge(sem("const"), 16 * N_CONST)
            for k in (8, 10):
                v.tensor_scalar(GAIN[:, k, 0:1], GAIN[:, k, 0:1], 0.125, None, ALU.mult)
            norm("mem", H, 2)
            features("mem", G_MEM, 2)
            norm("even", X)
            for j in range(2):
                wait_out(dve, "mem", 0, j, j == 1)
                v.tensor_copy(MEMKV[:, j, :], PS[:, j, :]).then_inc(bank_free, (1, 3)[j])
            features("even", G_EVEN)
            take("even_qk", lambda i, j: E_UT[:, bass.ds(4 * i + j, 1), :].rearrange("p a t -> p (a t)"))
            take("even_v", lambda i, j: E_V[:, j, bass.ds(512 * i, 512)])
            dve.wait_ge(sem("small_done"), 1)
            dve.wait_ge(sem("forget_bias"), 16)
            v.tensor_tensor(FL[:, :, :], PS[:, 4, 0:4 * 8].rearrange("p (t h) -> p t h", t=4),
                            BF[:, :].unsqueeze(1).to_broadcast((P, NT, 8)), ALU.add)
            v.drain()
            v.scalar_tensor_tensor(FL2[:, :, :], FL[:, :, :], -1.0, FL[:, :, :], ALU.mult, ALU.max).then_inc(sem("forget_abs"), 1)
            dve.wait_ge(sem("forget_ln"), 1)
            v.scalar_tensor_tensor(FL[:, :, :], FL[:, :, :], 0.0, FL2[:, :, :], ALU.min, ALU.subtract).then_inc(
                sem("forget_log"), 1)
            dve.wait_ge(sem("forget_turned"), 1)
            v.memset(FO[:, :], 1.0)
            v.drain()
            v.tensor_tensor_scan(FC[:, :], FO[:, :], PS[0:8, 4, :], 0.0, ALU.mult, ALU.add)
            v.drain()
            v.tensor_copy(FB[:, 0, :], FC[:, :])
            v.drain()
            v.tensor_tensor(FO[:, :], FC[:, :], FB[:, 0, :], ALU.subtract)
            v.drain()
            v.tensor_copy(FB[:, 1, :], FO[:, :])
            v.drain()
            v.tensor_tensor(FC[:, :], FO[:, :], FB[:, 1, :], ALU.subtract)
            v.drain()
            v.tensor_copy(FB[:, 2, :], FC[:, :]).then_inc(sem("forget_parts"), 1)

            with dve.Fori(0, 2) as i:
                def fox_head(j, four, values, i=i):
                    v.tensor_tensor(H[:, :, bass.ds(256 * i + HD * j, HD)], values, each(RSUM[:, four]),
                                    ALU.mult).then_inc(o_done, 1)
                units(UNITS["fox"] + 16 * i, 16, causal_ext, E_PT, fox_head)
            with dve.Fori(0, 2) as i:
                for b in range(2):
                    dve.wait_ge(sem(f"ret_decay{b}"), 16 * (i + 1))
                    for u in range(8):
                        at = 8 * (2 * i + b) + u
                        n = T - P * (u % 4)
                        dve.wait_ge(sem("ret_scores"), at + 1)
                        dve.wait_ge(sem("ret_used"), CREDIT + at - 1)
                        v.tensor_tensor(E_P[:, u % 2, 0:n], PS[:, S_BANK[u % 4], 0:n], RD[:, b, u // 4, 0:n],
                                        ALU.mult).then_inc(sem("ret_weighted"), 1)
            HR = H[:, :, 512:D].rearrange("p t (h d) -> p t h d", h=8)
            MEAN = SS[:, 0:32].rearrange("p (t h) -> p t h", t=4)
            dve.wait_ge(sem("ret_taken"), CREDIT + 8)
            v.tensor_reduce(MEAN, HR, AX.X, ALU.add)
            v.drain()
            v.tensor_scalar(SS[:, 0:32], SS[:, 0:32], 1.0 / HD, None, ALU.mult)
            v.drain()
            v.tensor_tensor(HR, HR, MEAN.unsqueeze(3).to_broadcast((P, NT, 8, HD)), ALU.subtract).then_inc(
                sem("gn_centered"), 1)
            dve.wait_ge(sem("gn_squared"), 1)
            v.tensor_reduce(MEAN, E_UT[:, 8:12, :].rearrange("p t (h d) -> p t h d", h=8), AX.X, ALU.add)
            v.drain()
            v.tensor_scalar(SS[:, 0:32], SS[:, 0:32], 1.0 / HD, GN_EPS, ALU.mult, ALU.add).then_inc(mean_ready, 1)
            dve.wait_ge(rstd_ready, RSTDS["gn"] + 1)
            v.tensor_tensor(HR, HR, RS[:, 0:32].rearrange("p (t h) -> p t h", t=4).unsqueeze(3).to_broadcast(
                (P, NT, 8, HD)), ALU.mult)
            v.drain()
            for t in range(NT):
                v.tensor_tensor(H[:, t, :], H[:, t, :], E_Z[:, t, :], ALU.mult).then_inc(normed_ready, 1)
            features("even_y", G_GN)
            residual("even_out", "odd")
            features("odd", G_ODD)

            take("odd_q", lambda i, j: O_Q[:, bass.ds(4 * i + j, 1), :].rearrange("p a t -> p (a t)"))
            for j in range(4):
                wait_out(dve, "odd_kv", 0, j, j == 3)
                v.tensor_copy(KCVC[:, j, :], PS[:, j, :]).then_inc(bank_free, 1)
            for j in range(4):
                wait_out(dve, "odd_kv", 1, j, j == 3)
                for gg in range(2):
                    for half in range(2):
                        last = v.tensor_copy(O_K[HD * half:HD * half + HD, j // 2, 2 * (j % 2) + gg, :],
                                             PS[HD * gg:HD * gg + HD, j, :])
                last.then_inc(bank_free, 1)
            take("odd_v", lambda i, j: O_V[:, j, :])
            dve.wait_ge(sem("odd_tables"), 16 * 11)
            dve.wait_ge(sem("small_done"), 2)
            v.tensor_tensor(GATE[:, :, :], PS[:, 4, 0:4 * 48].rearrange("p (t h) -> p t h", t=4),
                            BG[:, :].unsqueeze(1).to_broadcast((P, NT, 48)), ALU.add).then_inc(sem("gate_sum"), 1)
            dve.wait_ge(chunk_done, R + CH["cmp"])
            for i in range(2):
                if i:
                    dve.wait_ge(chunk_done, R + CH["cmp"] + R)
                for l in range(2):
                    for g in range(4):
                        src = KCVC[HD * (g % 2):HD * (g % 2) + HD, 2 * i + g // 2, :]
                        lo = src[:, l:l + 480].rearrange("p (c a r) -> p a c r", c=30, r=2)[:, :, :, 0]
                        v.tensor_copy(CI[HD * l:HD * l + HD, 0:8, g, 0:30], lo)
                        hi = src[:, 16 + l:16 + l + 480].rearrange("p (c a r) -> p a c r", c=30, r=2)[:, :, :, 0] \
                            if l == 0 else src[:, 17:497].rearrange("p (c a r) -> p a c r", c=30, r=2)[:, :, :, 0]
                        v.tensor_copy(CI[HD * l:HD * l + HD, 8:16, g, 0:30], hi)
                        v.tensor_copy(CI[HD * l:HD * l + HD, :, g, 30], src[:, 480 + l:512:2])
                v.drain()
                v.tensor_tensor(CI[:, :, :, :], CI[:, :, :, :],
                                PE2[:, i, :].unsqueeze(2).unsqueeze(3).to_broadcast((P, 16, 4, CMP)),
                                ALU.add).then_inc(sem("cmp_in"), 1)
                dve.wait_ge(sem("cmp_high"), i + 1)
                v.tensor_tensor(CIL[:, :, :], CI[:, :, :, :].rearrange("p l g c -> p l (g c)"),
                                CIH[:, :, :].bitcast(f32), ALU.subtract).then_inc(sem("cmp_low"), 1)
            v.memset(BDV[:, :, :, :], 0.0)
            dve.wait_ge(sem("cmp_kv"), 1)
            v.tensor_copy(KCMP[:, :, :], PS[:, 0, 0:P].rearrange("p (g c) -> p g c", g=4))
            v.drain()
            for j in range(4):
                last = v.tensor_copy(BDV[32 * j:32 * j + 32, :, j, :],
                                     PS[0:32, 1, 0:256].rearrange("p (g d) -> p g d", g=4))
            last.then_inc(sem("cmp_kv_taken"), 1)
            dve.wait_ge(sem("gates"), 1)
            for t in range(NT):
                dve.wait_ge(sem("cmp_scores"), t + 1)
                dve.wait_ge(sem("cmp_bias"), 16 * (t + 1))
                for odd in range(2):
                    last = v.tensor_tensor(SC[:, odd:16:2, :],
                                           PS[:, t % 2 + 4 * odd, 0:256].rearrange("p (h c) -> p h c", h=8),
                                           CB[:, odd:16:2, :], ALU.add)
                last.then_inc(sem("cmp_biased"), 1)
                v.drain()
                v.tensor_reduce(CMX[:, 0, :], SC[:, :, :], AX.X, ALU.max)
                v.drain()
                v.tensor_scalar(CMX[:, 0, :], CMX[:, 0, :], NEG / 10, None, ALU.max)
                v.drain()
                v.tensor_tensor(SC[:, :, :], SC[:, :, :], CMX[:, 0, :].unsqueeze(2).to_broadcast((P, 16, 32)),
                                ALU.subtract).then_inc(sem("cmp_shifted"), 1)
                dve.wait_ge(sem("cmp_exp"), t + 1)
                v.tensor_reduce(CMX[:, 1, :], SC[:, :, :], AX.X, ALU.add)
                v.drain()
                v.tensor_scalar(CMX[:, 1, :], CMX[:, 1, :], 1e-30, None, ALU.max)
                v.drain()
                v.reciprocal(CMX[:, 2, :], CMX[:, 1, :])
                v.drain()
                v.tensor_tensor(CMX[:, 3, :], CMX[:, 2, :], GATE[:, t, 0:48:3], ALU.mult)
                dve.wait_ge(sem("cmp_turned"), t + 1)
                v.tensor_copy(CPT[:, :, :], PS[:, 6, :].rearrange("p (g q) -> p g q", g=4)).then_inc(
                    sem("cmp_pt"), 1)
                dve.wait_ge(sem("cmp_values"), t + 1)
                for k in range(2):
                    v.tensor_tensor(H[:, t, 512 * k:512 * k + 512].rearrange("p (h d) -> p h d", h=8),
                                    PS[:, 2 + k, :].rearrange("p (h d) -> p h d", h=8),
                                    CMX[:, 3, 8 * k:8 * k + 8].unsqueeze(2).to_broadcast((P, 8, HD)),
                                    ALU.mult).then_inc(sem("cmp_taken"), 1)
            with dve.Fori(0, 4) as i:
                def odd_head(j, four, values, i=i):
                    b, a = divmod(j, 4)
                    v.tensor_tensor(SCL[:, four].unsqueeze(2), RSUM[:, four].unsqueeze(2),
                                    GATE[:, :, bass.ds(12 * i + 3 * a + 1 + b, 1)], ALU.mult)
                    v.drain()
                    dve.wait_ge(sem("head_added"), 8 * i + j + 1)
                    v.tensor_tensor(O_T[:, j % 2], values, each(SCL[:, four]), ALU.mult).then_inc(o_done, 1)
                units(UNITS["odd"] + 32 * i, 32, causal_ext, O_PT, odd_head)
            dve.wait_ge(sem("head_added"), 2 + 32)
            for t in range(NT):
                v.tensor_tensor(H[:, t, :], H[:, t, :], O_Z[:, t, :], ALU.mult).then_inc(normed_ready, 1)
            features("odd_y", None)
            dve.wait_ge(sem("final_gain"), 16)
            residual("odd_out", "fin")

            norm("sec", X)
            features("sec", G_SEC)
            take("sa_i", lambda i, j: I_Q[:, j, :])
            dve.wait_ge(sem("small_done"), 3)
            small = PS[:, 4, 0:4 * 72].rearrange("p (t n) -> p t n", t=4)
            v.tensor_copy(I_KN[:, :, 0:HD], small[:, :, 0:HD])
            v.tensor_copy(I_KN[:, :, HD:P], small[:, :, 0:HD])
            v.tensor_scalar(I_W[:, :, :], small[:, :, HD:72], 8 ** -0.5 * 64 ** -0.5, None, ALU.mult).then_inc(
                sem("index_kw"), 1)
            dve.wait_ge(sem("index_k_turned"), 1)
            v.tensor_copy(I_K[:, :], PS[:, 5, :]).then_inc(sem("index_k"), 1)
            v.tensor_copy(SEL[:, 0, 0:P], CAUSAL[:, :])
            dve.wait_ge(sem("sa_tables"), 16)
            for n in range(24):
                t, h = n // 8, n % 8
                k = P * (t + 2)
                dve.wait_ge(sem("index_relu"), n + 1)
                one, rl = I_W[:, t + 1, h:h + 1], RL[:, n % 2, 0:k]
                if h == 0:
                    v.tensor_scalar(SCO[:, t, 0:k], rl, one, None, ALU.mult).then_inc(sem("index_added"), 1)
                else:
                    v.scalar_tensor_tensor(SCO[:, t, 0:k], rl, one, SCO[:, t, 0:k], ALU.mult, ALU.add).then_inc(
                        sem("index_added"), 1)
                v.drain()
            for t in range(3):
                s = SCO[:, t, 0:P * (t + 2)]
                v.tensor_tensor(s[:, P * (t + 1):], s[:, P * (t + 1):], MASKF[:, :], ALU.add)
                v.drain()
                for k in range(16):
                    v.max(MX8[:, :], s)
                    v.drain()
                    v.match_replace(s, MX8[:, :], s, TAKEN)
                    v.drain()
                v.tensor_scalar(SEL[:, t + 1, 0:P * (t + 2)], s, TAKEN / 2, NEG, ALU.is_gt, ALU.mult).then_inc(
                    sem("selected"), 1)
            wait_group(dve, "hg_n")
            v.scalar_tensor_tensor(G_E[:, 0], G_F[:, 4:8, :], -1.0, G_F[:, 4:8, :], ALU.mult, ALU.max).then_inc(sem("hg_abs"), 1)
            v.memset(G_A[:, :, :, :], 0.0)
            dve.wait_ge(sem("hg_ln"), 1)
            v.scalar_tensor_tensor(G_E[:, 1], G_F[:, 4:8, :], 0.0, G_E[:, 0], ALU.min, ALU.subtract).then_inc(
                sem("hg_logf"), 1)
            v.drain()
            dve.wait_ge(sem("scan_reset"), 16)
            for h in range(4):
                last = v.tensor_tensor_scan(G_B[:, h, :], G_R[:, :], G_E[:, 1, h, :], 0.0, ALU.mult, ALU.add)
            last.then_inc(sem("hg_cumsum"), 1)
            dve.wait_ge(sem("hg_qk"), 1)
            dve.wait_ge(sem("sec_tables"), 16)
            v.drain()

            def halves(ap, s):
                a = ap.rearrange("p h (n s) -> p (h n) s", s=2 * s)
                return a[:, :, 0:s], a[:, :, s:2 * s]

            def differences(l):
                s = HALVES[l]
                n = 4 * T // (2 * s)
                if l >= 2:
                    dve.wait_ge(sem("hg_products"), 4 * (l - 2) + 4)
                lo, up = halves(G_E[:, l % 2], s)
                blo, bup = halves(G_B[:, :, :], s)
                mid = blo[:, :, s - 1:s].to_broadcast((P, n, s))
                v.tensor_tensor(up, bup, mid, ALU.subtract)
                v.tensor_tensor(lo, mid, blo, ALU.subtract).then_inc(sem("hg_diff"), 1)

            def mixed(l):
                s = HALVES[l]
                dve.wait_ge(sem("hg_exp"), l + 1)
                lo, up = halves(G_E[:, l % 2], s)
                v.tensor_tensor(up, up, halves(G_F[:, 0:4, :], s)[1], ALU.mult)
                v.tensor_tensor(lo, lo, halves(G_F[:, 4:8, :], s)[0], ALU.mult).then_inc(sem("hg_mixed"), 1)

            def products(l):
                for h in range(4):
                    dve.wait_ge(sem("hg_products"), 4 * l + h + 1)
                    v.copy_predicated(G_A[:, h], G_M[:, l, :].unsqueeze(1).to_broadcast((P, 4, P)),
                                      PS[:, 4 + h, :].rearrange("p (t q) -> p t q", t=4)).then_inc(
                                          sem("hg_weighted"), 1)

            NL = len(HALVES)
            differences(0)
            for l in range(NL):
                if l + 1 < NL:
                    differences(l + 1)
                mixed(l)
                if l >= 1:
                    products(l - 1)
            dve.wait_ge(sem("hg_products"), 4 * (NL - 2) + 4)
            last_b = G_B[:, :, :].rearrange("p h (t s) -> p (h t) s", s=P)
            v.tensor_tensor(G_E[:, NL % 2].rearrange("p h (t s) -> p (h t) s", s=P),
                            last_b[:, :, P - 1:P].to_broadcast((P, 16, P)), last_b, ALU.subtract).then_inc(
                                sem("hg_diff"), 1)
            products(NL - 1)
            dve.sem_inc(sem("hg_buffer_free"), 1)
            dve.wait_ge(sem("hg_exp"), NL + 1)
            v.tensor_tensor(G_E[:, NL % 2], G_E[:, NL % 2], G_F[:, 4:8, :], ALU.mult).then_inc(sem("hg_mixed"), 1)
            dve.wait_ge(sem("hg_exp"), NL + 2)
            v.tensor_tensor(G_E[:, (NL + 1) % 2], G_E[:, (NL + 1) % 2], G_F[:, 0:4, :], ALU.mult).then_inc(
                sem("hg_mixed"), 1)
            products(NL)
            for h in range(4):
                dve.wait_ge(sem("hg_k_turned"), h + 1)
                v.tensor_copy(G_KT[:, h], PS[:, h, 0:3 * P].rearrange("p (t d) -> p t d", t=3)).then_inc(
                    sem("hg_kt"), 1)
            dve.wait_ge(sem("hg_lasts"), 1)
            for h in range(4):
                dve.wait_ge(sem("hg_kv"), h + 1)
                v.tensor_copy(G_S[:, h, 0, :], PS[:, h, 0:P])
                for t in range(1, 3):
                    v.drain()
                    last = v.scalar_tensor_tensor(G_S[:, h, t, :], G_S[:, h, t - 1, :], G_X[:, h, t:t + 1],
                                                  PS[:, h, P * t:P * t + P], ALU.mult, ALU.add)
                last.then_inc(sem("hg_state"), 1)
            dve.wait_ge(sem("hg_squared"), 1)
            HG = H[:, :, 0:512].rearrange("p t (h d) -> p t h d", h=4)
            v.tensor_reduce(SS[:, 0:16].rearrange("p (t h) -> p t h", t=4),
                            G_E[:, 0].rearrange("p t (h d) -> p t h d", h=4), AX.X, ALU.add)
            v.drain()
            v.tensor_scalar(SS[:, 0:16], SS[:, 0:16], 1.0 / P, RMS_EPS, ALU.mult, ALU.add).then_inc(mean_ready, 1)
            dve.wait_ge(rstd_ready, RSTDS["hgo"] + 1)
            v.tensor_tensor(HG, HG, RS[:, 0:16].rearrange("p (t h) -> p t h", t=4).unsqueeze(3).to_broadcast(
                (P, NT, 4, P)), ALU.mult)
            v.drain()
            v.tensor_tensor(H[:, :, 0:512], H[:, :, 0:512], G_N[:, :, 512:D], ALU.mult).then_inc(sem("hg_gated"), 1)
            dve.wait_ge(sem("sa_squared"), 1)
            v.tensor_reduce(SS[:, 0:32].rearrange("p (t h) -> p t h", t=4),
                            S_2[:, :, 0:512].rearrange("p t (h d) -> p t h d", d=HD), AX.X, ALU.add)
            v.tensor_reduce(SS[:, 32:48].rearrange("p (t h) -> p t h", t=4),
                            S_2[:, :, 512:768].rearrange("p t (h d) -> p t h d", d=HD), AX.X, ALU.add)
            v.tensor_reduce(SS[:, 48:56].rearrange("p (t h) -> p t h", t=2),
                            S_2[:, 0:2, 768:D].rearrange("p t (h d) -> p t h d", d=HD), AX.X, ALU.add)
            v.drain()
            v.tensor_scalar(SS[:, 0:56], SS[:, 0:56], 1.0 / HD, RMS_EPS, ALU.mult, ALU.add).then_inc(mean_ready, 1)
            dve.wait_ge(rstd_ready, RSTDS["sa"] + 1)
            for ap, a, t, h in ((S_N[:, :, 0:512], 0, 4, 8), (S_N[:, :, 768:D], 32, 4, 4), (MEMKV[:, :, 0:256], 48, 2, 4)):
                four = ap.rearrange("p t (h d) -> p t h d", d=HD)
                v.tensor_tensor(four, four, RS[:, a:a + t * h].rearrange("p (t h) -> p t h", t=t).unsqueeze(
                    3).to_broadcast((P, t, h, HD)), ALU.mult).then_inc(sem("sa_normed"), 1)
            def last_head(j, four, values):
                v.tensor_tensor(H[:, :, 512 + HD * j:512 + HD * j + HD], values, each(RSUM[:, four]),
                                ALU.mult).then_inc(o_done, 1)
            units(UNITS["sa"], 32, last_ext, S_PT, last_head)
            features("sec_y", G_HG)
            residual("sec_out", "ffn")
            features("ffn", G_FFN)
            with dve.Fori(0, BLOCKS["ffn_in"]) as i:
                for j in range(2):
                    dve.wait_ge(sem("ffn_silu"), 2 * i + j + 1)
                    if j:
                        dve.wait_ge(chunk_done, R + CH["ffn_in"] + R * i + R)
                    else:
                        dve.wait_ge(out_done, ODONE["ffn_in"] + 3 * i + 2)
                    v.tensor_tensor(FT[:, j, :], PS[:, 2 + j, :], FT[:, j, :], ALU.mult).then_inc(sem("ffn_mul"), 1)
                for j in range(2):
                    dve.wait_ge(sem("hidden_high"), 2 * i + j + 1)
                    v.tensor_tensor(FLO[:, bass.ds(2 * i + j, 1), :].rearrange("p a t -> p (a t)"), FT[:, j, :],
                                    FH[:, bass.ds(2 * i + j, 1), :].rearrange("p a t -> p (a t)").bitcast(f32),
                                    ALU.subtract).then_inc(sem("hidden_low"), 1)
            dve.sem_inc(bank_free, 4 * BLOCKS["ffn_in"])
            for i in range(2):
                for j in range(4):
                    if j == NT - 1:
                        dve.wait_ge(chunk_done, R + CH["ffn_out"] + OUT_CHUNKS * (i + 1))
                    else:
                        dve.wait_ge(sem("ffn_out_done"), 3 * i + j + 1)
                    v.tensor_tensor(X[:, j, 512 * i:512 * i + 512], PS[:, 4 * i + j, :],
                                    X[:, j, 512 * i:512 * i + 512], ALU.add).then_inc(bank_free, 1)

        @block.tensor
        def _(pe):
            mm = nc.tensor.matmul
            pe.sem_inc(chunk_done, R)
            for one in (sc_ready, t_ready, o_ready, sem("ret_used")):
                pe.sem_inc(one, CREDIT)

            def features(use, nt=NT, normed=True):
                if normed:
                    pe.wait_ge(normed_ready, NORMED[use] + nt)
                for k in range(NK):
                    if k >= 4:
                        pe.wait_ge(act_low, AT[use] + k - 3)
                    for t in range(nt):
                        last = nc.tensor.transpose(PS[:, 4 + k % 4, P * t:P * t + P], H[:, t, P * k:P * k + P],
                                                   ID[:, :])
                    last.then_inc(turned, 1)

            def three(bank, hi_l, lo_l, hi_r, lo_r, start, stop):
                mm(bank, hi_l, hi_r, start=start, stop=False, skip_group_check=True)
                mm(bank, hi_l, lo_r, start=False, stop=False, skip_group_check=True)
                return mm(bank, lo_l, hi_r, start=False, stop=stop, skip_group_check=True)

            def block_products(n0, o0, tokens, use, outs=4, order=(0, 1, 2, 3), free=None, between=None):
                for r in range(R):
                    if between:
                        between(r)
                    pe.wait_ge(act_low, AT[use] + 2 * r + 2)
                    pe.wait_ge(split_ready, n0 + r + 1)
                    for at, j in enumerate(order[:outs]):
                        if r == 0:
                            if free:
                                free(at)
                            else:
                                pe.wait_ge(bank_free, o0 + at + 1)
                        for k in range(2):
                            kt = 2 * r + k
                            s = slice(P * j, P * j + P)
                            if tokens:
                                args = (AH[:, kt, s], AL[:, kt, s], WH[:, r, k, :], WL[:, r, k, :])
                            else:
                                args = (WH[:, r, k, s], WL[:, r, k, s], AH[:, kt, :], AL[:, kt, :])
                            last = three(PS[:, j, :], *args, start=kt == 0, stop=kt == NK - 1)
                        if r == R - 1 and at < outs - 1:
                            last.then_inc(out_done, 1)
                    last.then_inc(chunk_done, 1)

            def project(name, tokens, use):
                if BLOCKS[name] == 1:
                    block_products(CH[name], OUT[name], tokens, use)
                else:
                    with pe.Fori(0, BLOCKS[name]) as i:
                        block_products(CH[name] + R * i, OUT[name] + 4 * i, tokens, use)

            def small(k, m):
                pe.wait_ge(sem("small_low"), k + 1)
                for t in range(NT):
                    for kt in range(NK):
                        s = slice(P * t, P * t + P)
                        last = three(PS[:, 4, m * t:m * t + m], AH[:, kt, s], AL[:, kt, s], SMH[:, kt, 0:m],
                                     SML[:, kt, 0:m], start=kt == 0, stop=kt == NK - 1)
                last.then_inc(sem("small_done"), 1)

            def units(at0, head0, nu, ext, probs, pt, scores, values):
                for u in range(nu + 3):
                    if u < nu:
                        pe.wait_ge(p_ready, CREDIT + at0 + u - 3)
                        scores(u, PS[:, S_BANK[u % 4], 0:ext(u)]).then_inc(sc_ready, 1)
                    if 2 <= u < nu + 2:
                        k = u - 2
                        pe.wait_ge(p_ready, CREDIT + at0 + k + 1)
                        pe.wait_ge(pt_ready, CREDIT + at0 + k - 1)
                        for t in range(ext(k) // P):
                            last = nc.tensor.transpose(PS[:, T_BANK[k % 2], P * t:P * t + P],
                                                       probs[:, k % 2, P * t:P * t + P], ID[:, :])
                        last.then_inc(t_ready, 1)
                    if u >= 3:
                        j, q = divmod(u - 3, 4)
                        pe.wait_ge(pt_ready, CREDIT + at0 + u - 2)
                        if q == 0:
                            pe.wait_ge(o_done, CREDIT + head0 + j - 1)
                        nt = ext(u - 3) // P
                        for t in range(nt):
                            last = mm(PS[:, O_BANK[j % 2], HD * q:HD * q + HD], pt[:, (u - 3) % 2, P * t:P * t + P],
                                      values(u - 3, t), start=t == 0, stop=t == nt - 1, skip_group_check=True)
                        last.then_inc(o_ready, 1)

            def attention_done(name):
                pe.wait_ge(p_ready, CREDIT + UNITS[name])
                pe.wait_ge(o_done, CREDIT + UNITS[name] // 4)

            pe.wait_ge(sem("const"), 16 * N_CONST)
            features("mem", 2)
            block_products(CH["mem"], OUT["mem"], True, "mem", 2)
            features("even")
            project("even_qk", False, "even")
            project("even_v", True, "even")
            small(0, 8)
            block_products(CH["even_z"], OUT["even_z"], True, "even")
            pe.wait_ge(sem("forget_log"), 1)
            for t in range(NT):
                last = nc.tensor.transpose(PS[0:8, 4, P * t:P * t + P], FL[:, t, :], ID[:, :])
            last.then_inc(sem("forget_turned"), 1)
            block_products(CH["even_z"] + R, OUT["even_z"] + 4, True, "even")
            wait_group(pe, "even_z")
            pe.wait_ge(sem("decay_rows"), 48)
            with pe.Fori(0, 2) as i:
                pe.wait_ge(sem("q_staged"), i + 1)

                def fox_scores(u, bank, i=i):
                    b, half, q, n = u // 8, HD * (u // 4 % 2), u % 4, P * (u % 4 + 1)
                    mm(bank, E_Q[half:half + HD, b, P * q:P * q + P],
                       E_K[half:half + HD, b, 0:n],
                       start=True, stop=False, skip_group_check=True)
                    mm(bank, MINUS3[:, :], C3[:, bass.ds(4 * i + u // 4, 1), 0:n].rearrange("p a t -> p (a t)"),
                       start=False, stop=False, skip_group_check=True)
                    return mm(bank[:, n - P:n], IDB[:, :], CAUSAL[:, :], start=False, stop=True,
                              skip_group_check=True)

                units(UNITS["fox"] + 16 * i, UNITS["fox"] // 4 + 4 * i, 16, causal_ext, E_P, E_PT, fox_scores,
                      lambda k, t, i=i: E_V[:, t, bass.ds(256 * i + HD * (k // 4), HD)])
            attention_done("odd")
            with pe.Fori(0, 2) as i:
                for b in range(2):
                    pe.wait_ge(sem("ret_k_staged"), 2 * i + b + 1)
                    for u in range(9):
                        at = 8 * (2 * i + b) + u
                        if u < 8:
                            half, k = HD * (u // 4), u % 4
                            pe.wait_ge(sem("ret_weighted"), CREDIT + at - 3)
                            mm(PS[:, S_BANK[u % 4], 0:T - P * k], E_K[half:half + HD, b, P * k:P * k + P],
                               E_Q[half:half + HD, b, P * k:T], start=True, stop=True).then_inc(sem("ret_scores"), 1)
                        if u >= 1:
                            a, k = divmod(u - 1, 4)
                            pe.wait_ge(sem("ret_weighted"), CREDIT + at)
                            if k == 0:
                                pe.wait_ge(sem("ret_taken"), CREDIT + 4 * i + 2 * b + a - 1)
                            for q in range(k, NT):
                                last = mm(PS[:, O_BANK[a], HD * q:HD * q + HD],
                                          E_P[:, (u - 1) % 2, P * (q - k):P * (q - k) + P],
                                          E_V[:, k, bass.ds(512 + 256 * i + HD * (2 * b + a), HD)],
                                          start=k == 0 and q == 0, stop=k == q, skip_group_check=True)
                            last.then_inc(sem("ret_used"), 1)
            pe.wait_ge(sem("ret_taken"), CREDIT + 8)
            features("even_y")
            project("even_out", True, "even_y")
            features("odd")

            project("odd_q", False, "odd")
            project("odd_kv", False, "odd")
            project("odd_v", True, "odd")
            small(1, 48)
            project("odd_z", True, "odd")
            pe.wait_ge(sem("gate_sum"), 1)
            for i in range(2):
                pe.wait_ge(sem("cmp_low"), i + 1)
                for r in range(R):
                    n = CH["cmp"] + R * i + r
                    pe.wait_ge(split_ready, n + 1)
                    for q in range(4):
                        l = 4 * r + q
                        for h in range(2):
                            s = slice(256 * (q % 2) + P * h, 256 * (q % 2) + P * h + P)
                            last = three(PS[:, 4 + 2 * i + h, 0:4 * CMP], WH[:, r, q // 2, s], WL[:, r, q // 2, s],
                                         CIH[:, l, :], CIL[:, l, :], start=l == 0, stop=l == 15)
                    last.then_inc(chunk_done, 1)
            pe.wait_ge(sem("odd_tables"), 16 * 11)
            pe.wait_ge(sem("cmp_hidden"), 4)
            wait_group(pe, "odd_z")
            for h in range(2):
                mm(PS[:, 0, 0:P], W2D[:, h, :, :].rearrange("p a d -> p (a d)"),
                   CHID[:, 0, h, :, :].rearrange("p g c -> p (g c)"), start=h == 0, stop=h == 1)
            for g in range(4):
                for h in range(2):
                    last = mm(PS[0:32, 1, HD * g:HD * g + HD], CHID[:, 1, h, g, :], W2[:, 1, h, :],
                              start=h == 0, stop=h == 1)
            last.then_inc(sem("cmp_kv"), 1)
            pe.wait_ge(sem("cmp_kv_taken"), 1)

            def cmp_scores(t):
                if t >= 2:
                    pe.wait_ge(sem("cmp_biased"), t - 1)
                for h in range(16):
                    half = HD * (h % 2)
                    last = mm(PS[:, t % 2 + 4 * (h % 2), 16 * h - 16 * (h % 2):16 * h - 16 * (h % 2) + 32], O_Q[half:half + HD, h // 2, P * t:P * t + P],
                              KCMP[half:half + HD, h // 4, :], start=True, stop=True, skip_group_check=True)
                last.then_inc(sem("cmp_scores"), 1)

            cmp_scores(0)
            for t in range(NT):
                if t + 1 < NT:
                    cmp_scores(t + 1)
                pe.wait_ge(sem("cmp_exp"), t + 1)
                for g in range(4):
                    last = nc.tensor.transpose(PS[:, 6, P * g:P * g + P],
                                               SC[:, 4 * g:4 * g + 4, :].rearrange("p h c -> p (h c)"), ID[:, :])
                last.then_inc(sem("cmp_turned"), 1)
                pe.wait_ge(sem("cmp_pt"), t + 1)
                if t:
                    pe.wait_ge(sem("cmp_taken"), 2 * t)
                for g in range(4):
                    last = mm(PS[:, 2 + g // 2, 256 * (g % 2):256 * (g % 2) + 256], CPT[:, g, :],
                              BDV[:, g, :, :].rearrange("p j d -> p (j d)"), start=True, stop=True,
                              skip_group_check=True)
                last.then_inc(sem("cmp_values"), 1)
            pe.wait_ge(sem("cmp_taken"), 2 * NT)
            with pe.Fori(0, 4) as i:
                pe.wait_ge(sem("q_staged"), 2 + i + 1)

                def odd_scores(u, bank, i=i):
                    b, a, q = u // 16, u // 4 % 4, u % 4
                    half, n = HD * (a % 2), P * (q + 1)
                    mm(bank, O_QS[half:half + HD, a // 2, P * q:P * q + P],
                       O_KS[half:half + HD, b, 0:n],
                       start=True, stop=False, skip_group_check=True)
                    mm(bank, ALS[:, bass.ds(4 * i + a, 1), :].rearrange("p a q -> p (a q)"),
                       ALJ[:, T - P - P * q:T - P - P * q + n], start=False, stop=False, skip_group_check=True)
                    return mm(bank[:, n - P:n], IDB[:, :], CAUSAL[:, :], start=False, stop=True,
                              skip_group_check=True)

                units(UNITS["odd"] + 32 * i, UNITS["odd"] // 4 + 8 * i, 32, causal_ext, O_P, O_PT, odd_scores,
                      lambda k, t, i=i: O_V[:, t, bass.ds(256 * (k // 16) + HD * i, HD)])
            attention_done("sa")
            features("odd_y")
            project("odd_out", True, "odd_y")

            features("sec")
            project("sa_i", False, "sec")
            small(2, 72)
            pe.wait_ge(sem("index_kw"), 1)
            for t in range(NT):
                last = nc.tensor.transpose(PS[:, 5, P * t:P * t + P], I_KN[:, t, :], ID[:, :])
            last.then_inc(sem("index_k_turned"), 1)
            pe.wait_ge(sem("index_k"), 1)

            def index_scores(c):
                for n in range(3 * c, 3 * c + 3):
                    t, h = n // 8 + 1, n % 8
                    half = HD * (h % 2)
                    if n >= 4:
                        pe.wait_ge(sem("index_relu"), n - 3)
                    mm(PS[:, 4 + n % 4, 0:P * t + P], I_Q[half:half + HD, h // 2, P * t:P * t + P],
                       I_K[half:half + HD, 0:P * t + P], start=True, stop=True).then_inc(sem("index_ready"), 1)

            for i in range(2):
                block_products(CH["sa_n"] + R * i, OUT["sa_n"] + 4 * i, True, "sec",
                               between=lambda r, i=i: index_scores(R * i + r))
            project("hg_f", False, "sec")
            project("hg_n", True, "sec")
            pe.wait_ge(sem("index_relu"), 24)
            wait_group(pe, "hg_n")
            NL = len(HALVES)
            for l in range(NL + 1):
                if l < NL:
                    pe.wait_ge(sem("hg_mixed"), l + 1)
                for h in range(4):
                    if l:
                        pe.wait_ge(sem("hg_weighted"), 4 * (l - 1) + h + 1)
                    for t in range(NT):
                        s = slice(P * t, P * t + P)
                        lhs, rhs = (G_E[:, l % 2, h, s],) * 2 if l < NL else (G_F[:, 4 + h, s], G_F[:, h, s])
                        last = mm(PS[:, 4 + h, s], lhs, rhs, start=True, stop=True, skip_group_check=True)
                    last.then_inc(sem("hg_products"), 1)
            pe.wait_ge(sem("hg_mixed"), NL + 1)
            for h in range(4):
                for t in range(3):
                    last = nc.tensor.transpose(PS[:, h, P * t:P * t + P], G_E[:, NL % 2, h, P * t:P * t + P],
                                               ID[:, :])
                last.then_inc(sem("hg_k_turned"), 1)
            for h in range(4):
                pe.wait_ge(sem("hg_kt"), h + 1)
                for t in range(3):
                    last = mm(PS[:, h, P * t:P * t + P], G_KT[:, h, t, :], G_N[:, t, P * h:P * h + P],
                              start=True, stop=True, skip_group_check=True)
                last.then_inc(sem("hg_kv"), 1)
            pe.wait_ge(sem("hg_weighted"), 4 * (NL + 1))
            pe.wait_ge(sem("hg_mixed"), NL + 2)
            for h in range(4):
                pe.wait_ge(sem("hg_state"), h + 1)
                for t in range(NT):
                    s = slice(P * t, P * t + P)
                    last = mm(PS[:, 4 + h, s], G_A[:, h, t, :], G_N[:, t, P * h:P * h + P],
                              start=True, stop=t == 0, skip_group_check=True)
                    if t:
                        last = mm(PS[:, 4 + h, s], G_E[:, (NL + 1) % 2, h, s], G_S[:, h, t - 1, :],
                                  start=False, stop=True, skip_group_check=True)
                last.then_inc(sem("hg_out"), 1)
            pe.wait_ge(sem("sa_normed"), 3)
            for k in range(8):
                which, pair = divmod(k, 2)
                if k >= 4:
                    pe.wait_ge(sem("sa_features"), k - 3)
                for t in range(2 if which == 3 else NT):
                    src = MEMKV[:, t, P * pair:P * pair + P] if which == 3 else \
                        S_N[:, t, (0, 256, 768)[which] + P * pair:(0, 256, 768)[which] + P * pair + P]
                    last = nc.tensor.transpose(PS[:, 4 + k % 4, P * t:P * t + P], src, ID[:, :])
                last.then_inc(sem("sa_turned"), 1)
            pe.wait_ge(sem("sa_features"), 8)
            pe.wait_ge(sem("selected"), 3)
            def last_scores(u, bank):
                half, b, q = HD * (u // 4 % 2), u // 8 % 2, u % 4
                if u >= 16:
                    return mm(bank, M_Q[half:half + HD, b, P * q:P * q + P], M_K[half:half + HD, b, :],
                              start=True, stop=True)
                n = causal_ext(u)
                mm(bank, S_QK[half:half + HD, b, P * q:P * q + P], S_QK[half:half + HD, 2 + b, 0:n],
                   start=True, stop=False, skip_group_check=True)
                return mm(bank, IDB[:, :], SEL[:, q, 0:n], start=False, stop=True, skip_group_check=True)

            def last_values(u, t):
                col = HD * (u // 4 % 4)
                return MEMKV[:, t, 256 + col:256 + col + HD] if u >= 16 else S_N[:, t, 512 + col:512 + col + HD]

            units(UNITS["sa"], UNITS["sa"] // 4, 32, last_ext, S_P, S_PT, last_scores, last_values)
            attention_done("end")
            pe.wait_ge(sem("hg_gated"), 1)
            features("sec_y", normed=False)
            project("sec_out", True, "sec_y")
            features("ffn")
            with pe.Fori(0, BLOCKS["ffn_in"]) as i:
                def free(at, i=i):
                    if at % 2 == 0:
                        pe.wait_ge(sem("ffn_mul"), 2 * i + at // 2 + 1)
                block_products(CH["ffn_in"] + R * i, 0, False, "ffn", 4, FFN_ORDER, free)
            for i in range(2):
                if i == 0:
                    pe.wait_ge(sem("hidden_low"), NF)
                    wait_group(pe, "ffn_in")
                for r in range(OUT_CHUNKS):
                    n = CH["ffn_out"] + OUT_CHUNKS * i + r
                    pe.wait_ge(split_ready, n + 1)
                    for t in range(NT):
                        s = slice(P * t, P * t + P)
                        for k in range(2):
                            kt = 2 * r + k
                            last = three(PS[:, 4 * i + t, :], FH[:, kt, s], FLO[:, kt, s], WH[:, n % R, k, :],
                                         WL[:, n % R, k, :], start=kt == 0, stop=kt == NF - 1)
                        if t == NT - 1:
                            last.then_inc(chunk_done, 1)
                        elif r == OUT_CHUNKS - 1:
                            last.then_inc(sem("ffn_out_done"), 1)


def tables():
    bf = np.dtype("bfloat16")
    i = np.arange(P)
    c = {"identity": np.eye(P, dtype=np.float32)}
    c["identity_bf16"] = c["identity"].astype(bf)
    c["causal_f32"] = np.where(i[None, :] <= i[:, None], 0.0, NEG).astype(np.float32)
    c["causal_bf16"] = c["causal_f32"].astype(bf)
    c["minus_one3"] = np.full((3, P), -1.0, np.float32).astype(bf)
    lg = np.log(1.0 - 2.0 ** (-5.0 - np.arange(8)))
    diff = np.arange(T)[None, :] - i[:, None]
    dec = np.where(diff[None] >= 0, np.exp(lg[:, None, None] * np.maximum(diff, 0)[None]), 0.0)
    c["retention"] = np.ascontiguousarray(dec.transpose(1, 0, 2)).astype(np.float32)
    slopes = (2.0 ** (-8.0 * (np.arange(16) + 1) / 16)).astype(np.float32)
    parts, rest = [], slopes.copy()
    for _ in range(3):
        parts.append(rest.astype(bf))
        rest = rest - parts[-1].astype(np.float32)
    j = np.arange(T) - (T - P)
    places = [j // 16 * 16, j % 16]
    c["alibi_slopes"] = np.zeros((P, 16, P), bf)
    c["alibi_positions"] = np.zeros((P, T), bf)
    for a in range(3):
        for b in range(2):
            c["alibi_slopes"][2 * a + b] = np.broadcast_to(parts[a][:, None], (16, P))
            c["alibi_positions"][2 * a + b] = places[b].astype(np.float32).astype(bf)
    t = np.arange(T).reshape(NT, P).T
    end = np.arange(32) * 16 + 31
    gap = t[:, :, None] - end[None, None, :]
    bias = -8.0 * slopes[None, None, :, None] * gap[:, :, None, :].astype(np.float32)
    ok = (gap >= 0) & (np.arange(32) < CMP)
    c["cmp_bias"] = np.where(ok[:, :, None, :], bias, NEG).astype(np.float32)
    masks = []
    for s in HALVES:
        k, q = i[:, None], i[None, :]
        masks.append((k // (2 * s) == q // (2 * s)) & (k % (2 * s) < s) & (q % (2 * s) >= s))
    masks.append(np.eye(P, dtype=bool))
    c["tree_masks"] = np.ascontiguousarray(np.stack(masks, 1)).astype(np.uint32)
    c["scan_reset"] = np.broadcast_to((np.arange(T) % P != 0).astype(np.float32), (P, T)).copy()
    return c


INPUTS = ["x", "even_norm_g", "even_w_in", "even_b_f", "even_gn_g", "even_w_out", "odd_norm_g", "odd_w_in",
          "odd_b_gate", "odd_pe_k", "odd_pe_v", "odd_wk1", "odd_wk2", "odd_wv1", "odd_wv2", "odd_w_out", "final_g",
          "mem_2", "w_in_2", "w_out_2", "w_mem_kv_2", "lb_logits_2", "norm_mix_2", "norm_mem_2", "norm_ffn_2",
          "hg_out_gain_2", "sa_q_gain_2", "sa_k_gain_2", "mem_q_gain_2", "mem_k_gain_2", "w_ffn_in_2",
          "w_ffn_out_2"]


def kernel(**inputs):
    import concourse.bacc as bacc
    from concourse.bass_utils import run_bass_kernel_spmd

    nc = bacc.Bacc("TRN2", target_bir_lowering=False, num_devices=1)
    arrays, w, c = {}, {}, {}
    for name in INPUTS:
        a = np.ascontiguousarray(inputs[name])
        arrays[f"in_{name}"] = a
        w[name] = nc.dram_tensor(f"in_{name}", a.shape, mybir.dt.from_np(a.dtype), kind="ExternalInput").ap()
    for name, a in tables().items():
        arrays[f"table_{name}"] = a
        c[name] = nc.dram_tensor(f"table_{name}", a.shape, mybir.dt.from_np(a.dtype), kind="ExternalInput").ap()
    out = nc.dram_tensor("out", (1, T, D), f32, kind="ExternalOutput").ap()
    program(nc, w, c, out)
    r = run_bass_kernel_spmd(nc, [arrays], core_ids=[0])
    return r.results[0]["out"]
```

```python
from contextlib import ExitStack

import numpy as np
import concourse.bass as bass
from concourse import mybir

f32 = mybir.dt.float32
f32r = mybir.dt.float32r
bf16 = mybir.dt.bfloat16
u32 = mybir.dt.uint32
ALU = mybir.AluOpType
ACT = mybir.ActivationFunctionType
AX = mybir.AxisListType

P = 128
T = 512
NT = T // P
D = 1024
NK = D // P
HD = 64
R = 4
FF = 2816
NF = FF // P
NEG = -1e30
TAKEN = -3e38
RMS_EPS = 1e-6
GN_EPS = 1e-5
CMP = 31
CREDIT = 16
HALVES = [64, 32, 16, 8, 4, 2, 1]
BANKS = (0, 1, 4, 5), (6, 7), (2, 3)
FEW_BANKS = (0, 1), (2,), (3,)
S_BANK, T_BANK, O_BANK = BANKS
FFN_ORDER = (0, 2, 1, 3)

STREAM = [("mem", 1, 4), ("even_qk", 4, 4), ("even_v", 2, 4), ("even_z", 2, 4), ("even_out", 2, 4),
          ("odd_q", 2, 4), ("odd_kv", 2, 4), ("odd_v", 1, 4), ("odd_z", 2, 4), ("cmp", 2, 0), ("odd_out", 2, 4),
          ("sa_i", 1, 4), ("sa_n", 2, 4), ("hg_f", 2, 4), ("hg_n", 2, 4), ("sec_out", 2, 4), ("ffn_in", 11, 4)]
BLOCKS = {name: n for name, n, _ in STREAM}
CH, OUT, ODONE = {}, {}, {}
_c = _o = _d = 0
for _name, _blocks, _outs in STREAM:
    CH[_name], OUT[_name], ODONE[_name] = _c, _o, _d
    _c, _o, _d = _c + R * _blocks, _o + _outs * _blocks, _d + (1 if _name == "mem" else max(_outs - 1, 0)) * _blocks
CH["ffn_out"], OUT["ffn_out"], ODONE["ffn_out"] = _c, _o, _d
OUT_CHUNKS = NF // 2
UNITS = {"fox": 0, "odd": 32, "sa": 160, "mem": 176, "end": 192}

FEATURES = ("mem", "even", "even_y", "odd", "odd_y", "sec", "sec_y", "ffn")
SQUARES = {"mem": 0, "even": 2, "odd": 6, "fin": 10, "sec": 14, "ffn": 18}
NORMED = {"mem": 0, "even": 2, "even_y": 6, "odd": 10, "odd_y": 14, "sec": 18, "ffn": 22}
RSTDS = {"mem": 0, "even": 2, "gn": 6, "odd": 10, "fin": 14, "sec": 18, "sa": 22, "hgo": 23, "ffn": 27}
AT = {name: NK * i for i, name in enumerate(FEATURES)}

GAINS = [("norm_mem_2", 0), ("even_norm_g", 0), ("even_gn_g", 4), ("odd_norm_g", 0), ("norm_mix_2", 0),
         ("norm_ffn_2", 0)]
G_MEM, G_EVEN, G_GN, G_ODD, G_SEC, G_FFN, G_HG = range(7)
HEAD_GAINS = ["sa_q_gain_2", "sa_k_gain_2", "mem_q_gain_2", "mem_k_gain_2"]
N_CONST = 3 + len(GAINS) - 2 + 1 + 2 * len(HEAD_GAINS)


W_RET, W_FOX, W_GN, W_ODD, W_ODDY, W_HG, W_HGO = 5, 3, 3, 2, 4, 5, 1
W_PAIRS, W_CMP, W_NORMS, W_RES = 1, 2, 4, 1


def causal_ext(u):
    return P * (u % 4 + 1)


def last_ext(u):
    return causal_ext(u) if u < 16 else 2 * P


def program(nc, w, c, out):
    ctx = ExitStack()
    with ctx:
        def sb(on, name, shape, dt=f32):
            return on.enter_context(nc.sbuf_tensor(name, shape, dt))

        made = {}

        def sem(name):
            if name not in made:
                made[name] = ctx.enter_context(nc.semaphore(name))
            return made[name]

        X = sb(ctx, "x_tokens", [P, NT, D])
        RAW = sb(ctx, "weight_raw", [P, R, 2, 512])
        WH = sb(ctx, "weight_high", [P, R, 2, 512], f32r)
        WL = sb(ctx, "weight_low", [P, R, 2, 512], f32r)
        lay_m = ExitStack()
        SMR = sb(lay_m, "small_raw", [P, NK, 72])
        SMH = sb(lay_m, "small_high", [P, NK, 72], f32r)
        SML = sb(lay_m, "small_low", [P, NK, 72], f32r)
        lay_m.close()
        M_Q = sb(ctx, "mem_q", [P, 2, T])
        M_K = sb(ctx, "mem_k", [P, 2, 2 * P])
        sb(ctx, "small_rest", [P, 3 * NK * 72 - 6 * 2 * P])
        ID = sb(ctx, "identity", [P, P])
        IDB = sb(ctx, "identity_bf16", [P, P], bf16)
        CAUSAL = sb(ctx, "causal_bf16", [P, P], bf16)
        ZERO = sb(ctx, "zero_bf16", [P, T], bf16)
        MINUS3 = sb(ctx, "minus_ones_bf16", [3, P], bf16)
        HALF = sb(ctx, "minus_half", [P, 64])
        SS = sb(ctx, "mean_squares", [P, 64])
        RS = sb(ctx, "rstd", [P, 64])
        NMAX = sb(ctx, "minus_max", [P, 4])
        SUM = sb(ctx, "sums", [P, 8])
        RSUM = sb(ctx, "one_over_sum", [P, 8])
        SCL = sb(ctx, "gate_over_sum", [P, 8])
        GAIN = sb(ctx, "gains", [P, 12, NK])
        MEMKV = sb(ctx, "mem_k_v", [P, 2, 512])

        lay = ExitStack()
        AH = sb(lay, "act_high", [P, NK, T], f32r)
        AL = sb(lay, "act_low", [P, NK, T], f32r)
        H = sb(lay, "h_tokens", [P, NT, D])
        lay_e = ExitStack()
        E_UT = sb(lay_e, "even_qk", [P, 16, T])
        E_V = sb(lay_e, "even_v", [P, NT, D])
        E_Z = sb(lay_e, "even_silu_z", [P, NT, D])
        FL = sb(lay_e, "forget_tokens", [P, NT, 8])
        FL2 = sb(lay_e, "forget_abs", [P, NT, 8])
        BF = sb(lay_e, "forget_bias", [P, 8])
        FB = sb(lay_e, "forget_parts", [8, 3, T], bf16)
        FC = sb(lay_e, "forget_cumsum", [8, T])
        FO = sb(lay_e, "forget_ones", [8, T])
        C3 = sb(lay_e, "decay_rows", [3, 8, T], bf16)
        lay_e.close()
        lay_f = ExitStack()
        FING = sb(lay_f, "final_gain", [P, D])
        lay_f.close()
        lay_o = ExitStack()
        O_Q = sb(lay_o, "odd_q", [P, 8, T])
        O_K = sb(lay_o, "odd_k", [P, 2, 4, T])
        O_V = sb(lay_o, "odd_v", [P, NT, 512])
        O_Z = sb(lay_o, "odd_silu_z", [P, NT, D])
        lay_b = ExitStack()
        KCVC = sb(lay_b, "kc_vc", [P, 4, T])
        lay_b.close()
        CB = sb(lay_o, "cmp_bias", [P, NT, 16, 32])
        ALS = sb(lay_o, "alibi_slopes", [P, 16, P], bf16)
        ALJ = sb(lay_o, "alibi_positions", [P, T], bf16)
        GATE = sb(lay_o, "gates", [P, NT, 48])
        BG = sb(lay_o, "gate_bias", [P, 48])
        PE2 = sb(lay_o, "cmp_pe", [P, 2, 16])
        W2 = sb(lay_o, "cmp_w2", [P, 2, 2, HD])
        W2D = sb(lay_o, "cmp_w2_twice", [P, 2, 2, HD])
        CHID = sb(lay_o, "cmp_hidden", [P, 2, 2, 4, 32])
        lay_o.close()
        lay_s = ExitStack()
        S_N = sb(lay_s, "sa_q_k_v_mq", [P, NT, D])
        lay_i = ExitStack()
        I_Q = sb(lay_i, "index_q", [P, 4, T])
        I_K = sb(lay_i, "index_k", [P, T])
        lay_i.close()
        S_QK = sb(lay_s, "sa_q_k", [P, 4, T])
        G_R = sb(lay_s, "scan_reset", [P, T])
        I_W = sb(lay_s, "index_w", [P, NT, 8])
        SEL = sb(lay_s, "sel_mask", [P, NT, T], bf16)
        lay_g = ExitStack()
        G_F = sb(lay_g, "hg_q_f", [P, 8, T])
        G_N = sb(lay_g, "hg_i_g", [P, NT, D])
        G_B = sb(lay_g, "hg_cumsum", [P, 4, T])
        lay_l = ExitStack()
        G_L = sb(lay_l, "hg_log_forget", [P, 4, T])
        lay_l.close()
        G_M = sb(lay_g, "hg_masks", [P, 8, P], u32)
        G_S = sb(lay_g, "hg_state", [P, 4, 3, P])
        G_X = sb(lay_g, "hg_last", [P, 4, NT])
        lay_g.close()
        lay_s.close()
        lay.close()
        ov = ExitStack()
        ovr = ExitStack()
        E_Q = sb(ovr, "even_q_stage", [P, 2, T])
        E_K = sb(ovr, "even_k_stage", [P, 2, T])
        ovr.close()
        F_Q = [sb(ov, f"fox_q_{part}", [P, 2, T], f32r) for part in ("high", "low")]
        F_K = [sb(ov, f"fox_k_{part}", [P, 2, T], f32r) for part in ("high", "low")]
        E_P = sb(ov, "even_probs", [P, 2, T])
        E_PT = sb(ov, "even_probs_t", [P, 2, T])
        RD = sb(ov, "retention_decay", [P, 2, 2, T])
        ov.close()
        ovc = ExitStack()
        CIH = [sb(ovc, f"cmp_in_high{i}", [P, 16, 4 * CMP], f32r) for i in range(2)]
        CIL = [sb(ovc, f"cmp_in_low{i}", [P, 16, 4 * CMP], f32r) for i in range(2)]
        ovc.close()
        ovc = ExitStack()
        sb(ovc, "cmp_key_inputs", [P, 16 * 4 * CMP])
        KCMP = sb(ovc, "k_cmp_blocks", [P, 4, 2, 32])
        BDV = sb(ovc, "v_cmp_blocks", [P, 4, 4, HD])
        ovc.close()
        ovd = ExitStack()
        SC = sb(ovd, "cmp_scores", [P, 2, 16, 32])
        CPT = sb(ovd, "cmp_probs_t", [P, 4, P])
        CMX = sb(ovd, "cmp_max", [P, NT, 4, 16])
        ovd.close()
        ovo = ExitStack()
        O_QS = [sb(ovo, f"odd_q_{part}", [P, 2, T], f32r) for part in ("high", "low")]
        O_KS = [sb(ovo, f"odd_k_{part}", [P, 2, T], f32r) for part in ("high", "low")]
        O_P = sb(ovo, "odd_probs", [P, 2, T])
        O_PT = sb(ovo, "odd_probs_t", [P, 2, T])
        O_T = sb(ovo, "odd_head_out", [P, 2, 4, HD])
        ovo.close()
        ovg = ExitStack()
        G_E = sb(ovg, "hg_decay", [P, 2, 4, T])
        G_A = sb(ovg, "hg_weights", [P, 4, 4, P])
        G_KT = sb(ovg, "hg_key_tokens", [P, 4, 3, P])
        ovg.close()
        ovq = ExitStack()
        sb(ovq, "act_remains", [P, 2 * NK * T])
        CI = [sb(ovq, f"cmp_in{i}", [P, 16, 4, CMP]) for i in range(2)]
        ovq.close()
        ovq = ExitStack()
        sb(ovq, "act_is_there", [P, 2 * NK * T])
        HT = sb(ovq, "cmp_hidden_rows", [4 * CMP, 2, 256])
        ovq.close()
        ovh = ExitStack()
        sb(ovh, "act_stays", [P, 2 * NK * T])
        I_KN = sb(ovh, "index_k_tokens", [P, NT, P])
        RL = sb(ovh, "index_relu", [P, 2, T])
        SCO = sb(ovh, "index_scores", [P, 3, T])
        MX8 = sb(ovh, "max8", [P, 8])
        MASKF = sb(ovh, "causal_f32", [P, P])
        ovh.close()
        S_P, S_PT = H[:, 0:2, 0:T], H[:, 2:4, 0:T]
        ffn = ExitStack()
        sb(ffn, "act_still_there", [P, 2 * NK * T])
        FH = sb(ffn, "ffn_high", [P, NF, T], f32r)
        FLO = sb(ffn, "ffn_low", [P, NF, T], f32r)
        FT = sb(ffn, "ffn_silu", [P, 2, T])
        ffn.close()

        PS = ctx.enter_context(nc.psum_tensor("psum", [P, 8, 512], f32))

        raw_ready = [sem(f"raw_ready{i}") for i in range(R)]
        high_ready = sem("high_ready")
        split_ready = sem("split_ready")
        chunk_done = sem("chunk_done")
        out_done = sem("out_done")
        bank_free = sem("bank_free")
        squares_ready = sem("squares_ready")
        mean_ready = sem("mean_ready")
        rstd_ready = sem("rstd_ready")
        normed_ready = sem("normed_ready")
        turned = sem("turned")
        act_high = sem("act_high")
        act_low = sem("act_low")
        sc_ready = sem("scores_ready")
        mx_ready = sem("max_ready")
        p_ready = sem("probs_ready")
        t_ready = sem("transposed_ready")
        pt_ready = sem("probs_t_ready")
        o_ready = sem("values_ready")
        o_done = sem("output_taken")

        def wait_out(eng, name, i, k, last):
            outs = 2 if name == "mem" else 4
            if last:
                eng.wait_ge(chunk_done, R + CH[name] + R * i + R)
            else:
                eng.wait_ge(out_done, ODONE[name] + (outs - 1) * i + k + 1)

        def wait_group(eng, name):
            eng.wait_ge(bank_free, 4 + OUT[name] + BLOCKS[name] * 4)

        block = ctx.enter_context(nc.Block())

        @block.sync
        def _(sp):
            sp.dma_start(H[:, 0:2, :], w["mem_2"][0].rearrange("(t p) d -> p t d", p=P)).then_inc(sem("mem_loaded"), 16)
            sp.dma_start(ID[:, :], c["identity"]).then_inc(sem("first_const"), 16)

            def chunk(n, parts):
                if n >= R:
                    sp.wait_ge(split_ready, n - R + 1)
                for at, src in parts:
                    sp.dma_start(RAW[:, n % R, :, at:at + src.shape[1]],
                                 src.rearrange("(k p) n -> p k n", p=P)).then_inc(
                                     raw_ready[n % R], 32 // len(parts))

            def load_block(n, mat, parts):
                for r in range(R):
                    chunk(n + r, [(at, mat[256 * r:256 * r + 256, a:a + m]) for at, a, m in parts])

            def small(k, mat, a, m):
                if k:
                    sp.wait_ge(sem("small_done"), k)
                sp.dma_start(SMR[:, :, 0:m], mat[:, a:a + m].rearrange("(k p) n -> p k n", p=P)).then_inc(
                    sem("small_loaded"), 16)

            load_block(CH["mem"], w["w_mem_kv_2"][0], [(0, 0, 512)])
            sp.dma_start(X[:, :, :], w["x"][0].rearrange("(t p) d -> p t d", p=P)).then_inc(sem("x_loaded"), 16)
            we = w["even_w_in"][0]
            small(0, we, 1536, 8)
            for i, a in enumerate((0, 512, 1544, 2056)):
                load_block(CH["even_qk"] + R * i, we, [(0, a, 512)])
            for i, a in enumerate((1024, 2568)):
                load_block(CH["even_v"] + R * i, we, [(0, a, 512)])
            for i in range(2):
                load_block(CH["even_z"] + R * i, we, [(0, 3080 + 512 * i, 512)])
            for i in range(2):
                load_block(CH["even_out"] + R * i, w["even_w_out"][0], [(0, 512 * i, 512)])
            wo = w["odd_w_in"][0]
            small(1, wo, 2560, 48)
            for i in range(2):
                load_block(CH["odd_q"] + R * i, wo, [(0, 512 * i, 512)])
            load_block(CH["odd_kv"], wo, [(0, 1024, 512)])
            load_block(CH["odd_kv"] + R, wo, [(0, 1536, 256), (256, 2048, 256)])
            load_block(CH["odd_v"], wo, [(0, 1792, 256), (256, 2304, 256)])
            for i in range(2):
                load_block(CH["odd_z"] + R * i, wo, [(0, 2608 + 512 * i, 512)])
            for i, name in enumerate(("odd_wk1", "odd_wv1")):
                for r in range(R):
                    n = CH["cmp"] + R * i + r
                    sp.wait_ge(split_ready, n - R + 1)
                    sp.dma_start(RAW[:, n % R, :, :].rearrange("p a (b n) -> p (a b) n", b=2),
                                 w[name][0][512 * r:512 * r + 512, :].rearrange("(k p) n -> p k n", p=P)).then_inc(
                                     raw_ready[n % R], 32)
            for i in range(2):
                load_block(CH["odd_out"] + R * i, w["odd_w_out"][0], [(0, 512 * i, 512)])
            w2 = w["w_in_2"][0]
            small(2, w2, 3328, 72)
            load_block(CH["sa_i"], w2, [(0, 2816, 512)])
            load_block(CH["sa_n"], w2, [(0, 2048, 512)])
            load_block(CH["sa_n"] + R, w2, [(0, 2560, 256), (256, 3400, 256)])
            for i in range(2):
                load_block(CH["hg_f"] + R * i, w2, [(0, 512 * i, 512)])
            for i in range(2):
                load_block(CH["hg_n"] + R * i, w2, [(0, 1024 + 512 * i, 512)])
            for i in range(2):
                load_block(CH["sec_out"] + R * i, w["w_out_2"][0], [(0, 512 * i, 512)])
            for i in range(BLOCKS["ffn_in"]):
                load_block(CH["ffn_in"] + R * i, w["w_ffn_in_2"][0], [(0, 256 * i, 256), (256, FF + 256 * i, 256)])
            for i in range(2):
                for r in range(OUT_CHUNKS):
                    chunk(CH["ffn_out"] + OUT_CHUNKS * i + r,
                          [(0, w["w_ffn_out_2"][0][256 * r:256 * r + 256, 512 * i:512 * i + 512])])
            for i in range(2):
                sp.wait_ge(bank_free, 4 + OUT["ffn_out"] + 4 * (i + 1))
                sp.dma_start(out[0].rearrange("(t p) d -> p t d", p=P)[:, :, 512 * i:512 * i + 512],
                             X[:, :, 512 * i:512 * i + 512]).then_inc(sem("stored"), 16)
            sp.wait_ge(sem("stored"), 32)

        @block.gpsimd
        def _(pool):
            def load(dst, src, name):
                pool.dma_start(dst, src).then_inc(sem(name), 16)

            def split(n0, blocks, slots=range(R)):
                def body(i):
                    for r in slots:
                        pool.wait_ge(high_ready, n0 + R * i + r + 1)
                        nc.gpsimd.tensor_tensor(WL[:, r], RAW[:, r], WH[:, r].bitcast(f32),
                                                ALU.subtract).then_inc(split_ready, 1)
                if blocks == 1:
                    body(0)
                else:
                    with pool.Fori(0, blocks) as i:
                        body(i)

            def split_ahead(name):
                split(CH[name] + R, BLOCKS[name])

            def split_around_norm(name, use):
                split(CH[name] + R, 1)
                split(CH[name] + 2 * R, 1, range(R - 1))
                rstd(use, 1, NT)
                if use == "fin":
                    rstd("sec", 1, NT)
                split(CH[name] + 2 * R, 1, range(R - 1, R))

            def small_split(k, m):
                pool.wait_ge(sem("small_high"), k + 1)
                nc.gpsimd.tensor_tensor(SML[:, :, 0:m], SMR[:, :, 0:m], SMH[:, :, 0:m].bitcast(f32),
                                        ALU.subtract).then_inc(sem("small_low"), 1)

            def rstd(use, n, tiles=1):
                for t in range(tiles):
                    pool.wait_ge(mean_ready, RSTDS[use] + t + 1)
                    nc.gpsimd.tensor_tensor(RS[:, n * t:n * t + n], SS[:, n * t:n * t + n], HALF[:, 0:n],
                                            ALU.pow).then_inc(rstd_ready, 1)

            pool.sem_inc(sem("head_added"), 2)
            nc.gpsimd.memset(ZERO[:, :], 0.0).then_inc(sem("zero_ready"), 1)
            nc.gpsimd.memset(HALF[:, :], -0.5)
            nc.gpsimd.memset(GAIN[:, G_GN, 0:4], 1.0)
            nc.gpsimd.memset(GAIN[:, G_HG, 4:8], 1.0).then_inc(sem("half_ready"), 1)
            pool.wait_ge(sem("half_ready"), 1)
            rstd("mem", 1, 2)
            split(0, 1)
            rstd("even", 1, NT)
            split_ahead("mem")
            small_split(0, 8)
            load(IDB[:, :], c["identity_bf16"], "const")
            load(CAUSAL[:, :], c["causal_bf16"], "const")
            load(MINUS3[:, :], c["minus_one3"], "const")
            with nc.allow_non_contiguous_dma(reason="gain vectors, once"):
                for i, (name, first) in list(enumerate(GAINS))[2:]:
                    load(GAIN[:, i, first:NK], w[name][0].rearrange("(k p) -> p k", p=P), "const")
                load(GAIN[:, G_HG, 0:1], w["hg_out_gain_2"][0].rearrange("(d o) -> d o", o=1), "const")
                for i, name in enumerate(HEAD_GAINS):
                    for half in range(2):
                        load(GAIN[HD * half:HD * half + HD, 8 + i, 0:1],
                             w[name][0].rearrange("(d o) -> d o", o=1), "const")
            load(BF[:, :], w["even_b_f"][0:1, :].to_broadcast((P, 8)), "forget_bias")
            split_ahead("even_qk")
            split_ahead("even_v")
            split_ahead("even_z")
            pool.wait_ge(chunk_done, R + CH["even_out"])
            with pool.Fori(0, 2) as i:
                for b in range(2):
                    pool.wait_ge(sem("ret_used"), CREDIT + 8 * (2 * i + b) - 8)
                    load(RD[:, b], c["retention"][:, bass.ds(4 * i + 2 * b, 2), :], f"ret_decay{b}")
            pool.wait_ge(sem("forget_parts"), 1)
            for i in range(3):
                load(C3[i:i + 1, :, :], FB[:, i, :], "decay_rows")
            rstd("gn", 8, NT)
            split_around_norm("even_out", "odd")
            wait_group(pool, "even_out")
            load(ALS[:, :, :], c["alibi_slopes"], "odd_tables")
            load(ALJ[:, :], c["alibi_positions"], "odd_tables")
            load(BG[:, :], w["odd_b_gate"][0:1, :].to_broadcast((P, 48)), "odd_tables")
            with nc.allow_non_contiguous_dma(reason="position vectors, once"):
                for i, name in enumerate(("odd_pe_k", "odd_pe_v")):
                    for l in range(2):
                        load(PE2[HD * l:HD * l + HD, i, :],
                             w[name][0].rearrange("(a l) d -> d l a", l=2)[:, l, :], "odd_tables")
            for i, name in enumerate(("odd_wk2", "odd_wv2")):
                load(W2[:, i, :, :], w[name][0].rearrange("(k p) d -> p k d", p=P), "odd_tables")
            for k in range(2):
                load(W2D[:, :, k, :], w["odd_wk2"][0].rearrange("(k p) d -> p k d", p=P), "odd_tables")
            nc.gpsimd.memset(CHID[:, :, :, :, :], 0.0).then_inc(sem("cmp_hidden_zero"), 1)
            split_ahead("odd_q")
            small_split(1, 48)
            split_ahead("odd_kv")
            split_ahead("odd_v")
            split_ahead("odd_z")
            pool.wait_ge(sem("cmp_in"), 2)
            load(CB[:, :, :, :], c["cmp_bias"], "cmp_bias")
            split_ahead("cmp")
            with pool.Fori(0, 4) as i:
                for j in range(8):
                    pool.wait_ge(o_done, CREDIT + (UNITS["odd"] // 4) + 8 * i + j + 1)
                    pool.sem_inc(sem("head_seen"), 1)
                    cols = bass.ds(256 * i + HD * (j % 4), HD)
                    nc.gpsimd.tensor_tensor(H[:, :, cols], H[:, :, cols], O_T[:, j % 2], ALU.add).then_inc(
                        sem("head_added"), 1)
            pool.wait_ge(o_ready, CREDIT + UNITS["sa"])
            load(FING[:, :], w["final_g"].rearrange("(o d) -> o d", o=1).to_broadcast((P, D)), "final_gain")
            split_around_norm("odd_out", "fin")
            small_split(2, 72)
            pool.wait_ge(turned, AT["sec"] + NK)
            load(MASKF[:, :], c["causal_f32"], "sa_tables")
            split_ahead("sa_i")
            split_ahead("sa_n")
            pool.wait_ge(sem("index_relu"), 24)
            load(G_R[:, :], c["scan_reset"], "scan_reset")
            split(CH["hg_f"] + R, 1)
            rstd("sa", 56)
            split(CH["hg_f"] + 2 * R, 1)
            split(CH["hg_n"] + R, 1)
            pool.wait_ge(sem("hg_cumsum"), 1)
            load(G_M[:, :, :], c["tree_masks"], "sec_tables")
            split(CH["hg_n"] + 2 * R, 1)
            pool.wait_ge(chunk_done, R + CH["sec_out"])
            nc.gpsimd.memset(G_A[:, :, :, :], 0.0).then_inc(sem("hg_zero"), 1)
            for h in range(4):
                pool.wait_ge(mean_ready, RSTDS["hgo"] + h + 1)
                nc.gpsimd.tensor_tensor(RS[:, 4 * h:4 * h + 4], SS[:, 4 * h:4 * h + 4], HALF[:, 0:4],
                                        ALU.pow).then_inc(rstd_ready, 1)
            split_around_norm("sec_out", "ffn")
            split_ahead("ffn_in")
            split(CH["ffn_out"] + R, 4)
            for r in range(2):
                pool.wait_ge(high_ready, CH["ffn_out"] + 5 * R + r + 1)
                nc.gpsimd.tensor_tensor(WL[:, r], RAW[:, r], WH[:, r].bitcast(f32),
                                        ALU.subtract).then_inc(split_ready, 1)

        @block.scalar
        def _(act):
            act.sem_inc(p_ready, CREDIT)
            act.sem_inc(sem("ret_taken"), CREDIT)

            def split(n0, blocks, slots=range(R)):
                def body(i):
                    for r in slots:
                        act.wait_ge(raw_ready[r], 32 * (n0 // R + i + 1))
                        act.wait_ge(chunk_done, n0 + R * i + r + 1)
                        nc.scalar.activation(WH[:, r], RAW[:, r], ACT.Copy).then_inc(high_ready, 1)
                if blocks == 1:
                    body(0)
                else:
                    with act.Fori(0, blocks) as i:
                        body(i)

            def split_ahead(name):
                split(CH[name] + R, BLOCKS[name])

            def small_split(k, m):
                act.wait_ge(sem("small_loaded"), 16 * (k + 1))
                nc.scalar.activation(SMH[:, :, 0:m], SMR[:, :, 0:m], ACT.Copy).then_inc(sem("small_high"), 1)

            def split_around_norm(name, use):
                split(CH[name] + R, 1)
                split(CH[name] + 2 * R, 1, range(R - 1))
                squares(use, X, H, after=(bank_free, 4 + OUT[name] + 4))
                if use == "fin":
                    squares("sec", X, H, after=(sem("fin_x"), 0))
                split(CH[name] + 2 * R, 1, range(R - 1, R))

            def squares(use, src, dst, nt=NT, after=None):
                for t in range(nt):
                    if after:
                        act.wait_ge(after[0], after[1] + t + 1)
                    nc.scalar.activation(dst[:, t, :], src[:, t, :], ACT.Square,
                                         accum_out=SS[:, t:t + 1]).then_inc(squares_ready, 1)

            def features(use, gain, nt=NT):
                for k in range(NK):
                    act.wait_ge(turned, AT[use] + k + 1)
                    g = 0 if gain == G_HG and k < 4 else k
                    scale = 1.0 if gain is None else GAIN[:, gain, g:g + 1]
                    nc.scalar.activation(AH[:, k, 0:P * nt], PS[:, 4 + k % 4, 0:P * nt],
                                         ACT.Identity, scale=scale).then_inc(act_high, 1)

            def exps(at0, steps, ext, probs, banks=S_BANK):
                for u in steps:
                    act.wait_ge(mx_ready, CREDIT + at0 + u + 1)
                    act.wait_ge(t_ready, CREDIT + at0 + u - 1)
                    n = ext(u)
                    nc.scalar.activation(probs[:, u % 2, 0:n], PS[:, banks[u % len(banks)], 0:n], ACT.Exp,
                                         bias=NMAX[:, u % 4:u % 4 + 1],
                                         accum_out=SUM[:, u % 8:u % 8 + 1]).then_inc(p_ready, 1)

            def high(block, i, r):
                act.wait_ge(raw_ready[r], 32 * (block + i + 1))
                act.wait_ge(chunk_done, R * block + R * i + r + 1)
                nc.scalar.activation(WH[:, r], RAW[:, r], ACT.Copy).then_inc(high_ready, 1)

            def split_and_take(name, i, dst, between=None, func=ACT.Copy):
                for r in range(R):
                    if between:
                        between(R * i + r)
                    if r == R - 1:
                        for j in range(3):
                            wait_out(act, name, i, j, False)
                            nc.scalar.activation(dst[:, j, :], PS[:, j, :], func).then_inc(bank_free, 1)
                    high(CH[name] // R + 1, i, r)
                wait_out(act, name, i, 3, True)
                nc.scalar.activation(dst[:, 3, :], PS[:, 3, :], func).then_inc(bank_free, 1)

            def sa_squares(c):
                heads = [(S_N, t, HD * h) for t in range(NT) for h in range(8)]
                heads += [(S_N, t, 768 + HD * h) for t in range(NT) for h in range(4)]
                heads += [(MEMKV, t, HD * h) for t in range(2) for h in range(4)]
                nc.scalar.drain()
                for n in range(14 * c, 14 * c + 14):
                    src, t, a = heads[n]
                    last = nc.scalar.activation(RL[:, n % 2, HD * (n % 14 // 2):HD * (n % 14 // 2) + HD], src[:, t, a:a + HD], ACT.Square,
                                                accum_out=SS[:, n:n + 1])
                last.then_inc(sem("sa_squared"), 1)

            def sa_feature(k):
                act.wait_ge(sem("sa_turned"), k + 1)
                which, pair = divmod(k, 2)
                dst = (S_QK[:, pair, :], S_QK[:, 2 + pair, :], M_Q[:, pair, :], M_K[:, pair, :])[which]
                nc.scalar.activation(dst, PS[:, 4 + k % 4, 0:2 * P if which == 3 else T], ACT.Identity,
                                     scale=GAIN[:, 8 + which, 0:1]).then_inc(sem("sa_features"), 1)

            def relus(c):
                for n in range(3 * c, 3 * c + 3):
                    act.wait_ge(sem("index_ready"), n + 1)
                    if n >= 2:
                        act.wait_ge(sem("index_added"), n - 1)
                    k = P * (n // 8 + 2)
                    nc.scalar.activation(RL[:, n % 2, 0:k], PS[:, 4 + n % 4, 0:k], ACT.Relu).then_inc(
                        sem("index_relu"), 1)

            with nc.allow_non_contiguous_dma(reason="gain vectors, once"):
                for i, (name, first) in list(enumerate(GAINS))[:2]:
                    act.dma_start(GAIN[:, i, :], w[name][0].rearrange("(k p) -> p k", p=P)).then_inc(
                        sem("first_const"), 16)
            act.wait_ge(sem("mem_loaded"), 16)
            squares("mem", H, H[:, 2:4, :], 2)
            split(0, 1)
            act.wait_ge(sem("first_const"), 16 * 3)
            features("mem", G_MEM, 2)
            act.wait_ge(sem("x_loaded"), 16)
            squares("even", X, H)
            split_ahead("mem")
            small_split(0, 8)
            features("even", G_EVEN)
            split_ahead("even_qk")
            split_ahead("even_v")
            act.wait_ge(sem("forget_abs"), 1)
            nc.scalar.activation(FL2[:, :, :], FL2[:, :, :], ACT.Exp, scale=-1.0)
            nc.scalar.drain()
            nc.scalar.activation(FL2[:, :, :], FL2[:, :, :], ACT.Ln, bias=1.0).then_inc(sem("forget_ln"), 1)
            for i in range(2):
                split_and_take("even_z", i, E_Z[:, :, 512 * i:512 * i + 512], func=ACT.Silu)
            with act.Fori(0, 2) as i:
                act.wait_ge(sem("ret_used"), CREDIT + 16 * i)
                nc.scalar.activation(E_Q[:, :, :], E_UT[:, bass.ds(8 + 2 * i, 2), :], ACT.Copy)
                nc.scalar.activation(E_K[:, :, :], E_UT[:, bass.ds(12 + 2 * i, 2), :], ACT.Copy,
                                     scale=0.125).then_inc(sem("ret_k_staged"), 1)
                for a in range(4):
                    act.wait_ge(sem("ret_used"), CREDIT + 16 * i + 4 * a + 4)
                    nc.scalar.activation(H[:, :, bass.ds(512 + 256 * i + HD * a, HD)],
                                         PS[:, O_BANK[a % 2], 0:4 * HD].rearrange("p (t d) -> p t d", t=4),
                                         ACT.Copy).then_inc(sem("ret_taken"), 1)
            with act.Fori(0, 2) as i:
                at0 = UNITS["fox"] + 16 * i
                act.wait_ge(sc_ready, CREDIT + at0)
                nc.scalar.activation(F_K[0][:, :, :], E_UT[:, bass.ds(4 + 2 * i, 2), :], ACT.Copy)
                nc.scalar.activation(F_Q[0][:, :, :], E_UT[:, bass.ds(2 * i, 2), :], ACT.Copy,
                                     scale=0.125).then_inc(sem("q_high"), 1)
                exps(at0, range(8), causal_ext, E_P)
                for n in range(2):
                    act.wait_ge(sem("gn_centered"), 2 * i + n + 1)
                    act.sem_inc(sem("gn_seen"), 1)
                    nc.scalar.activation(E_UT[:, bass.ds(8 + 2 * i + n, 1), :], H[:, bass.ds(2 * i + n, 1), 512:D],
                                         ACT.Square).then_inc(sem("gn_squared"), 1)
                exps(at0, range(8, 16), causal_ext, E_P)
            features("even_y", G_GN)
            split_around_norm("even_out", "odd")
            features("odd", G_ODD)
            split_ahead("odd_q")
            small_split(1, 48)
            split_ahead("odd_kv")
            split_ahead("odd_v")
            act.wait_ge(sem("gate_sum"), 1)
            nc.scalar.activation(GATE[:, :, :], GATE[:, :, :], ACT.Sigmoid).then_inc(sem("gates"), 1)
            for i in range(2):
                split_and_take("odd_z", i, O_Z[:, :, 512 * i:512 * i + 512], func=ACT.Silu)
            act.wait_ge(chunk_done, R + CH["cmp"])
            for i in range(2):
                act.wait_ge(sem("cmp_in"), i + 1)
                nc.scalar.activation(CIH[i][:, :, :], CI[i][:, :, :, :].rearrange("p l g c -> p l (g c)"),
                                     ACT.Copy).then_inc(sem("cmp_high"), 1)
            for i in range(2):
                split(CH["cmp"] + R + R * i, 1)
                act.wait_ge(chunk_done, R + CH["cmp"] + R * i + R)
                nc.scalar.activation(HT[:, i, :], PS[0:4 * CMP, 4 + i, 0:256], ACT.Silu).then_inc(
                    sem("cmp_silu"), 1)
            act.wait_ge(sem("cmp_hidden_zero"), 1)
            for i in range(2):
                act.wait_ge(sem("cmp_hidden_turned"), i + 1)
                for h in range(2):
                    nc.scalar.activation(CHID[:, i, h, :, 0:CMP],
                                         PS[:, 6 + i, P * h:P * h + 4 * CMP].rearrange("p (g c) -> p g c", g=4),
                                         ACT.Copy).then_inc(sem("cmp_hidden"), 1)
            for t in range(NT):
                act.wait_ge(sem("cmp_shifted"), t + 1)
                nc.scalar.activation(SC[:, t % 2], SC[:, t % 2], ACT.Exp, scale=0.125).then_inc(sem("cmp_exp"), 1)
            act.wait_ge(sem("cmp_taken"), 2 * NT)
            with act.Fori(0, 4) as i:
                at0 = UNITS["odd"] + 32 * i
                act.wait_ge(sc_ready, CREDIT + at0)
                act.sem_inc(sem("q_stage_free"), 1)
                nc.scalar.activation(O_KS[0][:, :, :].unsqueeze(2), O_K[:, :, bass.ds(i, 1), :], ACT.Copy)
                nc.scalar.activation(O_QS[0][:, :, :], O_Q[:, bass.ds(2 * i, 2), :], ACT.Copy,
                                     scale=0.125).then_inc(sem("q_high"), 1)
                exps(at0, range(32), causal_ext, O_P)
            features("odd_y", None)
            split_around_norm("odd_out", "fin")
            features("sec", G_SEC)
            small_split(2, 72)
            split_ahead("sa_i")
            for i in range(2):
                split_and_take("sa_n", i, S_N[:, :, 512 * i:512 * i + 512], relus)
            act.wait_ge(sem("index_added"), 24)
            for i in range(2):
                split_and_take("hg_f", i, G_F[:, 4 * i:4 * i + 4, :], sa_squares if i == 0 else None)
            act.wait_ge(sem("hg_abs"), 1)
            nc.scalar.activation(G_B[:, :, :], G_B[:, :, :], ACT.Exp, scale=-1.0)
            nc.scalar.drain()
            nc.scalar.activation(G_B[:, :, :], G_B[:, :, :], ACT.Ln, bias=1.0).then_inc(sem("hg_ln"), 1)
            act.wait_ge(sem("hg_logf"), 1)
            nc.scalar.activation(G_F[:, 4:8, :], G_F[:, 4:8, :], ACT.Sigmoid, scale=-1.0)
            nc.scalar.activation(G_F[:, 0:4, :], G_F[:, 0:4, :], ACT.Silu).then_inc(sem("hg_qk"), 1)
            for i in range(2):
                split_and_take("hg_n", i, G_N[:, :, 512 * i:512 * i + 512], sa_feature, (ACT.Copy, ACT.Silu)[i])
            NL = len(HALVES)

            def hg_exp(e):
                if e <= NL:
                    act.wait_ge(sem("hg_diff"), e + 1)
                else:
                    act.wait_ge(sem("hg_buffer_free"), 1)
                nc.scalar.activation(G_E[:, e % 2], G_E[:, e % 2] if e <= NL else G_B[:, :, :],
                                     ACT.Exp).then_inc(sem("hg_exp"), 1)

            hg_exp(0)
            nc.scalar.activation(G_X[:, :, :], G_B[:, :, P - 1::P], ACT.Exp).then_inc(sem("hg_lasts"), 1)
            for l in range(NL + 1):
                exps(UNITS["sa"], range(4 * l, 4 * l + 1), last_ext, S_P, FEW_BANKS[0])
                hg_exp(l + 1)
                exps(UNITS["sa"], range(4 * l + 1, 4 * l + 4), last_ext, S_P, FEW_BANKS[0])
            for h in range(4):
                act.wait_ge(sem("hg_out"), h + 1)
                for t in range(NT):
                    last = nc.scalar.activation(G_E[:, 0, h, P * t:P * t + P], PS[:, 4 + h, P * t:P * t + P],
                                                ACT.Square, accum_out=SS[:, 4 * h + t:4 * h + t + 1])
                last.then_inc(sem("hg_squared"), 1)
            features("sec_y", G_HG)
            split_around_norm("sec_out", "ffn")
            features("ffn", G_FFN)
            with act.Fori(0, BLOCKS["ffn_in"]) as i:
                def high(r, i=i):
                    act.wait_ge(raw_ready[r], 32 * ((CH["ffn_in"] + R) // R + i + 1))
                    act.wait_ge(chunk_done, CH["ffn_in"] + R + R * i + r + 1)
                    nc.scalar.activation(WH[:, r], RAW[:, r], ACT.Copy).then_inc(high_ready, 1)
                for r in range(R - 1):
                    high(r)
                for j in range(2):
                    act.wait_ge(out_done, ODONE["ffn_in"] + 3 * i + 2 * j + 1)
                    act.wait_ge(sem("hidden_low"), 2 * i)
                    nc.scalar.activation(FT[:, j, :], PS[:, j, :], ACT.Silu).then_inc(sem("ffn_silu"), 1)
                for j in range(2):
                    if j:
                        high(R - 1)
                    act.wait_ge(sem("ffn_mul"), 2 + 2 * i + j + 1)
                    nc.scalar.activation(FH[:, bass.ds(2 * i + j, 1), :].rearrange("p a t -> p (a t)"),
                                         FT[:, j, :], ACT.Copy).then_inc(sem("hidden_high"), 1)
            split(CH["ffn_out"] + R, 4)
            for r in range(2):
                n = CH["ffn_out"] + 5 * R + r
                act.wait_ge(raw_ready[r], 32 * (n // R + 1))
                act.wait_ge(chunk_done, n + 1)
                nc.scalar.activation(WH[:, r], RAW[:, r], ACT.Copy).then_inc(high_ready, 1)

        @block.vector
        def _(dve):
            v = nc.vector
            dve.sem_inc(bank_free, 4)
            dve.sem_inc(sem("ffn_mul"), 2)
            for one in (mx_ready, pt_ready, o_done, sem("ret_weighted")):
                dve.sem_inc(one, CREDIT)

            def norm(use, src, nt=NT):
                for t in range(nt + 1):
                    if t < nt:
                        mean(use, t)
                    if t:
                        scale(use, t - 1, src)

            def mean(use, t):
                dve.wait_ge(squares_ready, SQUARES[use] + t + 1)
                v.tensor_scalar(SS[:, t:t + 1], SS[:, t:t + 1], 1.0 / D, RMS_EPS, ALU.mult, ALU.add).then_inc(
                    mean_ready, 1)

            def scale(use, t, src=X):
                dve.wait_ge(rstd_ready, RSTDS[use] + t + 1)
                if use == "fin":
                    v.scalar_tensor_tensor(X[:, t, :], X[:, t, :], RS[:, t:t + 1], FING[:, :], ALU.mult,
                                           ALU.mult).then_inc(sem("fin_x"), 1)
                else:
                    v.tensor_scalar(H[:, t, :], src[:, t, :], RS[:, t:t + 1], None, ALU.mult).then_inc(
                        normed_ready, 1)

            def features(use, gain, nt=NT):
                for k in range(NK):
                    dve.wait_ge(act_high, AT[use] + k + 1)
                    g = 0 if gain == G_HG and k < 4 else k
                    scale = 1.0 if gain is None else GAIN[:, gain, g:g + 1]
                    v.scalar_tensor_tensor(AL[:, k, 0:P * nt], PS[:, 4 + k % 4, 0:P * nt], scale,
                                           AH[:, k, 0:P * nt].bitcast(f32), ALU.mult, ALU.subtract).then_inc(act_low, 1)

            def take(name, dst, loop=True):
                def body(i):
                    for j in range(4):
                        wait_out(dve, name, i, j, j == 3)
                        v.tensor_copy(dst(i, j), PS[:, j, :]).then_inc(bank_free, 1)
                if BLOCKS[name] == 1 or not loop:
                    for i in range(BLOCKS[name]):
                        body(i)
                else:
                    with dve.Fori(0, BLOCKS[name]) as i:
                        body(i)

            def residual(name, use):
                for i in range(2):
                    for j in range(4):
                        wait_out(dve, name, i, j, j == 3)
                        v.tensor_tensor(X[:, j, 512 * i:512 * i + 512], PS[:, j, :],
                                        X[:, j, 512 * i:512 * i + 512], ALU.add).then_inc(bank_free, 1)
                        if i and j >= 1:
                            mean(use, j - 1)
                        if i and j >= 2:
                            scale(use, j - 2)
                mean(use, 3)
                scale(use, 2)
                scale(use, 3)

            def units(at0, nu, ext, pt, take_head, banks=BANKS, steps=None, beside=None):
                S, TR, O = banks
                for u in steps or range(nu + 4):
                    if u < nu:
                        dve.wait_ge(sc_ready, CREDIT + at0 + u + 1)
                        v.tensor_reduce(NMAX[:, u % 4:u % 4 + 1], PS[:, S[u % len(S)], 0:ext(u)], AX.X, ALU.max,
                                        negate=True).then_inc(mx_ready, 1)
                    if 2 <= u < nu + 2:
                        k = u - 2
                        dve.wait_ge(t_ready, CREDIT + at0 + k + 1)
                        dve.wait_ge(o_ready, CREDIT + at0 + k - 1)
                        v.tensor_copy(pt[:, k % 2, 0:ext(k)], PS[:, TR[k % len(TR)], 0:ext(k)]).then_inc(pt_ready, 1)
                    if u >= 7 and u % 4 == 3:
                        j = (u - 7) // 4
                        dve.wait_ge(o_ready, CREDIT + at0 + 4 * j + 4)
                        four = slice(4 * (j % 2), 4 * (j % 2) + 4)
                        v.reciprocal(RSUM[:, four], SUM[:, four])
                        v.drain()
                        take_head(j, four, PS[:, O[j % len(O)], 0:4 * HD].rearrange("p (q d) -> p q d", q=4))
                    if beside:
                        beside(u)

            def low_parts(n, k_parts, k, q_parts, q):
                dve.wait_ge(sem("q_high"), n)
                v.tensor_tensor(k_parts[1][:, :, :], k, k_parts[0][:, :, :].bitcast(f32), ALU.subtract)
                v.scalar_tensor_tensor(q_parts[1][:, :, :], q, 0.125, q_parts[0][:, :, :].bitcast(f32), ALU.mult,
                                       ALU.subtract).then_inc(sem("q_staged"), 1)

            def each(cols):
                return cols.unsqueeze(2).to_broadcast((P, 4, HD))

            dve.wait_ge(sem("first_const"), 16 * 3)
            norm("mem", H, 2)
            features("mem", G_MEM, 2)
            norm("even", X)
            for j in range(2):
                wait_out(dve, "mem", 0, j, j == 1)
                v.tensor_copy(MEMKV[:, j, :], PS[:, j, :]).then_inc(bank_free, (1, 3)[j])
            features("even", G_EVEN)
            take("even_qk", lambda i, j: E_UT[:, bass.ds(4 * i + j, 1), :].rearrange("p a t -> p (a t)"))
            take("even_v", lambda i, j: E_V[:, j, bass.ds(512 * i, 512)])
            dve.wait_ge(sem("const"), 16 * N_CONST)
            for k in (8, 10):
                v.tensor_scalar(GAIN[:, k, 0:1], GAIN[:, k, 0:1], 0.125, None, ALU.mult)
            dve.wait_ge(sem("small_done"), 1)
            dve.wait_ge(sem("forget_bias"), 16)
            v.tensor_tensor(FL[:, :, :], PS[:, 4, 0:4 * 8].rearrange("p (t h) -> p t h", t=4),
                            BF[:, :].unsqueeze(1).to_broadcast((P, NT, 8)), ALU.add)
            v.drain()
            v.scalar_tensor_tensor(FL2[:, :, :], FL[:, :, :], -1.0, FL[:, :, :], ALU.mult, ALU.max).then_inc(sem("forget_abs"), 1)
            dve.wait_ge(sem("forget_ln"), 1)
            v.scalar_tensor_tensor(FL[:, :, :], FL[:, :, :], 0.0, FL2[:, :, :], ALU.min, ALU.subtract).then_inc(
                sem("forget_log"), 1)
            dve.wait_ge(sem("forget_turned"), 1)
            v.memset(FO[:, :], 1.0)
            v.drain()
            v.tensor_tensor_scan(FC[:, :], FO[:, :], PS[0:8, 4, :], 0.0, ALU.mult, ALU.add)
            v.drain()
            v.tensor_copy(FB[:, 0, :], FC[:, :])
            v.drain()
            v.tensor_tensor(FO[:, :], FC[:, :], FB[:, 0, :], ALU.subtract)
            v.drain()
            v.tensor_copy(FB[:, 1, :], FO[:, :])
            v.drain()
            v.tensor_tensor(FC[:, :], FO[:, :], FB[:, 1, :], ALU.subtract)
            v.drain()
            v.tensor_copy(FB[:, 2, :], FC[:, :]).then_inc(sem("forget_parts"), 1)

            with dve.Fori(0, 2) as i:
                for b in range(2):
                    dve.wait_ge(sem(f"ret_decay{b}"), 16 * (i + 1))
                    for u in range(8):
                        at = 8 * (2 * i + b) + u
                        n = T - P * (u % 4)
                        dve.wait_ge(sem("ret_scores"), at + 1)
                        dve.wait_ge(sem("ret_used"), CREDIT + at - 1)
                        v.tensor_tensor(E_P[:, u % 2, 0:n], PS[:, S_BANK[u % 4], 0:n], RD[:, b, u // 4, 0:n],
                                        ALU.mult).then_inc(sem("ret_weighted"), 1)
            dve.wait_ge(sem("ret_taken"), CREDIT + 8)
            with dve.Fori(0, 2) as i:
                low_parts(i + 1, F_K, E_UT[:, bass.ds(4 + 2 * i, 2), :], F_Q, E_UT[:, bass.ds(2 * i, 2), :])

                def fox_head(j, four, values, i=i):
                    v.tensor_tensor(H[:, :, bass.ds(256 * i + HD * j, HD)], values, each(RSUM[:, four]),
                                    ALU.mult).then_inc(o_done, 1)
                def group_norm(u, i=i):
                    if u not in (2, 3, 4, 5, 9, 10, 14, 15):
                        return
                    n = {2: 0, 3: 1, 4: 0, 5: 1, 9: 0, 10: 1, 14: 0, 15: 1}[u]
                    t = 2 * i + n
                    rows = H[:, bass.ds(t, 1), 512:D].rearrange("p a (h d) -> p (a h) d", d=HD)
                    mean = SS[:, bass.ds(8 * t, 8)]
                    if u < 4:
                        v.tensor_reduce(mean, rows, AX.X, ALU.add)
                        v.drain()
                        v.tensor_scalar(mean, mean, 1.0 / HD, None, ALU.mult)
                        v.drain()
                    elif u < 6:
                        v.tensor_tensor(rows, rows, mean.unsqueeze(2).to_broadcast((P, 8, HD)),
                                        ALU.subtract).then_inc(sem("gn_centered"), 1)
                    elif u < 11:
                        dve.wait_ge(sem("gn_squared"), t + 1)
                        v.tensor_reduce(mean, E_UT[:, bass.ds(8 + t, 1), :].rearrange("p a (h d) -> p (a h) d", d=HD),
                                        AX.X, ALU.add)
                        v.drain()
                        v.tensor_scalar(mean, mean, 1.0 / HD, GN_EPS, ALU.mult, ALU.add).then_inc(mean_ready, 1)
                    else:
                        dve.wait_ge(rstd_ready, RSTDS["gn"] + t + 1)
                        v.tensor_tensor(rows, rows, RS[:, bass.ds(8 * t, 8)].unsqueeze(2).to_broadcast((P, 8, HD)),
                                        ALU.mult)

                units(UNITS["fox"] + 16 * i, 16, causal_ext, E_PT, fox_head, beside=group_norm)
            v.drain()
            for t in range(NT):
                v.tensor_tensor(H[:, t, :], H[:, t, :], E_Z[:, t, :], ALU.mult).then_inc(normed_ready, 1)
            features("even_y", G_GN)
            residual("even_out", "odd")
            features("odd", G_ODD)

            take("odd_q", lambda i, j: O_Q[:, bass.ds(4 * i + j, 1), :].rearrange("p a t -> p (a t)"))
            for j in range(4):
                wait_out(dve, "odd_kv", 0, j, j == 3)
                v.tensor_copy(KCVC[:, j, :], PS[:, j, :]).then_inc(bank_free, 1)
            for j in range(4):
                wait_out(dve, "odd_kv", 1, j, j == 3)
                for gg in range(2):
                    for half in range(2):
                        last = v.tensor_copy(O_K[HD * half:HD * half + HD, j // 2, 2 * (j % 2) + gg, :],
                                             PS[HD * gg:HD * gg + HD, j, :])
                last.then_inc(bank_free, 1)
            take("odd_v", lambda i, j: O_V[:, j, :])
            dve.wait_ge(sem("odd_tables"), 16 * 11)
            dve.wait_ge(sem("small_done"), 2)
            v.tensor_tensor(GATE[:, :, :], PS[:, 4, 0:4 * 48].rearrange("p (t h) -> p t h", t=4),
                            BG[:, :].unsqueeze(1).to_broadcast((P, NT, 48)), ALU.add).then_inc(sem("gate_sum"), 1)
            for i in range(2):
                for l in range(2):
                    for g in range(4):
                        src = KCVC[HD * (g % 2):HD * (g % 2) + HD, 2 * i + g // 2, :]
                        lo = src[:, l:l + 480].rearrange("p (c a r) -> p a c r", c=30, r=2)[:, :, :, 0]
                        v.tensor_copy(CI[i][HD * l:HD * l + HD, 0:8, g, 0:30], lo)
                        hi = src[:, 16 + l:16 + l + 480].rearrange("p (c a r) -> p a c r", c=30, r=2)[:, :, :, 0] \
                            if l == 0 else src[:, 17:497].rearrange("p (c a r) -> p a c r", c=30, r=2)[:, :, :, 0]
                        v.tensor_copy(CI[i][HD * l:HD * l + HD, 8:16, g, 0:30], hi)
                        v.tensor_copy(CI[i][HD * l:HD * l + HD, :, g, 30], src[:, 480 + l:512:2])
                v.drain()
                v.tensor_tensor(CI[i][:, :, :, :], CI[i][:, :, :, :],
                                PE2[:, i, :].unsqueeze(2).unsqueeze(3).to_broadcast((P, 16, 4, CMP)),
                                ALU.add).then_inc(sem("cmp_in"), 1)
            for i in range(2):
                dve.wait_ge(sem("cmp_high"), i + 1)
                v.tensor_tensor(CIL[i][:, :, :], CI[i][:, :, :, :].rearrange("p l g c -> p l (g c)"),
                                CIH[i][:, :, :].bitcast(f32), ALU.subtract).then_inc(sem("cmp_low"), 1)
            dve.wait_ge(chunk_done, R + CH["cmp"] + 2 * R)
            v.memset(BDV[:, :, :, :], 0.0)
            v.memset(KCMP[:, :, :, :], 0.0)
            v.drain()
            dve.wait_ge(sem("cmp_kv"), 1)
            for half in range(2):
                rows = slice(HD * half, HD * half + HD)
                v.tensor_copy(KCMP[rows, :, half, :], PS[rows, 0, 0:P].rearrange("p (g c) -> p g c", g=4))
            v.drain()
            for j in range(4):
                last = v.tensor_copy(BDV[32 * j:32 * j + 32, :, j, :],
                                     PS[0:32, 1, 0:256].rearrange("p (g d) -> p g d", g=4))
            last.then_inc(sem("cmp_kv_taken"), 1)
            dve.wait_ge(sem("gates"), 1)
            dve.wait_ge(sem("cmp_bias"), 16)
            for step in range(NT + 2):
                t = step
                if t < NT:
                    if t >= 2:
                        dve.wait_ge(sem("cmp_turned"), t - 1)
                    dve.wait_ge(sem("cmp_scores"), t + 1)
                    v.tensor_tensor(SC[:, t % 2], PS[:, 4 + t % 2, :].rearrange("p (h c) -> p h c", h=16),
                                    CB[:, t], ALU.add).then_inc(sem("cmp_biased"), 1)
                    v.drain()
                    v.tensor_reduce(CMX[:, t, 0, :], SC[:, t % 2], AX.X, ALU.max)
                    v.drain()
                    v.tensor_scalar(CMX[:, t, 0, :], CMX[:, t, 0, :], NEG / 10, None, ALU.max)
                    v.drain()
                    v.tensor_tensor(SC[:, t % 2], SC[:, t % 2], CMX[:, t, 0, :].unsqueeze(2).to_broadcast(
                        (P, 16, 32)), ALU.subtract).then_inc(sem("cmp_shifted"), 1)
                t = step - 1
                if 0 <= t < NT:
                    dve.wait_ge(sem("cmp_exp"), t + 1)
                    v.tensor_reduce(CMX[:, t, 1, :], SC[:, t % 2], AX.X, ALU.add)
                    dve.wait_ge(sem("cmp_turned"), t + 1)
                    if t:
                        dve.wait_ge(sem("cmp_values"), t)
                    v.tensor_copy(CPT[:, :, :], PS[:, 6 + t % 2, :].rearrange("p (g q) -> p g q", g=4)).then_inc(
                        sem("cmp_pt"), 1)
                    v.drain()
                    v.tensor_scalar(CMX[:, t, 1, :], CMX[:, t, 1, :], 1e-30, None, ALU.max)
                    v.drain()
                    v.reciprocal(CMX[:, t, 2, :], CMX[:, t, 1, :])
                    v.drain()
                    v.tensor_tensor(CMX[:, t, 3, :], CMX[:, t, 2, :], GATE[:, t, 0:48:3], ALU.mult)
                t = step - 2
                if t >= 0:
                    dve.wait_ge(sem("cmp_values"), t + 1)
                    for k in range(2):
                        v.tensor_tensor(H[:, t, 512 * k:512 * k + 512].rearrange("p (h d) -> p h d", h=8),
                                        PS[:, 2 + k, :].rearrange("p (h d) -> p h d", h=8),
                                        CMX[:, t, 3, 8 * k:8 * k + 8].unsqueeze(2).to_broadcast((P, 8, HD)),
                                        ALU.mult).then_inc(sem("cmp_taken"), 1)
            with dve.Fori(0, 4) as i:
                low_parts(2 + i + 1, O_KS, O_K[:, :, bass.ds(i, 1), :].rearrange("p b a t -> p (b a) t"), O_QS,
                          O_Q[:, bass.ds(2 * i, 2), :])

                def odd_head(j, four, values, i=i):
                    b, a = divmod(j, 4)
                    v.tensor_tensor(SCL[:, four].unsqueeze(2), RSUM[:, four].unsqueeze(2),
                                    GATE[:, :, bass.ds(12 * i + 3 * a + 1 + b, 1)], ALU.mult)
                    v.drain()
                    dve.wait_ge(sem("head_added"), 8 * i + j + 1)
                    v.tensor_tensor(O_T[:, j % 2], values, each(SCL[:, four]), ALU.mult).then_inc(o_done, 1)
                units(UNITS["odd"] + 32 * i, 32, causal_ext, O_PT, odd_head)
            dve.wait_ge(sem("head_added"), 2 + 32)
            for t in range(NT):
                v.tensor_tensor(H[:, t, :], H[:, t, :], O_Z[:, t, :], ALU.mult).then_inc(normed_ready, 1)
            features("odd_y", None)
            dve.wait_ge(sem("final_gain"), 16)
            residual("odd_out", "fin")

            norm("sec", X)
            features("sec", G_SEC)
            take("sa_i", lambda i, j: I_Q[:, j, :])
            dve.wait_ge(sem("small_done"), 3)
            small = PS[:, 4, 0:4 * 72].rearrange("p (t n) -> p t n", t=4)
            v.tensor_copy(I_KN[:, :, 0:HD], small[:, :, 0:HD])
            v.tensor_copy(I_KN[:, :, HD:P], small[:, :, 0:HD])
            v.tensor_scalar(I_W[:, :, :], small[:, :, HD:72], 8 ** -0.5 * 64 ** -0.5, None, ALU.mult).then_inc(
                sem("index_kw"), 1)
            dve.wait_ge(sem("index_k_turned"), 1)
            v.tensor_copy(I_K[:, :], PS[:, 5, :]).then_inc(sem("index_k"), 1)
            v.tensor_copy(SEL[:, 0, 0:P], CAUSAL[:, :])
            dve.wait_ge(sem("sa_tables"), 16)
            for n in range(24):
                t, h = n // 8, n % 8
                k = P * (t + 2)
                dve.wait_ge(sem("index_relu"), n + 1)
                one, rl = I_W[:, t + 1, h:h + 1], RL[:, n % 2, 0:k]
                if h == 0:
                    v.tensor_scalar(SCO[:, t, 0:k], rl, one, None, ALU.mult).then_inc(sem("index_added"), 1)
                else:
                    v.scalar_tensor_tensor(SCO[:, t, 0:k], rl, one, SCO[:, t, 0:k], ALU.mult, ALU.add).then_inc(
                        sem("index_added"), 1)
                v.drain()

            def top(t):
                s = SCO[:, t, 0:P * (t + 2)]
                v.tensor_tensor(s[:, P * (t + 1):], s[:, P * (t + 1):], MASKF[:, :], ALU.add)
                v.drain()
                for k in range(16):
                    v.max(MX8[:, :], s)
                    v.drain()
                    v.match_replace(s, MX8[:, :], s, TAKEN)
                    v.drain()
                v.tensor_scalar(SEL[:, t + 1, 0:P * (t + 2)], s, TAKEN / 2, NEG, ALU.is_gt, ALU.mult).then_inc(
                    sem("selected"), 1)

            top(0)
            dve.wait_ge(sem("sa_squared"), 4)
            v.tensor_scalar(SS[:, 0:56], SS[:, 0:56], 1.0 / HD, RMS_EPS, ALU.mult, ALU.add).then_inc(mean_ready, 1)
            top(1)
            dve.wait_ge(rstd_ready, RSTDS["sa"] + 1)
            for ap, a, t, h in ((S_N[:, :, 0:512], 0, 4, 8), (S_N[:, :, 768:D], 32, 4, 4), (MEMKV[:, :, 0:256], 48, 2, 4)):
                four = ap.rearrange("p t (h d) -> p t h d", d=HD)
                v.tensor_tensor(four, four, RS[:, a:a + t * h].rearrange("p (t h) -> p t h", t=t).unsqueeze(
                    3).to_broadcast((P, t, h, HD)), ALU.mult).then_inc(sem("sa_normed"), 1)
            dve.wait_ge(bank_free, 4 + OUT["hg_f"] + 8)
            v.scalar_tensor_tensor(G_B[:, :, :], G_F[:, 4:8, :], -1.0, G_F[:, 4:8, :], ALU.mult,
                                   ALU.max).then_inc(sem("hg_abs"), 1)
            dve.wait_ge(sem("hg_ln"), 1)
            v.scalar_tensor_tensor(G_L[:, :, :], G_F[:, 4:8, :], 0.0, G_B[:, :, :], ALU.min, ALU.subtract).then_inc(
                sem("hg_logf"), 1)
            v.drain()
            dve.wait_ge(sem("scan_reset"), 16)
            for h in range(4):
                last = v.tensor_tensor_scan(G_B[:, h, :], G_R[:, :], G_L[:, h, :], 0.0, ALU.mult, ALU.add)
            last.then_inc(sem("hg_cumsum"), 1)
            top(2)
            wait_group(dve, "hg_n")
            dve.wait_ge(sem("hg_qk"), 1)
            dve.wait_ge(sem("sec_tables"), 16)
            v.drain()

            def halves(ap, s):
                a = ap.rearrange("p h (n s) -> p (h n) s", s=2 * s)
                return a[:, :, 0:s], a[:, :, s:2 * s]

            def differences(l):
                if l >= 2:
                    dve.wait_ge(sem("hg_products"), 4 * (l - 2) + 4)
                if l == NL:
                    b = G_B[:, :, :].rearrange("p h (t s) -> p (h t) s", s=P)
                    v.tensor_tensor(G_E[:, l % 2].rearrange("p h (t s) -> p (h t) s", s=P),
                                    b[:, :, P - 1:P].to_broadcast((P, 16, P)), b, ALU.subtract).then_inc(
                                        sem("hg_diff"), 1)
                    return
                s = HALVES[l]
                n = 4 * T // (2 * s)
                lo, up = halves(G_E[:, l % 2], s)
                blo, bup = halves(G_B[:, :, :], s)
                mid = blo[:, :, s - 1:s].to_broadcast((P, n, s))
                v.tensor_tensor(up, bup, mid, ALU.subtract)
                v.tensor_tensor(lo, mid, blo, ALU.subtract).then_inc(sem("hg_diff"), 1)

            def mixed(l):
                dve.wait_ge(sem("hg_exp"), l + 1)
                if l >= NL:
                    side = G_F[:, 4:8, :] if l == NL else G_F[:, 0:4, :]
                    v.tensor_tensor(G_E[:, l % 2], G_E[:, l % 2], side, ALU.mult).then_inc(sem("hg_mixed"), 1)
                    return
                s = HALVES[l]
                lo, up = halves(G_E[:, l % 2], s)
                v.tensor_tensor(up, up, halves(G_F[:, 0:4, :], s)[1], ALU.mult)
                v.tensor_tensor(lo, lo, halves(G_F[:, 4:8, :], s)[0], ALU.mult).then_inc(sem("hg_mixed"), 1)

            def products(l):
                def queries(ap):
                    if l == NL:
                        return ap.rearrange("p t (n s) -> p t n s", n=1)
                    return ap.rearrange("p t (n s) -> p t n s", s=2 * HALVES[l])[:, :, :, HALVES[l]:]

                if l == 0:
                    dve.wait_ge(sem("hg_zero"), 1)
                for h in range(4):
                    dve.wait_ge(sem("hg_products"), 4 * l + h + 1)
                    mask = queries(G_M[:, l:l + 1, :])
                    v.copy_predicated(queries(G_A[:, h]), mask.to_broadcast((P, 4, mask.shape[2], mask.shape[3])),
                                      queries(PS[:, 4 + h, :].rearrange("p (t q) -> p t q", t=4))).then_inc(
                                          sem("hg_weighted"), 1)

            def last_head(j, four, values):
                v.tensor_tensor(H[:, :, 512 + HD * j:512 + HD * j + HD], values, each(RSUM[:, four]),
                                ALU.mult).then_inc(o_done, 1)

            def last_units(steps):
                units(UNITS["sa"], 32, last_ext, S_PT, last_head, FEW_BANKS, steps)

            NL = len(HALVES)
            differences(0)
            mixed(0)
            for l in range(NL + 1):
                if l:
                    products(l - 1)
                if l < NL:
                    differences(l + 1)
                else:
                    dve.sem_inc(sem("hg_buffer_free"), 1)
                last_units(range(4 * l, 4 * l + 2))
                mixed(l + 1)
                last_units(range(4 * l + 2, 4 * l + 4))
            products(NL)
            last_units(range(4 * NL + 4, 4 * NL + 8))
            for h in range(4):
                dve.wait_ge(sem("hg_k_turned"), h + 1)
                v.tensor_copy(G_KT[:, h], PS[:, h, 0:3 * P].rearrange("p (t d) -> p t d", t=3)).then_inc(
                    sem("hg_kt"), 1)
            dve.wait_ge(sem("hg_lasts"), 1)
            for h in range(4):
                dve.wait_ge(sem("hg_kv"), h + 1)
                v.tensor_copy(G_S[:, h, 0, :], PS[:, h, 0:P])
                for t in range(1, 3):
                    v.drain()
                    last = v.scalar_tensor_tensor(G_S[:, h, t, :], G_S[:, h, t - 1, :], G_X[:, h, t:t + 1],
                                                  PS[:, h, P * t:P * t + P], ALU.mult, ALU.add)
                last.then_inc(sem("hg_state"), 1)
            for h in range(5):
                s = slice(P * h, P * h + P)
                if h < 4:
                    dve.wait_ge(sem("hg_squared"), h + 1)
                    cols = slice(4 * h, 4 * h + 4)
                    v.tensor_scalar(SS[:, cols], SS[:, cols], 1.0 / P, RMS_EPS, ALU.mult, ALU.add).then_inc(
                        mean_ready, 1)
                    v.tensor_tensor(H[:, :, s], PS[:, 4 + h, :].rearrange("p (t d) -> p t d", t=4),
                                    G_N[:, :, 512 + P * h:512 + P * h + P], ALU.mult)
                if h:
                    s = slice(P * h - P, P * h)
                    dve.wait_ge(rstd_ready, RSTDS["hgo"] + h)
                    v.drain()
                    v.tensor_tensor(H[:, :, s], H[:, :, s], RS[:, 4 * h - 4:4 * h].unsqueeze(2).to_broadcast(
                        (P, NT, P)), ALU.mult).then_inc(sem("hg_gated"), 1)
            features("sec_y", G_HG)
            residual("sec_out", "ffn")
            features("ffn", G_FFN)
            with dve.Fori(0, BLOCKS["ffn_in"]) as i:
                for j in range(2):
                    dve.wait_ge(sem("ffn_silu"), 2 * i + j + 1)
                    if j:
                        dve.wait_ge(chunk_done, R + CH["ffn_in"] + R * i + R)
                    else:
                        dve.wait_ge(out_done, ODONE["ffn_in"] + 3 * i + 2)
                    v.tensor_tensor(FT[:, j, :], PS[:, 2 + j, :], FT[:, j, :], ALU.mult).then_inc(sem("ffn_mul"), 1)
                for j in range(2):
                    dve.wait_ge(sem("hidden_high"), 2 * i + j + 1)
                    v.tensor_tensor(FLO[:, bass.ds(2 * i + j, 1), :].rearrange("p a t -> p (a t)"), FT[:, j, :],
                                    FH[:, bass.ds(2 * i + j, 1), :].rearrange("p a t -> p (a t)").bitcast(f32),
                                    ALU.subtract).then_inc(sem("hidden_low"), 1)
            dve.sem_inc(bank_free, 4 * BLOCKS["ffn_in"])
            for i in range(2):
                for j in range(4):
                    if j == NT - 1:
                        dve.wait_ge(chunk_done, R + CH["ffn_out"] + OUT_CHUNKS * (i + 1))
                    else:
                        dve.wait_ge(sem("ffn_out_done"), 3 * i + j + 1)
                    v.tensor_tensor(X[:, j, 512 * i:512 * i + 512], PS[:, 4 * i + j, :],
                                    X[:, j, 512 * i:512 * i + 512], ALU.add).then_inc(bank_free, 1)

        @block.tensor
        def _(pe):
            mm = nc.tensor.matmul
            pe.sem_inc(chunk_done, R)
            for one in (sc_ready, t_ready, o_ready, sem("ret_used")):
                pe.sem_inc(one, CREDIT)

            def keep_clock(bank, rounds):
                pe.wait_ge(sem("zero_ready"), 1)
                with pe.Fori(0, rounds):
                    for _ in range(8):
                        mm(PS[:, bank, :], ZERO[:, 0:P], ZERO[:, :], start=True, stop=True, skip_group_check=True)

            def features(use, nt=NT, normed=True):
                if normed:
                    pe.wait_ge(normed_ready, NORMED[use] + nt)
                for k in range(NK):
                    if k >= 4:
                        pe.wait_ge(act_low, AT[use] + k - 3)
                    elif use == "sec_y":
                        pe.wait_ge(sem("hg_gated"), k + 1)
                    for t in range(nt):
                        last = nc.tensor.transpose(PS[:, 4 + k % 4, P * t:P * t + P], H[:, t, P * k:P * k + P],
                                                   ID[:, :])
                    last.then_inc(turned, 1)

            def three(bank, hi_l, lo_l, hi_r, lo_r, start, stop):
                mm(bank, hi_l, hi_r, start=start, stop=False, skip_group_check=True)
                mm(bank, hi_l, lo_r, start=False, stop=False, skip_group_check=True)
                return mm(bank, lo_l, hi_r, start=False, stop=stop, skip_group_check=True)

            def half_width(q, k, bank):
                for n, (a, b) in enumerate(((0, 0), (0, 1), (1, 0))):
                    mm(bank, q[a], k[b], start=n == 0, stop=False, skip_group_check=True)

            def block_products(n0, o0, tokens, use, outs=4, order=(0, 1, 2, 3), free=None, between=None):
                for r in range(R):
                    if between:
                        between(r)
                    pe.wait_ge(act_low, AT[use] + 2 * r + 2)
                    pe.wait_ge(split_ready, n0 + r + 1)
                    for at, j in enumerate(order[:outs]):
                        if r == 0:
                            if free:
                                free(at)
                            else:
                                pe.wait_ge(bank_free, o0 + at + 1)
                        for k in range(2):
                            kt = 2 * r + k
                            s = slice(P * j, P * j + P)
                            if tokens:
                                args = (AH[:, kt, s], AL[:, kt, s], WH[:, r, k, :], WL[:, r, k, :])
                            else:
                                args = (WH[:, r, k, s], WL[:, r, k, s], AH[:, kt, :], AL[:, kt, :])
                            last = three(PS[:, j, :], *args, start=kt == 0, stop=kt == NK - 1)
                        if r == R - 1 and at < outs - 1:
                            last.then_inc(out_done, 1)
                    last.then_inc(chunk_done, 1)

            def project(name, tokens, use):
                if BLOCKS[name] == 1:
                    block_products(CH[name], OUT[name], tokens, use)
                else:
                    with pe.Fori(0, BLOCKS[name]) as i:
                        block_products(CH[name] + R * i, OUT[name] + 4 * i, tokens, use)

            def small(k, m):
                pe.wait_ge(sem("small_low"), k + 1)
                for t in range(NT):
                    for kt in range(NK):
                        s = slice(P * t, P * t + P)
                        last = three(PS[:, 4, m * t:m * t + m], AH[:, kt, s], AL[:, kt, s], SMH[:, kt, 0:m],
                                     SML[:, kt, 0:m], start=kt == 0, stop=kt == NK - 1)
                last.then_inc(sem("small_done"), 1)

            def units(at0, head0, nu, ext, probs, pt, scores, values, banks=BANKS, steps=None):
                S, TR, O = banks
                for u in steps or range(nu + 3):
                    if u < nu:
                        pe.wait_ge(p_ready, CREDIT + at0 + u - len(S) + 1)
                        scores(u, PS[:, S[u % len(S)], 0:ext(u)]).then_inc(sc_ready, 1)
                    if 2 <= u < nu + 2:
                        k = u - 2
                        pe.wait_ge(p_ready, CREDIT + at0 + k + 1)
                        pe.wait_ge(pt_ready, CREDIT + at0 + k - len(TR) + 1)
                        for t in range(ext(k) // P):
                            last = nc.tensor.transpose(PS[:, TR[k % len(TR)], P * t:P * t + P],
                                                       probs[:, k % 2, P * t:P * t + P], ID[:, :])
                        last.then_inc(t_ready, 1)
                    if u >= 3:
                        j, q = divmod(u - 3, 4)
                        pe.wait_ge(pt_ready, CREDIT + at0 + u - 2)
                        if q == 0:
                            pe.wait_ge(o_done, CREDIT + head0 + j - len(O) + 1)
                        nt = ext(u - 3) // P
                        for t in range(nt):
                            last = mm(PS[:, O[j % len(O)], HD * q:HD * q + HD], pt[:, (u - 3) % 2, P * t:P * t + P],
                                      values(u - 3, t), start=t == 0, stop=t == nt - 1, skip_group_check=True)
                        last.then_inc(o_ready, 1)

            def attention_done(name):
                pe.wait_ge(p_ready, CREDIT + UNITS[name])
                pe.wait_ge(o_done, CREDIT + UNITS[name] // 4)

            pe.wait_ge(sem("first_const"), 16 * 3)
            features("mem", 2)
            block_products(CH["mem"], OUT["mem"], True, "mem", 2)
            features("even")
            project("even_qk", False, "even")
            project("even_v", True, "even")
            small(0, 8)
            block_products(CH["even_z"], OUT["even_z"], True, "even")
            pe.wait_ge(sem("forget_log"), 1)
            for t in range(NT):
                last = nc.tensor.transpose(PS[0:8, 4, P * t:P * t + P], FL[:, t, :], ID[:, :])
            last.then_inc(sem("forget_turned"), 1)
            block_products(CH["even_z"] + R, OUT["even_z"] + 4, True, "even")
            keep_clock(6, W_RET)
            wait_group(pe, "even_z")
            pe.wait_ge(sem("forget_parts"), 1)
            with pe.Fori(0, 2) as i:
                keep_clock(6, W_PAIRS)
                pe.wait_ge(sem("ret_k_staged"), i + 1)
                for u in range(17):
                    at = 16 * i + u
                    if u < 16:
                        half, b, k = HD * (u // 4 % 2), u // 8, u % 4
                        pe.wait_ge(sem("ret_weighted"), CREDIT + at - 3)
                        mm(PS[:, S_BANK[u % 4], 0:T - P * k], E_K[half:half + HD, b, P * k:P * k + P],
                           E_Q[half:half + HD, b, P * k:T], start=True, stop=True).then_inc(sem("ret_scores"), 1)
                    if u >= 1:
                        a, k = divmod(u - 1, 4)
                        pe.wait_ge(sem("ret_weighted"), CREDIT + at)
                        if k == 0:
                            pe.wait_ge(sem("ret_taken"), CREDIT + 4 * i + a - 1)
                        for q in range(k, NT):
                            last = mm(PS[:, O_BANK[a % 2], HD * q:HD * q + HD],
                                      E_P[:, (u - 1) % 2, P * (q - k):P * (q - k) + P],
                                      E_V[:, k, bass.ds(512 + 256 * i + HD * a, HD)],
                                      start=k == 0 and q == 0, stop=k == q, skip_group_check=True)
                        last.then_inc(sem("ret_used"), 1)
            keep_clock(6, W_FOX)
            pe.wait_ge(sem("ret_weighted"), CREDIT + 32)
            pe.wait_ge(sem("ret_taken"), CREDIT + 8)
            pe.wait_ge(sem("decay_rows"), 48)
            with pe.Fori(0, 2) as i:
                keep_clock(7, W_PAIRS)
                pe.wait_ge(sem("q_staged"), i + 1)

                def fox_scores(u, bank, i=i):
                    b, half, q, n = u // 8, HD * (u // 4 % 2), u % 4, P * (u % 4 + 1)
                    half_width([part[half:half + HD, b, P * q:P * q + P] for part in F_Q],
                               [part[half:half + HD, b, 0:n] for part in F_K], bank)
                    mm(bank, MINUS3[:, :], C3[:, bass.ds(4 * i + u // 4, 1), 0:n].rearrange("p a t -> p (a t)"),
                       start=False, stop=False, skip_group_check=True)
                    return mm(bank[:, n - P:n], IDB[:, :], CAUSAL[:, :], start=False, stop=True,
                              skip_group_check=True)

                units(UNITS["fox"] + 16 * i, UNITS["fox"] // 4 + 4 * i, 16, causal_ext, E_P, E_PT, fox_scores,
                      lambda k, t, i=i: E_V[:, t, bass.ds(256 * i + HD * (k // 4), HD)])
            keep_clock(7, W_GN)
            attention_done("odd")
            features("even_y")
            project("even_out", True, "even_y")
            keep_clock(7, W_RES)
            features("odd")

            project("odd_q", False, "odd")
            project("odd_kv", False, "odd")
            project("odd_v", True, "odd")
            small(1, 48)
            project("odd_z", True, "odd")
            pe.wait_ge(sem("gate_sum"), 1)
            wait_group(pe, "odd_z")
            for i in range(2):
                keep_clock(3, W_CMP)
                pe.wait_ge(sem("cmp_low"), i + 1)
                for r in range(R):
                    n = CH["cmp"] + R * i + r
                    pe.wait_ge(split_ready, n + 1)
                    for q in range(4):
                        l, s = 4 * r + q, slice(256 * (q % 2), 256 * (q % 2) + 256)
                        last = three(PS[0:4 * CMP, 4 + i, 0:256], CIH[i][:, l, :], CIL[i][:, l, :],
                                     WH[:, r, q // 2, s], WL[:, r, q // 2, s], start=l == 0, stop=l == 15)
                    last.then_inc(chunk_done, 1)
            for i in range(2):
                pe.wait_ge(sem("cmp_silu"), i + 1)
                for h in range(2):
                    last = nc.tensor.transpose(PS[:, 6 + i, P * h:P * h + 4 * CMP], HT[:, i, P * h:P * h + P],
                                               ID[0:4 * CMP, 0:4 * CMP])
                last.then_inc(sem("cmp_hidden_turned"), 1)
            keep_clock(3, W_CMP // 2)
            pe.wait_ge(sem("odd_tables"), 16 * 11)
            pe.wait_ge(sem("cmp_hidden"), 4)
            wait_group(pe, "odd_z")
            for h in range(2):
                mm(PS[:, 0, 0:P], W2D[:, h, :, :].rearrange("p a d -> p (a d)"),
                   CHID[:, 0, h, :, :].rearrange("p g c -> p (g c)"), start=h == 0, stop=h == 1)
            for g in range(4):
                for h in range(2):
                    last = mm(PS[0:32, 1, HD * g:HD * g + HD], CHID[:, 1, h, g, :], W2[:, 1, h, :],
                              start=h == 0, stop=h == 1)
            last.then_inc(sem("cmp_kv"), 1)
            pe.wait_ge(sem("cmp_kv_taken"), 1)

            def cmp_scores(t):
                if t >= 2:
                    pe.wait_ge(sem("cmp_biased"), t - 1)
                for pair in range(8):
                    last = mm(PS[:, 4 + t % 2, 64 * pair:64 * pair + 64], O_Q[:, pair, P * t:P * t + P],
                              KCMP[:, pair // 2, :, :].rearrange("p a c -> p (a c)"), start=True, stop=True,
                              skip_group_check=True)
                last.then_inc(sem("cmp_scores"), 1)

            for step in range(NT + 2):
                if step < NT:
                    cmp_scores(step)
                t = step - 1
                if 0 <= t < NT:
                    pe.wait_ge(sem("cmp_exp"), t + 1)
                    if t >= 2:
                        pe.wait_ge(sem("cmp_pt"), t - 1)
                    for g in range(4):
                        last = nc.tensor.transpose(PS[:, 6 + t % 2, P * g:P * g + P],
                                                   SC[:, t % 2, 4 * g:4 * g + 4, :].rearrange("p h c -> p (h c)"),
                                                   ID[:, :])
                    last.then_inc(sem("cmp_turned"), 1)
                t = step - 2
                if t >= 0:
                    pe.wait_ge(sem("cmp_pt"), t + 1)
                    if t:
                        pe.wait_ge(sem("cmp_taken"), 2 * t)
                    for g in range(4):
                        last = mm(PS[:, 2 + g // 2, 256 * (g % 2):256 * (g % 2) + 256], CPT[:, g, :],
                                  BDV[:, g, :, :].rearrange("p j d -> p (j d)"), start=True, stop=True,
                                  skip_group_check=True)
                    last.then_inc(sem("cmp_values"), 1)
            pe.wait_ge(sem("cmp_taken"), 2 * NT)
            with pe.Fori(0, 4) as i:
                keep_clock(7, W_ODD)
                pe.wait_ge(sem("q_staged"), 2 + i + 1)

                def odd_scores(u, bank, i=i):
                    b, a, q = u // 16, u // 4 % 4, u % 4
                    half, n = HD * (a % 2), P * (q + 1)
                    half_width([part[half:half + HD, a // 2, P * q:P * q + P] for part in O_QS],
                               [part[half:half + HD, b, 0:n] for part in O_KS], bank)
                    mm(bank, ALS[:, bass.ds(4 * i + a, 1), :].rearrange("p a q -> p (a q)"),
                       ALJ[:, T - P - P * q:T - P - P * q + n], start=False, stop=False, skip_group_check=True)
                    return mm(bank[:, n - P:n], IDB[:, :], CAUSAL[:, :], start=False, stop=True,
                              skip_group_check=True)

                units(UNITS["odd"] + 32 * i, UNITS["odd"] // 4 + 8 * i, 32, causal_ext, O_P, O_PT, odd_scores,
                      lambda k, t, i=i: O_V[:, t, bass.ds(256 * (k // 16) + HD * i, HD)])
            keep_clock(7, W_ODDY)
            attention_done("sa")
            features("odd_y")
            project("odd_out", True, "odd_y")

            keep_clock(7, W_NORMS)
            features("sec")
            project("sa_i", False, "sec")
            small(2, 72)
            pe.wait_ge(sem("index_kw"), 1)
            for t in range(NT):
                last = nc.tensor.transpose(PS[:, 5, P * t:P * t + P], I_KN[:, t, :], ID[:, :])
            last.then_inc(sem("index_k_turned"), 1)
            pe.wait_ge(sem("index_k"), 1)

            def index_scores(c):
                for n in range(3 * c, 3 * c + 3):
                    t, h = n // 8 + 1, n % 8
                    half = HD * (h % 2)
                    if n >= 4:
                        pe.wait_ge(sem("index_relu"), n - 3)
                    mm(PS[:, 4 + n % 4, 0:P * t + P], I_Q[half:half + HD, h // 2, P * t:P * t + P],
                       I_K[half:half + HD, 0:P * t + P], start=True, stop=True).then_inc(sem("index_ready"), 1)

            for i in range(2):
                block_products(CH["sa_n"] + R * i, OUT["sa_n"] + 4 * i, True, "sec",
                               between=lambda r, i=i: index_scores(R * i + r))
            project("hg_f", False, "sec")
            pe.wait_ge(sem("index_relu"), 24)
            keep_clock(7, W_RES)
            pe.wait_ge(sem("sa_normed"), 3)
            for k in range(8):
                which, pair = divmod(k, 2)
                if k >= 4:
                    pe.wait_ge(sem("sa_features"), k - 3)
                for t in range(2 if which == 3 else NT):
                    src = MEMKV[:, t, P * pair:P * pair + P] if which == 3 else \
                        S_N[:, t, (0, 256, 768)[which] + P * pair:(0, 256, 768)[which] + P * pair + P]
                    last = nc.tensor.transpose(PS[:, 4 + k % 4, P * t:P * t + P], src, ID[:, :])
                last.then_inc(sem("sa_turned"), 1)
                if k % 4 == 3:
                    i = k // 4
                    block_products(CH["hg_n"] + R * i, OUT["hg_n"] + 4 * i, True, "sec")
            pe.wait_ge(sem("sa_features"), 8)
            keep_clock(7, W_HG)
            wait_group(pe, "hg_n")

            def last_scores(u, bank):
                half, b, q = HD * (u // 4 % 2), u // 8 % 2, u % 4
                if u >= 16:
                    return mm(bank, M_Q[half:half + HD, b, P * q:P * q + P], M_K[half:half + HD, b, :],
                              start=True, stop=True)
                n = causal_ext(u)
                if q:
                    pe.wait_ge(sem("selected"), q)
                mm(bank, S_QK[half:half + HD, b, P * q:P * q + P], S_QK[half:half + HD, 2 + b, 0:n],
                   start=True, stop=False, skip_group_check=True)
                return mm(bank, IDB[:, :], SEL[:, q, 0:n], start=False, stop=True, skip_group_check=True)

            def last_values(u, t):
                col = HD * (u // 4 % 4)
                return MEMKV[:, t, 256 + col:256 + col + HD] if u >= 16 else S_N[:, t, 512 + col:512 + col + HD]

            def last_units(steps):
                units(UNITS["sa"], UNITS["sa"] // 4, 32, last_ext, S_P, S_PT, last_scores, last_values,
                      FEW_BANKS, steps)

            NL = len(HALVES)
            for l in range(NL + 1):
                if l < NL:
                    pe.wait_ge(sem("hg_mixed"), l + 1)
                for h in range(4):
                    if l:
                        pe.wait_ge(sem("hg_weighted"), 4 * (l - 1) + h + 1)
                    for t in range(NT):
                        s = slice(P * t, P * t + P)
                        lhs, rhs = (G_E[:, l % 2, h, s],) * 2 if l < NL else (G_F[:, 4 + h, s], G_F[:, h, s])
                        last = mm(PS[:, 4 + h, s], lhs, rhs, start=True, stop=True, skip_group_check=True)
                    last.then_inc(sem("hg_products"), 1)
                    last_units(range(4 * l + h, 4 * l + h + 1))
            last_units(range(4 * NL + 4, 4 * NL + 7))
            attention_done("end")
            pe.wait_ge(sem("hg_mixed"), NL + 1)
            for h in range(4):
                for t in range(3):
                    last = nc.tensor.transpose(PS[:, h, P * t:P * t + P], G_E[:, NL % 2, h, P * t:P * t + P],
                                               ID[:, :])
                last.then_inc(sem("hg_k_turned"), 1)
            for h in range(4):
                pe.wait_ge(sem("hg_kt"), h + 1)
                for t in range(3):
                    last = mm(PS[:, h, P * t:P * t + P], G_KT[:, h, t, :], G_N[:, t, P * h:P * h + P],
                              start=True, stop=True, skip_group_check=True)
                last.then_inc(sem("hg_kv"), 1)
            pe.wait_ge(sem("hg_weighted"), 4 * (NL + 1))
            pe.wait_ge(sem("hg_mixed"), NL + 2)
            for h in range(4):
                pe.wait_ge(sem("hg_state"), h + 1)
                for t in range(NT):
                    s = slice(P * t, P * t + P)
                    last = mm(PS[:, 4 + h, s], G_A[:, h, t, :], G_N[:, t, P * h:P * h + P],
                              start=True, stop=t == 0, skip_group_check=True)
                    if t:
                        last = mm(PS[:, 4 + h, s], G_E[:, (NL + 1) % 2, h, s], G_S[:, h, t - 1, :],
                                  start=False, stop=True, skip_group_check=True)
                last.then_inc(sem("hg_out"), 1)
            keep_clock(0, W_HGO)
            features("sec_y", normed=False)
            project("sec_out", True, "sec_y")
            keep_clock(7, W_RES)
            features("ffn")
            with pe.Fori(0, BLOCKS["ffn_in"]) as i:
                def free(at, i=i):
                    if at % 2 == 0:
                        pe.wait_ge(sem("ffn_mul"), 2 * i + at // 2 + 1)
                block_products(CH["ffn_in"] + R * i, 0, False, "ffn", 4, FFN_ORDER, free)
            for i in range(2):
                if i == 0:
                    pe.wait_ge(sem("hidden_low"), NF)
                    wait_group(pe, "ffn_in")
                for r in range(OUT_CHUNKS):
                    n = CH["ffn_out"] + OUT_CHUNKS * i + r
                    pe.wait_ge(split_ready, n + 1)
                    for t in range(NT):
                        s = slice(P * t, P * t + P)
                        for k in range(2):
                            kt = 2 * r + k
                            last = three(PS[:, 4 * i + t, :], FH[:, kt, s], FLO[:, kt, s], WH[:, n % R, k, :],
                                         WL[:, n % R, k, :], start=kt == 0, stop=kt == NF - 1)
                        if t == NT - 1:
                            last.then_inc(chunk_done, 1)
                        elif r == OUT_CHUNKS - 1:
                            last.then_inc(sem("ffn_out_done"), 1)


def tables():
    bf = np.dtype("bfloat16")
    i = np.arange(P)
    c = {"identity": np.eye(P, dtype=np.float32)}
    c["identity_bf16"] = c["identity"].astype(bf)
    c["causal_f32"] = np.where(i[None, :] <= i[:, None], 0.0, NEG).astype(np.float32)
    c["causal_bf16"] = c["causal_f32"].astype(bf)
    c["minus_one3"] = np.full((3, P), -1.0, np.float32).astype(bf)
    lg = np.log(1.0 - 2.0 ** (-5.0 - np.arange(8)))
    diff = np.arange(T)[None, :] - i[:, None]
    dec = np.where(diff[None] >= 0, np.exp(lg[:, None, None] * np.maximum(diff, 0)[None]), 0.0)
    c["retention"] = np.ascontiguousarray(dec.transpose(1, 0, 2)).astype(np.float32)
    slopes = (2.0 ** (-8.0 * (np.arange(16) + 1) / 16)).astype(np.float32)
    parts, rest = [], slopes.copy()
    for _ in range(3):
        parts.append(rest.astype(bf))
        rest = rest - parts[-1].astype(np.float32)
    j = np.arange(T) - (T - P)
    places = [j // 16 * 16, j % 16]
    c["alibi_slopes"] = np.zeros((P, 16, P), bf)
    c["alibi_positions"] = np.zeros((P, T), bf)
    for a in range(3):
        for b in range(2):
            c["alibi_slopes"][2 * a + b] = np.broadcast_to(parts[a][:, None], (16, P))
            c["alibi_positions"][2 * a + b] = places[b].astype(np.float32).astype(bf)
    t = np.arange(T).reshape(NT, P).T
    end = np.arange(32) * 16 + 31
    gap = t[:, :, None] - end[None, None, :]
    bias = -8.0 * slopes[None, None, :, None] * gap[:, :, None, :].astype(np.float32)
    ok = (gap >= 0) & (np.arange(32) < CMP)
    c["cmp_bias"] = np.where(ok[:, :, None, :], bias, NEG).astype(np.float32)
    masks = []
    for s in HALVES:
        k, q = i[:, None], i[None, :]
        masks.append((k // (2 * s) == q // (2 * s)) & (k % (2 * s) < s) & (q % (2 * s) >= s))
    masks.append(np.eye(P, dtype=bool))
    c["tree_masks"] = np.ascontiguousarray(np.stack(masks, 1)).astype(np.uint32)
    c["scan_reset"] = np.broadcast_to((np.arange(T) % P != 0).astype(np.float32), (P, T)).copy()
    return c


INPUTS = ["x", "even_norm_g", "even_w_in", "even_b_f", "even_gn_g", "even_w_out", "odd_norm_g", "odd_w_in",
          "odd_b_gate", "odd_pe_k", "odd_pe_v", "odd_wk1", "odd_wk2", "odd_wv1", "odd_wv2", "odd_w_out", "final_g",
          "mem_2", "w_in_2", "w_out_2", "w_mem_kv_2", "lb_logits_2", "norm_mix_2", "norm_mem_2", "norm_ffn_2",
          "hg_out_gain_2", "sa_q_gain_2", "sa_k_gain_2", "mem_q_gain_2", "mem_k_gain_2", "w_ffn_in_2",
          "w_ffn_out_2"]


def kernel(**inputs):
    import concourse.bacc as bacc
    from concourse.bass_utils import run_bass_kernel_spmd

    nc = bacc.Bacc("TRN2", target_bir_lowering=False, num_devices=1)
    arrays, w, c = {}, {}, {}
    for name in INPUTS:
        a = np.ascontiguousarray(inputs[name])
        arrays[f"in_{name}"] = a
        w[name] = nc.dram_tensor(f"in_{name}", a.shape, mybir.dt.from_np(a.dtype), kind="ExternalInput").ap()
    for name, a in tables().items():
        arrays[f"table_{name}"] = a
        c[name] = nc.dram_tensor(f"table_{name}", a.shape, mybir.dt.from_np(a.dtype), kind="ExternalInput").ap()
    out = nc.dram_tensor("out", (1, T, D), f32, kind="ExternalOutput").ap()
    program(nc, w, c, out)
    r = run_bass_kernel_spmd(nc, [arrays], core_ids=[0])
    return r.results[0]["out"]
```
